# Optimizing a Trainium2 kernel written in Bass

```python
import math
import jax, jax.numpy as jnp
from jax import lax
import numpy as np

D_MODEL = 1024
BATCH = 1
SEQ = 512
DEPTH = 2

GRID_W = 64
CTX_LEN = 256

NA_HEADS = 8
NA_HEAD_DIM = 64
NA_DIM = NA_HEADS * NA_HEAD_DIM
NA_WIN_ROWS = 8
NA_WIN_COLS = 16
GM_GROUPS = 4
GM_GROUP_DIM = 128
GM_WIDTH = GM_GROUPS * GM_GROUP_DIM
GM_CHUNK = 128
AB_QKV = 3 * NA_DIM
AB_IN = AB_QKV + 2 * GM_WIDTH
AB_MIX = NA_DIM + GM_WIDTH
HY_WIDTH = D_MODEL
HY_SHORT = 3
HY_BANDS = 16
HY_EMB = 1 + 2 * HY_BANDS
HY_FFN = 64
HY_DECAY_TARGET = 1e-2
HY_FAST_PCT = 0.3
HY_SLOW_PCT = 1.5
PEER_HEADS = 8
PEER_NKEYS = 128
PEER_EXPERTS = PEER_NKEYS * PEER_NKEYS
PEER_DK = 256
PEER_TOPK = 16
PEER_BLOCK = 128

N_AB = (DEPTH + 1) // 2
N_C = DEPTH // 2
DN_ALPHA = (2 * DEPTH) ** 0.25
DN_BETA = (8 * DEPTH) ** -0.25
LN_EPS = 1e-5
F32 = jnp.float32

kernel_name = 'hybrid_natten_gmlp_hyena_peer_dit'

def normalize(x):
    xf = x.astype(F32)
    mu = jnp.mean(xf, axis=-1, keepdims=True)
    var = jnp.mean(jnp.square(xf - mu), axis=-1, keepdims=True)
    return ((xf - mu) * lax.rsqrt(var + LN_EPS)).astype(x.dtype)

def layer_norm(x, g, b):
    return normalize(x) * g + b

def modulate(x, shift, scale):
    return x * (1 + scale) + shift

def split_heads(t):
    return t.reshape(t.shape[0], t.shape[1], NA_HEADS, NA_HEAD_DIM)

def neighbourhood_attention(q, k, v, k_ctx, v_ctx, rpb):
    B, L, H, dh = q.shape
    rows = L // GRID_W
    wr = min(NA_WIN_ROWS, rows)
    wc = NA_WIN_COLS
    qg = q.reshape(B, rows, GRID_W, H, dh)
    kg = k.reshape(B, rows, GRID_W, H, dh)
    vg = v.reshape(B, rows, GRID_W, H, dh)
    cols = jnp.arange(GRID_W)
    col_start = jnp.clip(cols - wc // 2, 0, GRID_W - wc)
    col_idx = col_start[:, None] + jnp.arange(wc)[None, :]
    col_rel = col_idx - cols[:, None] + (NA_WIN_COLS - 1)
    scale = dh ** -0.5

    def row_block(r):
        rs = jnp.clip(r - wr // 2, 0, rows - wr)
        q_r = lax.dynamic_index_in_dim(qg, r, axis=1, keepdims=False)
        k_r = lax.dynamic_slice_in_dim(kg, rs, wr, axis=1)[:, :, col_idx]
        v_r = lax.dynamic_slice_in_dim(vg, rs, wr, axis=1)[:, :, col_idx]
        row_rel = rs + jnp.arange(wr) - r + (NA_WIN_ROWS - 1)
        bias = rpb[:, row_rel][:, :, col_rel].transpose(0, 2, 1, 3)
        s_loc = jnp.einsum('bqhd,brqwhd->bhqrw', q_r, k_r).astype(F32) * scale + bias[None].astype(F32)
        s_ctx = jnp.einsum('bqhd,bkhd->bhqk', q_r, k_ctx).astype(F32) * scale
        logits = jnp.concatenate([s_loc.reshape(B, H, GRID_W, wr * wc), s_ctx], axis=-1)
        p = jax.nn.softmax(logits, axis=-1).astype(v.dtype)
        p_loc = p[..., :wr * wc].reshape(B, H, GRID_W, wr, wc)
        p_ctx = p[..., wr * wc:]
        return (jnp.einsum('bhqrw,brqwhd->bqhd', p_loc, v_r)
                + jnp.einsum('bhqk,bkhd->bqhd', p_ctx, v_ctx))

    out = lax.map(row_block, jnp.arange(rows))
    return out.transpose(1, 0, 2, 3, 4).reshape(B, L, H * dh)

def context_attention(q, k, v):
    B, Lc, H, dh = q.shape
    s = jnp.einsum('bqhd,bkhd->bhqk', q, k).astype(F32) * dh ** -0.5
    p = jax.nn.softmax(s, axis=-1).astype(v.dtype)
    return jnp.einsum('bhqk,bkhd->bqhd', p, v).reshape(B, Lc, H * dh)

def chunk_spatial_gating(u, gv, w_s, b_s):
    B, L, _ = u.shape
    n = L // GM_CHUNK
    gvc = normalize(gv).reshape(B, n, GM_CHUNK, GM_GROUPS, GM_GROUP_DIM)
    mixed = jnp.einsum('gpq,bnqgc->bnpgc', w_s, gvc) + b_s.T[None, None, :, :, None]
    return u * mixed.reshape(B, L, GM_WIDTH)

def ab_project(h, w_in):
    p = h @ w_in
    q, k, v = [split_heads(t) for t in jnp.split(p[..., :AB_QKV], 3, axis=-1)]
    u, gv = jnp.split(jax.nn.gelu(p[..., AB_QKV:], approximate=False), 2, axis=-1)
    return q, k, v, u, gv

def mixer_ab(h, h_ctx, w_in, w_out, rpb, w_s, b_s, ctx_out):
    q, k, v, u, gv = ab_project(h, w_in)
    if ctx_out:
        qc, kc, vc, uc, gvc = ab_project(h_ctx, w_in)
    else:
        kc, vc = [split_heads(t) for t in jnp.split(h_ctx @ w_in[:, NA_DIM:AB_QKV], 2, axis=-1)]
    a = neighbourhood_attention(q, k, v, kc, vc, rpb)
    g = chunk_spatial_gating(u, gv, w_s, b_s)
    y = jnp.concatenate([a, g], axis=-1) @ w_out
    y_ctx = None
    if ctx_out:
        ac = context_attention(qc, kc, vc)
        gc = chunk_spatial_gating(uc, gvc, w_s, b_s)
        y_ctx = jnp.concatenate([ac, gc], axis=-1) @ w_out
    return y, y_ctx

def hyena_filter(L, w1, b1, f1, w2, b2, f2, w3):
    w1, b1, f1, w2, b2, f2, w3 = [t.astype(F32) for t in (w1, b1, f1, w2, b2, f2, w3)]
    t = jnp.linspace(0.0, 1.0, L, dtype=F32)[:, None]
    ang = 2.0 * math.pi * jnp.arange(L, dtype=F32)[:, None] / L
    bands = jnp.linspace(1e-4, HY_BANDS - 1, HY_BANDS, dtype=F32)[None, :]
    z = jnp.concatenate([t, jnp.cos(bands * ang), jnp.sin(-bands * ang)], axis=-1)
    hid = jnp.sin(f1 * (z @ w1 + b1))
    hid = jnp.sin(f2 * (hid @ w2 + b2))
    filt = hid @ w3
    deltas = jnp.abs(jnp.linspace(math.log(HY_DECAY_TARGET) / HY_SLOW_PCT,
                                  math.log(HY_DECAY_TARGET) / HY_FAST_PCT, HY_WIDTH, dtype=F32))
    decay = jnp.exp(-t * deltas[None, :])
    fwd = filt[:, :HY_WIDTH] * decay
    bwd = filt[:, HY_WIDTH:] * decay
    l1 = jnp.sum(jnp.abs(fwd), axis=0) + jnp.sum(jnp.abs(bwd[1:]), axis=0)
    k2 = jnp.concatenate([fwd, jnp.zeros((1, HY_WIDTH), F32), bwd[:0:-1]], axis=0)
    return k2 / l1[None, :]

def long_conv(v, k2):
    L = v.shape[1]
    vf = jnp.fft.rfft(v.astype(F32), n=2 * L, axis=1)
    kf = jnp.fft.rfft(k2, n=2 * L, axis=0)
    y = jnp.fft.irfft(vf * kf[None], n=2 * L, axis=1)[:, :L]
    return y.astype(v.dtype)

def hyena(h, w_in, b_in, conv_w, conv_b, w1, b1, f1, w2, b2, f2, w3, d_skip, w_out):
    L = h.shape[1]
    z = h @ w_in + b_in
    z = lax.conv_general_dilated(z, conv_w[:, None, :], window_strides=(1,), padding=[(1, 1)],
                                 dimension_numbers=('NWC', 'WIO', 'NWC'),
                                 feature_group_count=3 * HY_WIDTH) + conv_b
    x0, x1, v = jnp.split(z, 3, axis=-1)
    k2 = hyena_filter(L, w1, b1, f1, w2, b2, f2, w3)
    v = v * x1
    y = (long_conv(v, k2) + v * d_skip) * x0
    return y @ w_out

def peer(h, wq, keys, u_tab, v_tab):
    B, L, D = h.shape
    n_tok = B * L
    xt = h.reshape(n_tok, D)
    q = (xt @ wq).reshape(n_tok, PEER_HEADS, 2, PEER_DK // 2)
    s = jnp.einsum('nhpd,hpkd->nhpk', q, keys).astype(F32)
    s1, i1 = lax.top_k(s[:, :, 0], PEER_TOPK)
    s2, i2 = lax.top_k(s[:, :, 1], PEER_TOPK)
    cand_s = (s1[..., :, None] + s2[..., None, :]).reshape(n_tok, PEER_HEADS, PEER_TOPK * PEER_TOPK)
    cand_i = (i1[..., :, None] * PEER_NKEYS + i2[..., None, :]).reshape(n_tok, PEER_HEADS, PEER_TOPK * PEER_TOPK)
    top_s, pos = lax.top_k(cand_s, PEER_TOPK)
    idx = jnp.take_along_axis(cand_i, pos, axis=-1)
    gate = jax.nn.softmax(top_s, axis=-1)
    nblk = n_tok // PEER_BLOCK

    def block(args):
        xb, ib, gb = args
        act = jax.nn.gelu(jnp.einsum('nd,nhkd->nhk', xb, u_tab[ib]).astype(F32), approximate=False)
        w = (gb * act).astype(xb.dtype)
        return jnp.einsum('nhk,nhkd->nd', w, v_tab[ib])

    out = lax.map(block, (xt.reshape(nblk, PEER_BLOCK, D),
                          idx.reshape(nblk, PEER_BLOCK, PEER_HEADS, PEER_TOPK),
                          gate.reshape(nblk, PEER_BLOCK, PEER_HEADS, PEER_TOPK)))
    return out.reshape(B, L, D)

def setup_inputs(seed: int = 0) -> dict:
    key = jax.random.key(seed)
    ks = iter(jax.random.split(key, 40))
    D = D_MODEL

    def nrm(shape, s):
        return jax.random.normal(next(ks), shape, F32) * s

    return {
        'x': nrm((BATCH, SEQ, D), 1.0),
        'c': nrm((BATCH, D), 1.0),
        'ctx': nrm((BATCH, CTX_LEN, D), 1.0),
        'c_ctx': nrm((D,), 1.0),
        'mod_w': nrm((DEPTH, D, 6 * D), D ** -0.5),
        'mod_b': nrm((DEPTH, 6 * D), 0.02),
        'ln_g': 1.0 + nrm((DEPTH, 2, D), 0.02),
        'ln_b': nrm((DEPTH, 2, D), 0.02),
        'ab_w_in': nrm((N_AB, D, AB_IN), D ** -0.5),
        'ab_w_out': nrm((N_AB, AB_MIX, D), DN_BETA * AB_MIX ** -0.5),
        'na_rpb': nrm((N_AB, NA_HEADS, 2 * NA_WIN_ROWS - 1, 2 * NA_WIN_COLS - 1), 0.5),
        'gm_w_s': nrm((N_AB, GM_GROUPS, GM_CHUNK, GM_CHUNK), GM_CHUNK ** -0.5),
        'gm_b_s': 1.0 + nrm((N_AB, GM_GROUPS, GM_CHUNK), 0.02),
        'hy_w_in': nrm((N_C, D, 3 * HY_WIDTH), D ** -0.5),
        'hy_b_in': nrm((N_C, 3 * HY_WIDTH), 0.02),
        'hy_conv_w': nrm((N_C, HY_SHORT, 3 * HY_WIDTH), HY_SHORT ** -0.5),
        'hy_conv_b': nrm((N_C, 3 * HY_WIDTH), 0.02),
        'hy_ffn_w1': nrm((N_C, HY_EMB, HY_FFN), HY_EMB ** -0.5),
        'hy_ffn_b1': nrm((N_C, HY_FFN), 0.02),
        'hy_ffn_f1': 1.0 + nrm((N_C, HY_FFN), 0.02),
        'hy_ffn_w2': nrm((N_C, HY_FFN, HY_FFN), HY_FFN ** -0.5),
        'hy_ffn_b2': nrm((N_C, HY_FFN), 0.02),
        'hy_ffn_f2': 1.0 + nrm((N_C, HY_FFN), 0.02),
        'hy_ffn_w3': nrm((N_C, HY_FFN, 2 * HY_WIDTH), HY_FFN ** -0.5),
        'hy_d': nrm((N_C, HY_WIDTH), 0.5),
        'hy_w_out': nrm((N_C, HY_WIDTH, D), DN_BETA * HY_WIDTH ** -0.5),
        'peer_wq': nrm((DEPTH, D, PEER_HEADS * PEER_DK), D ** -0.5),
        'peer_keys': nrm((DEPTH, PEER_HEADS, 2, PEER_NKEYS, PEER_DK // 2), (PEER_DK // 2) ** -0.5),
        'peer_u': nrm((DEPTH, PEER_EXPERTS, D), D ** -0.5),
        'peer_v': nrm((DEPTH, PEER_EXPERTS, D), DN_BETA),
    }

def reference(x, c, ctx, c_ctx, mod_w, mod_b, ln_g, ln_b, ab_w_in, ab_w_out, na_rpb, gm_w_s, gm_b_s,
              hy_w_in, hy_b_in, hy_conv_w, hy_conv_b, hy_ffn_w1, hy_ffn_b1, hy_ffn_f1, hy_ffn_w2,
              hy_ffn_b2, hy_ffn_f2, hy_ffn_w3, hy_d, hy_w_out, peer_wq, peer_keys, peer_u, peer_v):
    D = D_MODEL
    for i in range(DEPTH):
        j = i // 2
        ctx_out = any(m % 2 == 0 for m in range(i + 1, DEPTH))
        mod = (jax.nn.silu(c) @ mod_w[i] + mod_b[i])[:, None, :]
        sh1, sc1, g1, sh2, sc2, g2 = jnp.split(mod, 6, axis=-1)
        h = modulate(x, sh1, sc1)
        if i % 2 == 0 or ctx_out:
            mod_c = (jax.nn.silu(c_ctx[None, :]) @ mod_w[i] + mod_b[i])[:, None, :]
            csh1, csc1, cg1, csh2, csc2, cg2 = jnp.split(mod_c, 6, axis=-1)
            h_ctx = modulate(ctx, csh1, csc1)
        if i % 2 == 0:
            y, y_ctx = mixer_ab(h, h_ctx, ab_w_in[j], ab_w_out[j], na_rpb[j], gm_w_s[j], gm_b_s[j], ctx_out)
        else:
            hy_args = (hy_w_in[j], hy_b_in[j], hy_conv_w[j], hy_conv_b[j], hy_ffn_w1[j], hy_ffn_b1[j],
                       hy_ffn_f1[j], hy_ffn_w2[j], hy_ffn_b2[j], hy_ffn_f2[j], hy_ffn_w3[j], hy_d[j], hy_w_out[j])
            y = hyena(h, *hy_args)
            y_ctx = hyena(h_ctx, *hy_args) if ctx_out else None
        x = layer_norm(DN_ALPHA * x + g1 * y, ln_g[i, 0], ln_b[i, 0])
        x = layer_norm(DN_ALPHA * x + g2 * peer(modulate(x, sh2, sc2), peer_wq[i], peer_keys[i], peer_u[i], peer_v[i]),
                       ln_g[i, 1], ln_b[i, 1])
        if ctx_out:
            ctx = layer_norm(DN_ALPHA * ctx + cg1 * y_ctx, ln_g[i, 0], ln_b[i, 0])
            ctx = layer_norm(DN_ALPHA * ctx + cg2 * peer(modulate(ctx, csh2, csc2), peer_wq[i], peer_keys[i], peer_u[i], peer_v[i]),
                             ln_g[i, 1], ln_b[i, 1])
    return x


_drawn_inputs = setup_inputs


def setup_inputs(seed=0):
    import zlib

    import numpy as np

    out = dict(_drawn_inputs(seed))
    spreads = {}
    factors = {'gm_b_s': 4.185,
     'hy_b_in': 4.167,
     'hy_conv_b': 4.184,
     'hy_ffn_b1': 7.483,
     'hy_ffn_f1': 8.0,
     'hy_ffn_b2': 7.872,
     'hy_ffn_f2': 44.948}
    for name, (base, spread) in spreads.items():
        noise = np.random.default_rng([zlib.crc32(name.encode()), seed]).standard_normal(out[name].shape)
        drawn = base * np.exp(spread * noise) if base else spread * noise
        out[name] = __import__('jax').numpy.asarray(drawn.astype(out[name].dtype))
    for name, factor in factors.items():
        out[name] = (out[name] * factor).astype(out[name].dtype)
    return out
```

```python
from contextlib import ExitStack

import numpy as np

import concourse.bass as bass
from concourse import mybir

F32 = mybir.dt.float32
U32 = mybir.dt.uint32
ALU = mybir.AluOpType
ACT = mybir.ActivationFunctionType
AX_X = mybir.AxisListType.X

P = 128
D = 1024
SEQ = 512
CTX = 256
KT = D // P
TT = SEQ // P
CT = CTX // P
HALF = 512
ALPHA = 4 ** 0.25
EPS = 1e-5

HEADS = 8
HEAD_DIM = 64
GRID_W = 64
GRID_ROWS = SEQ // GRID_W
WIN_COLS = 16
NA_DIM = HEADS * HEAD_DIM
KEYS_ALL = SEQ + CTX
RPB_ROWS = 2 * 8 - 1
TAB = RPB_ROWS - 1
MASKED = -1e30

GROUPS = 4
PEER_HEADS = 8
NKEYS = 128
TOPK = 16
SLOTS = PEER_HEADS * TOPK
HP = 2 * PEER_HEADS
RING = 8
LOWEST = -3.4e38

NFFT = 2 * SEQ
EMB = 33
FFN = 64
MAGIC = 1.5 * 2 ** 23
TWO_PI_HIGH = 6.28125
TWO_PI_MID = float(np.floor((2 * np.pi - TWO_PI_HIGH) * 2 ** 21) / 2 ** 21)
TWO_PI_LOW = float(2 * np.pi - TWO_PI_HIGH - TWO_PI_MID)
PI_BELOW = float(np.nextafter(np.float32(np.pi), np.float32(0)))


class Machine:
    pass


class Chain:

    def __init__(self, semaphore):
        self.semaphore, self.count = semaphore, 0

    def mark(self, instruction):
        instruction.then_inc(self.semaphore, 1)
        self.count += 1

    def wait(self, engine):
        engine.wait_ge(self.semaphore, self.count)

    def link(self, engine, instruction):
        self.mark(instruction)
        self.wait(engine)


class SelectionChain(Chain):

    def __init__(self, semaphore):
        super().__init__(semaphore)
        self.each, self.before = None, 0

    def begin(self, nth):
        if self.each is None and self.count:
            self.each = self.count
        self.before = (nth - 1) * self.each if self.each else 0
        self.count = 0

    def wait(self, engine):
        engine.wait_ge(self.semaphore, self.before + self.count)
        engine.nop(nofuse=True)


def setup(nc, m, a):
    with ExitStack() as scope:
        cond = scope.enter_context(nc.sbuf_tensor("cond", [P, 2, KT], F32))
        cond_silu = scope.enter_context(nc.sbuf_tensor("cond_silu", [P, 2, KT], F32))
        block = scope.enter_context(nc.Block(no_gpsimd_drain=True))

        @block.sync
        def _(sp):
            sp.dma_start(cond[:, 0, :], a["c"].rearrange("a (p k) -> p (a k)", k=KT)).then_inc(m.setup_landed, 16)
            sp.dma_start(cond[:, 1, :], a["c_ctx"].rearrange("(p k) -> p k", k=KT)).then_inc(m.setup_landed, 16)
            sp.dma_start(m.ident[:], a["ident"]).then_inc(m.setup_landed, 16)
            sp.dma_start(m.ranks[:], a["ranks"]).then_inc(m.setup_landed, 16)
            sp.dma_start(m.x[:], a["x"][0].rearrange("(t p) d -> p t d", p=P)).then_inc(m.setup_landed, 16)
            sp.dma_start(m.xm[:, 0:CT, :], a["ctx"][0].rearrange("(t p) d -> p t d", p=P)).then_inc(m.setup_landed, 16)

        @block.scalar
        def _(act):
            act.wait_ge(m.setup_landed, 96)
            act.activation(cond_silu[:], cond[:], ACT.Silu).then_inc(m.silu_done, 1)

        @block.vector
        def _(dve):
            m.vector.mark(dve.memset(m.ones[:], 1.0))
            dve.wait_ge(m.silu_done, 1)
            m.vector.link(dve, dve.tensor_copy(m.cond_wide[:], cond_silu[:].unsqueeze(3).to_broadcast([P, 2, KT, P])))


def modulation(nc, m, a, layer):
    blocks = 6 * D // HALF
    ctx_blocks = 2 * D // HALF if layer == 0 else 0
    ring = 3
    done_before = (blocks + 2 * D // HALF) * layer
    products = [(n, who) for n in range(blocks) for who in range(2 if n < ctx_blocks else 1)]
    weights = a["mod_w"][layer].rearrange("(p k) n -> p k n", k=KT)
    biases = a["mod_b"][layer:layer + 1, :]
    with ExitStack() as scope:
        w = scope.enter_context(nc.sbuf_tensor(f"mod_w{layer}_sb", [P, ring, KT, HALF], F32))
        b = scope.enter_context(nc.sbuf_tensor(f"mod_b{layer}_sb", [1, ring, HALF], F32))
        block = scope.enter_context(nc.Block(no_gpsimd_drain=True))

        @block.sync
        def _(sp):
            for n in range(blocks):
                if n >= ring:
                    last = max(i for i, (block_n, _) in enumerate(products) if block_n == n - ring)
                    sp.wait_ge(m.mod_row_ready, done_before + last + 1)
                sp.dma_start(w[:, n % ring], weights[:, :, n * HALF:(n + 1) * HALF]).then_inc(m.mod_landed[n % ring], 16)
                sp.dma_start(b[:, n % ring], biases[:, n * HALF:(n + 1) * HALF]).then_inc(m.mod_landed[n % ring], 16)

        @block.tensor
        def _(pe):
            for i, (n, who) in enumerate(products):
                pe.wait_ge(m.mod_landed[n % ring], 32 * (layer * blocks // ring + n // ring + 1))
                if i >= 4:
                    pe.wait_ge(m.mod_row_taken, done_before + i - 3)
                bank = m.psum[:, i % 4, :]
                pe.matmul(bank, m.ones[0:1, :], b[:, n % ring], start=True, stop=False)
                for k in range(KT):
                    mm = pe.matmul(bank, m.cond_wide[:, who, k, :], w[:, n % ring, k, :], start=False, stop=k == KT - 1)
                mm.then_inc(m.mod_row_ready, 1)

        @block.vector
        def _(dve):
            for i, (n, who) in enumerate(products):
                dve.wait_ge(m.mod_row_ready, done_before + i + 1)
                is_scale = n * HALF // D in (1, 4)
                cols = slice(n * HALF, (n + 1) * HALF)
                out = m.mod[:, cols] if who == 0 else m.xm[:, 2:4, :].rearrange("p t d -> p (t d)")[:, cols]
                dve.tensor_scalar_add(out, m.psum[:, i % 4, :], 1.0 if is_scale else 0.0).then_inc(m.mod_row_taken, 1)


def project(nc, m, a):
    blocks = 5
    weights = a["ab_w_in"][0].rearrange("(k p) n -> p k n", p=P)
    products = [(0, "q", f) for f in range(4)] + [(1, part, f) for f in range(4) for part in ("k", "kc")]
    products += [(2, "v", t) for t in range(TT + CT)] + [(3, "u", t) for t in range(TT)] + [(4, "g", t) for t in range(TT)]
    with ExitStack() as scope:
        w = scope.enter_context(nc.sbuf_tensor("ab_w_sb", [P, 2, KT, HALF], F32))
        h = scope.enter_context(nc.sbuf_tensor("h_rows0", [P, 2, D], F32))
        block = scope.enter_context(nc.Block(no_gpsimd_drain=True))

        @block.sync
        def _(sp):
            for n in range(blocks):
                if n >= 2:
                    last = max(i for i, product in enumerate(products) if product[0] == n - 2)
                    sp.wait_ge(m.proj_ready, last + 1)
                sp.dma_start(w[:, n % 2], weights[:, :, n * HALF:(n + 1) * HALF]).then_inc(m.proj_landed[n % 2], 16)

        @block.vector
        def _(dve):
            modulate_rows_vector(m, dve, h, TT + CT)

        @block.tensor
        def _(pe):
            for t in range(TT + CT):
                pe.wait_ge(m.rows_ready, m.rows_before + t + 1)
                transpose_tile_tensor(m, pe, h[:, t % 2, :], t)
            pe.wait_ge(m.columns_ready, m.turned_before + 2 * (TT + CT))
            for i, (n, what, j) in enumerate(products):
                pe.wait_ge(m.proj_landed[n % 2], 16 * (n // 2 + 1))
                if i >= 4:
                    pe.wait_ge(m.proj_taken, i - 3)
                for k in range(KT):
                    if what == "q":
                        out, left, right = m.psum[:, i % 4, :], w[:, n % 2, k, j * P:(j + 1) * P], m.cols[:, k, 0:SEQ]
                    elif what == "k":
                        out, left, right = m.psum[:, i % 4, :], w[:, n % 2, k, j * P:(j + 1) * P], m.cols[:, k, 0:SEQ]
                    elif what == "kc":
                        out, left, right = m.psum[:, i % 4, 0:CTX], w[:, n % 2, k, j * P:(j + 1) * P], m.cols[:, k, SEQ:KEYS_ALL]
                    else:
                        out, left, right = m.psum[:, i % 4, :], m.cols[:, k, j * P:(j + 1) * P], w[:, n % 2, k, :]
                    mm = pe.matmul(out, left, right, start=k == 0, stop=k == KT - 1)
                mm.then_inc(m.proj_ready, 1)

        @block.scalar
        def _(act):
            for t in range(TT + CT):
                transpose_tile_scalar(m, act, t, t)
            for i, (n, what, j) in enumerate(products):
                act.wait_ge(m.proj_ready, i + 1)
                bank = m.psum[:, i % 4, :]
                if what == "q":
                    act.mul(m.q_cols[:, j, :], bank, HEAD_DIM ** -0.5).then_inc(m.proj_taken, 1)
                elif what == "k":
                    act.copy(m.k_cols[:, j, 0:SEQ], bank).then_inc(m.proj_taken, 1)
                elif what == "kc":
                    act.copy(m.k_cols[:, j, SEQ:KEYS_ALL], bank[:, 0:CTX]).then_inc(m.proj_taken, 1)
                elif what == "v":
                    act.copy(m.v_rows[:, j, :], bank).then_inc(m.proj_taken, 1)
                else:
                    half = m.gate_rows[:, j, (0 if what == "u" else HALF):(HALF if what == "u" else D)]
                    act.activation(half, bank, ACT.Gelu).then_inc(m.proj_taken, 1)
    m.rows_before += TT + CT
    m.turned_before += 2 * (TT + CT)


def modulate_rows_vector(m, dve, h, tiles):
    for t in range(tiles):
        if t >= 2:
            dve.wait_ge(m.rows_transposed, m.turned_before + 2 * (t - 1))
        if t < TT:
            rows, shift, scale = m.x[:, t, :], m.mod[:, 0:D], m.mod[:, D:2 * D]
        else:
            rows, shift, scale = m.xm[:, t - TT, :], m.xm[:, 2, :], m.xm[:, 3, :]
        m.vector.link(dve, dve.tensor_tensor(h[:, t % 2, :], rows, scale, ALU.mult))
        dve.tensor_tensor(h[:, t % 2, :], h[:, t % 2, :], shift, ALU.add).then_inc(m.rows_ready, 1)


def transpose_tile_tensor(m, pe, rows, i):
    for half in range(2):
        n = 2 * i + half
        if n >= 4:
            pe.wait_ge(m.columns_ready, m.turned_before + n - 3)
        for k in range(4):
            tile = rows[:, (4 * half + k) * P:(4 * half + k + 1) * P]
            mm = pe.transpose(m.psum[:, 4 + n % 4, k * P:(k + 1) * P], tile, m.ident[:])
        mm.then_inc(m.rows_transposed, 1)


def transpose_tile_scalar(m, act, t, i):
    for half in range(2):
        n = 2 * i + half
        act.wait_ge(m.rows_transposed, m.turned_before + n + 1)
        bank = m.psum[:, 4 + n % 4, :].rearrange("p (k n) -> p k n", k=4)
        act.copy(m.cols[:, 4 * half:4 * half + 4, t * P:(t + 1) * P], bank).then_inc(m.columns_ready, 1)


def mix(nc, m, a):
    items = [(head, t) for head in range(HEADS) for t in range(TT)]
    with ExitStack() as scope:
        table = scope.enter_context(nc.sbuf_tensor("bias_table", [P, 2, TAB, GRID_W], F32))
        window = scope.enter_context(nc.sbuf_tensor("window", [P, GRID_W], F32))
        w_s = scope.enter_context(nc.sbuf_tensor("w_s_sb", [P, GROUPS, P], F32))
        b_s = scope.enter_context(nc.sbuf_tensor("b_s_sb", [P, GROUPS], F32))
        logits = scope.enter_context(nc.sbuf_tensor("logits", [P, 2, KEYS_ALL], F32))
        probs_t = scope.enter_context(nc.sbuf_tensor("probs_t", [P, 2, KEYS_ALL], F32))
        neg_max = scope.enter_context(nc.sbuf_tensor("neg_max", [P, 2], F32))
        row_sum = scope.enter_context(nc.sbuf_tensor("row_sum", [P, 2], F32))
        inv_sum = scope.enter_context(nc.sbuf_tensor("inv_sum", [P, 2], F32))
        stats = scope.enter_context(nc.sbuf_tensor("gv_stats", [P, TT, 6], F32))
        moments = scope.enter_context(nc.sbuf_tensor("gv_moments", [P, TT, 2], F32))
        block = scope.enter_context(nc.Block(no_gpsimd_drain=True))
        score_bank, ctx_bank = (0, 1), (2, 3)
        turn_bank, out_bank, mixed_bank = (4, 5), 6, 7

        @block.sync
        def _(sp):
            sp.dma_start(window[:], a["window"]).then_inc(m.mix_consts_landed, 16)
            sp.dma_start(w_s[:], a["gm_w_s_t"].rearrange("g q p -> q g p")).then_inc(m.mix_consts_landed, 16)
            sp.dma_start(b_s[:], a["gm_b_s_t"]).then_inc(m.mix_consts_landed, 16)
            for head in range(HEADS):
                if head >= 2:
                    sp.wait_ge(m.scores_biased, TT * (head - 1))
                for r2 in range(2):
                    source = a["rpb_shifted"][head, :, 1 - r2:1 - r2 + TAB, :]
                    sp.dma_start(table[r2 * GRID_W:(r2 + 1) * GRID_W, head % 2], source).then_inc(m.table_landed[head % 2], 16)

        @block.vector
        def _(dve):
            for t in range(TT):
                m.vector.mark(dve.bn_stats(stats[:, t, :], m.gate_rows[:, t, HALF:D]))
            m.vector.wait(dve)
            for t in range(TT):
                m.vector.mark(dve.bn_aggr(moments[:, t, :], stats[:, t, :]))
            m.vector.wait(dve)
            dve.tensor_scalar_add(moments[:, :, 1], moments[:, :, 1], EPS).then_inc(m.gv_var_ready, 1)
            dve.wait_ge(m.gv_std_ready, 1)
            m.vector.link(dve, dve.reciprocal(moments[:, :, 1], moments[:, :, 1]))
            for t in range(TT):
                gv = m.gate_rows[:, t, HALF:D]
                dve.tensor_scalar(gv, gv, moments[:, t, 0:1], moments[:, t, 1:2], ALU.subtract, ALU.mult).then_inc(m.gv_ready, 1)
            dve.wait_ge(m.mix_consts_landed, 48)

            def gate(t):
                dve.wait_ge(m.mixed_ready, t + 1)
                for g in range(GROUPS):
                    cols = slice(g * P, (g + 1) * P)
                    last = dve.scalar_tensor_tensor(m.xm[:, t, HALF + g * P:HALF + (g + 1) * P], m.psum[:, mixed_bank, cols],
                                                    b_s[:, g:g + 1], m.gate_rows[:, t, cols], ALU.add, ALU.mult)
                last.then_inc(m.mixed_taken, 1)

            def bias_scores(i):
                head, t = items[i]
                if t == 0:
                    dve.wait_ge(m.table_landed[head % 2], 32 * (head // 2 + 1))
                    mask = window[:].unsqueeze(1).to_broadcast([P, TAB, GRID_W])
                    m.vector.link(dve, dve.tensor_tensor(table[:, head % 2], table[:, head % 2], mask, ALU.add))
                dve.wait_ge(m.scores_ready, i + 1)
                if i >= 2:
                    dve.wait_ge(m.probs_turned, 2 * (i - 1))
                j = 2 * (TT - 1 - t)
                rows = table[:, head % 2, j:j + GRID_ROWS, :].rearrange("p r c -> p (r c)")
                dve.tensor_tensor(logits[:, i % 2, 0:SEQ], m.psum[:, score_bank[i % 2], :], rows, ALU.add).then_inc(m.scores_biased, 1)
                dve.wait_ge(m.scores_biased, i + 1)
                dve.wait_ge(m.ctx_scores_taken, i + 1)
                m.vector.link(dve, dve.reduce_max(neg_max[:, i % 2:i % 2 + 1], logits[:, i % 2, :], AX_X))
                dve.tensor_scalar_mul(neg_max[:, i % 2:i % 2 + 1], neg_max[:, i % 2:i % 2 + 1], -1.0).then_inc(m.max_ready, 1)

            def take_turned(i):
                dve.wait_ge(m.probs_turned, 2 * i + 1)
                if i >= 2:
                    dve.wait_ge(m.heads_out_ready, i - 1)
                dve.tensor_copy(probs_t[:, i % 2, 0:HALF], m.psum[:, turn_bank[0], :]).then_inc(m.turned_taken_vector, 1)
                dve.wait_ge(m.probs_ready, i + 1)
                m.vector.mark(dve.reciprocal(inv_sum[:, i % 2:i % 2 + 1], row_sum[:, i % 2:i % 2 + 1]))

            def take_out(i):
                head, t = items[i]
                m.vector.wait(dve)
                dve.wait_ge(m.heads_out_ready, i + 1)
                dve.tensor_scalar(m.xm[:, t, head * HEAD_DIM:(head + 1) * HEAD_DIM],
                                  m.psum[:, out_bank, (i % 2) * HEAD_DIM:(i % 2 + 1) * HEAD_DIM],
                                  inv_sum[:, i % 2:i % 2 + 1], None, ALU.mult).then_inc(m.heads_out_taken, 1)

            bias_scores(0)
            for t in range(TT):
                gate(t)
            for i in range(len(items)):
                if i + 1 < len(items):
                    bias_scores(i + 1)
                take_turned(i)
                take_out(i)

        @block.scalar
        def _(act):
            act.wait_ge(m.gv_var_ready, 1)
            act.activation(moments[:, :, 1], moments[:, :, 1], ACT.Sqrt).then_inc(m.gv_std_ready, 1)

            def take_ctx(i):
                act.wait_ge(m.scores_ready, i + 1)
                if i >= 2:
                    act.wait_ge(m.probs_turned, 2 * (i - 1))
                act.copy(logits[:, i % 2, SEQ:KEYS_ALL], m.psum[:, ctx_bank[i % 2], 0:CTX]).then_inc(m.ctx_scores_taken, 1)

            def exponentials(i):
                act.wait_ge(m.max_ready, i + 1)
                if i >= 2:
                    act.wait_ge(m.heads_out_taken, i - 1)
                act.activation(logits[:, i % 2, :], logits[:, i % 2, :], ACT.Exp, bias=neg_max[:, i % 2:i % 2 + 1],
                               accum_out=row_sum[:, i % 2:i % 2 + 1]).then_inc(m.probs_ready, 1)

            def take_turned(i):
                act.wait_ge(m.probs_turned, 2 * i + 2)
                if i >= 2:
                    act.wait_ge(m.heads_out_ready, i - 1)
                act.copy(probs_t[:, i % 2, HALF:KEYS_ALL], m.psum[:, turn_bank[1], 0:CTX]).then_inc(m.turned_taken_scalar, 1)

            take_ctx(0)
            exponentials(0)
            for i in range(len(items)):
                if i + 1 < len(items):
                    take_ctx(i + 1)
                take_turned(i)
                if i + 1 < len(items):
                    exponentials(i + 1)

        def scores(pe, i):
            head, t = items[i]
            part = slice((head % 2) * HEAD_DIM, (head % 2 + 1) * HEAD_DIM)
            if i >= 2:
                pe.wait_ge(m.scores_biased, i - 1)
                pe.wait_ge(m.ctx_scores_taken, i - 1)
            q = m.q_cols[part, head // 2, t * P:(t + 1) * P]
            pe.matmul(m.psum[:, score_bank[i % 2], :], q, m.k_cols[part, head // 2, 0:SEQ], start=True, stop=True)
            pe.matmul(m.psum[:, ctx_bank[i % 2], 0:CTX], q, m.k_cols[part, head // 2, SEQ:KEYS_ALL],
                      start=True, stop=True).then_inc(m.scores_ready, 1)

        @block.tensor
        def _(pe):
            pe.wait_ge(m.mix_consts_landed, 48)
            for t in range(TT):
                pe.wait_ge(m.gv_ready, t + 1)
                if t >= 1:
                    pe.wait_ge(m.mixed_taken, t)
                for g in range(GROUPS):
                    mm = pe.matmul(m.psum[:, mixed_bank, g * P:(g + 1) * P], w_s[:, g, :],
                                   m.gate_rows[:, t, HALF + g * P:HALF + (g + 1) * P], start=True, stop=True)
                mm.then_inc(m.mixed_ready, 1)
                if t == 0:
                    scores(pe, 0)
            for i, (head, t) in enumerate(items):
                if i + 1 < len(items):
                    scores(pe, i + 1)
                pe.wait_ge(m.probs_ready, i + 1)
                if i >= 1:
                    pe.wait_ge(m.turned_taken_vector, i)
                    pe.wait_ge(m.turned_taken_scalar, i)
                for c in range(KEYS_ALL // P):
                    mm = pe.transpose(m.psum[:, turn_bank[c // 4], (c % 4) * P:(c % 4 + 1) * P],
                                      logits[:, i % 2, c * P:(c + 1) * P], m.ident[:])
                    if c == 3 or c == 5:
                        mm.then_inc(m.probs_turned, 1)
                pe.wait_ge(m.turned_taken_vector, i + 1)
                pe.wait_ge(m.turned_taken_scalar, i + 1)
                if i >= 1:
                    pe.wait_ge(m.heads_out_taken, i)
                for c in range(KEYS_ALL // P):
                    mm = pe.matmul(m.psum[:, out_bank, (i % 2) * HEAD_DIM:(i % 2 + 1) * HEAD_DIM],
                                   probs_t[:, i % 2, c * P:(c + 1) * P], m.v_rows[:, c, head * HEAD_DIM:(head + 1) * HEAD_DIM],
                                   start=c == 0, stop=c == KEYS_ALL // P - 1)
                mm.then_inc(m.heads_out_ready, 1)


def norm_tile_vector(m, dve, t, gate_row, ln, scratch, banks, moments, stats):
    x = m.x[:, t, :]
    for half in range(2):
        cols = slice(half * HALF, (half + 1) * HALF)
        m.vector.mark(dve.tensor_tensor(scratch[:, cols], m.psum[:, banks[half], :], gate_row[:, cols], ALU.mult))
    m.vector.wait(dve)
    m.vector.link(dve, dve.scalar_tensor_tensor(x, x, ALPHA, scratch[:], ALU.mult, ALU.add))
    for half in range(2):
        m.vector.mark(dve.bn_stats(stats[:, half, :], m.x[:, t, half * HALF:(half + 1) * HALF]))
    m.vector.wait(dve)
    m.vector.link(dve, dve.bn_aggr(moments[:], stats[:]))
    dve.tensor_scalar_add(moments[:, 1:2], moments[:, 1:2], EPS).then_inc(m.var_ready, 1)
    m.norms += 1
    dve.wait_ge(m.std_ready, m.norms)
    m.vector.link(dve, dve.reciprocal(moments[:, 1:2], moments[:, 1:2]))
    m.vector.link(dve, dve.tensor_scalar(x, x, moments[:, 0:1], moments[:, 1:2], ALU.subtract, ALU.mult))
    m.vector.link(dve, dve.tensor_tensor(x, x, ln[:, 0, :], ALU.mult))
    return dve.tensor_tensor(x, x, ln[:, 1, :], ALU.add)


def norm_tile_scalar(m, act, moments):
    m.roots += 1
    act.wait_ge(m.var_ready, m.roots)
    act.activation(moments[:, 1:2], moments[:, 1:2], ACT.Sqrt).then_inc(m.std_ready, 1)


def residual(nc, m, a, layer):
    weights = (a["ab_w_out"] if layer == 0 else a["hy_w_out"])[0].rearrange("(k p) n -> p k n", p=P)
    turned_first = TT if layer == 0 else 0
    with ExitStack() as scope:
        w = scope.enter_context(nc.sbuf_tensor(f"w_out{layer}", [P, 2, KT, HALF], F32))
        ln = scope.enter_context(nc.sbuf_tensor(f"ln_mix{layer}", [P, 2, D], F32))
        scratch = scope.enter_context(nc.sbuf_tensor(f"scratch_mix{layer}", [P, D], F32))
        stats = scope.enter_context(nc.sbuf_tensor(f"stats_mix{layer}", [P, 2, 6], F32))
        moments = scope.enter_context(nc.sbuf_tensor(f"moments_mix{layer}", [P, 2], F32))
        block = scope.enter_context(nc.Block(no_gpsimd_drain=True))

        @block.sync
        def _(sp):
            for half in range(2):
                sp.dma_start(w[:, half], weights[:, :, half * HALF:(half + 1) * HALF]).then_inc(m.out_landed, 16)
            sp.dma_start(ln[:, 0, :], a["ln_g"][layer, 0:1, :].to_broadcast([P, D])).then_inc(m.ln_landed, 16)
            sp.dma_start(ln[:, 1, :], a["ln_b"][layer, 0:1, :].to_broadcast([P, D])).then_inc(m.ln_landed, 16)

        @block.tensor
        def _(pe):
            for t in range(turned_first):
                transpose_tile_tensor(m, pe, m.xm[:, t, :], t)
            pe.wait_ge(m.out_landed, 32 * (layer + 1))
            for t in range(TT + 1):
                if t < TT:
                    if layer == 0:
                        pe.wait_ge(m.columns_ready, m.turned_before + 2 * (t + 1))
                    if t >= 2:
                        pe.wait_ge(m.tile_modulated, layer * TT + t - 1)
                    for half in range(2):
                        for k in range(KT):
                            mm = pe.matmul(m.psum[:, 2 * (t % 2) + half, :], m.cols[:, k, t * P:(t + 1) * P],
                                           w[:, half, k, :], start=k == 0, stop=k == KT - 1)
                    mm.then_inc(m.mix_out_ready, 1)
                if t >= 1:
                    pe.wait_ge(m.tile_modulated, layer * TT + t)
                    transpose_tile_tensor(m, pe, m.xm[:, t - 1, :], turned_first + t - 1)

        @block.vector
        def _(dve):
            dve.wait_ge(m.ln_landed, 32 * (2 * layer + 1))
            for t in range(TT):
                dve.wait_ge(m.mix_out_ready, layer * TT + t + 1)
                m.vector.link(dve, norm_tile_vector(m, dve, t, m.mod[:, 2 * D:3 * D], ln, scratch,
                                                    (2 * (t % 2), 2 * (t % 2) + 1), moments, stats))
                m.vector.link(dve, dve.tensor_tensor(m.xm[:, t, :], m.x[:, t, :], m.mod[:, 4 * D:5 * D], ALU.mult))
                dve.tensor_tensor(m.xm[:, t, :], m.xm[:, t, :], m.mod[:, 3 * D:4 * D], ALU.add).then_inc(m.tile_modulated, 1)

        @block.scalar
        def _(act):
            for t in range(turned_first):
                transpose_tile_scalar(m, act, t, t)
            for t in range(TT):
                norm_tile_scalar(m, act, moments)
                transpose_tile_scalar(m, act, t, turned_first + t)
    m.turned_before += 2 * (turned_first + TT)


def score_keys(nc, m, a, layer):
    weights = a["peer_wq"][layer].rearrange("(k p) n -> p k n", p=P)
    blocks = HP * P // HALF
    with ExitStack() as scope:
        w = scope.enter_context(nc.sbuf_tensor(f"wq{layer}", [P, 2, KT, HALF], F32))
        keys = scope.enter_context(nc.sbuf_tensor(f"keys{layer}", [P, HP, NKEYS], F32))
        query = scope.enter_context(nc.sbuf_tensor(f"query{layer}", [P, 2, SEQ], F32))
        block = scope.enter_context(nc.Block(no_gpsimd_drain=True))
        done = layer * HP

        @block.sync
        def _(sp):
            for n in range(blocks):
                if n >= 2:
                    sp.wait_ge(m.query_ready, done + 4 * (n - 1))
                sp.dma_start(w[:, n % 2], weights[:, :, n * HALF:(n + 1) * HALF]).then_inc(m.wq_landed[n % 2], 16)
                if n == 0:
                    sp.dma_start(keys[:], a["peer_keys_t"][layer].rearrange("h d k -> d h k")).then_inc(m.keys_landed, 16)

        @block.tensor
        def _(pe):
            for i in range(HP + 1):
                if i < HP:
                    n = i // 4
                    pe.wait_ge(m.wq_landed[n % 2], 16 * (layer * blocks // 2 + n // 2 + 1))
                    if i >= 2:
                        pe.wait_ge(m.query_taken, done + i - 1)
                    for k in range(KT):
                        mm = pe.matmul(m.psum[:, i % 2, :], w[:, n % 2, k, (i % 4) * P:(i % 4 + 1) * P],
                                       m.cols[:, k, 0:SEQ], start=k == 0, stop=k == KT - 1)
                    mm.then_inc(m.query_ready, 1)
                if i >= 1:
                    j = i - 1
                    if j == 0:
                        pe.wait_ge(m.keys_landed, 16 * (layer + 1))
                    pe.wait_ge(m.query_taken, done + j + 1)
                    if j >= 2:
                        pe.wait_ge(m.key_scores_taken, done + j - 1)
                    for t in range(TT):
                        mm = pe.matmul(m.psum[:, 2 + j % 2, t * P:(t + 1) * P], query[:, j % 2, t * P:(t + 1) * P],
                                       keys[:, j, :], start=True, stop=True)
                    mm.then_inc(m.key_scores_ready, 1)

        @block.scalar
        def _(act):
            for i in range(HP):
                act.wait_ge(m.query_ready, done + i + 1)
                if i >= 2:
                    act.wait_ge(m.key_scores_ready, done + i - 1)
                act.copy(query[:, i % 2, :], m.psum[:, i % 2, :]).then_inc(m.query_taken, 1)

        @block.vector
        def _(dve):
            m.vector.mark(dve.memset(m.scores[:, TT * 4, :], 0.0))
            by_tile = m.scores[:, 0:TT * 4, :].rearrange("p (t q) (j k) -> p t q j k", t=TT, j=4)
            for i in range(HP):
                dve.wait_ge(m.key_scores_ready, done + i + 1)
                dve.tensor_copy(by_tile[:, :, i // 4, i % 4, :],
                                m.psum[:, 2 + i % 2, :].rearrange("p (t k) -> p t k", t=TT)).then_inc(m.key_scores_taken, 1)


def experts(nc, m, a, layer):
    sections = SLOTS // 32
    groups = 32 // RING
    u_table, v_table = a[f"peer_u{layer}"], a[f"peer_v{layer}"]
    with ExitStack() as scope:
        def sb(name, shape, dtype=F32):
            return scope.enter_context(nc.sbuf_tensor(f"{name}{layer}", shape, dtype))
        idx = sb("idx", [P, (4 * TT + 1) * 32], U32)
        gates = sb("gates", [P, (4 * TT + 1) * 32])
        u_more = sb("u_more", [P, 2, D])
        v_ring = sb("v_ring", [P, RING, D])
        current = sb("current", [P, 2, RING], U32)
        dots = sb("dots", [P, 2, RING])
        acted = sb("acted", [P, 2, RING])
        weights = sb("weights", [P, 2, RING])
        diagonal = sb("diagonal", [P, 2, RING, P])
        zeros = sb("zeros", [1, HALF])
        ln = sb("ln_peer", [P, 2, D])
        scratch = sb("scratch_peer", [P, D])
        stats = sb("stats_peer", [P, 2, 6])
        moments = sb("moments_peer", [P, 2])
        first = sb("first", [P, 4, NKEYS])
        rest = sb("rest", [P, 4, NKEYS])
        top = sb("top", [P, 4, TOPK])
        top_at = sb("top_at", [P, 4, TOPK], U32)
        top_at_f = sb("top_at_f", [P, 4, TOPK])
        sums = sb("sums", [P, 2, TOPK * TOPK])
        sums_rest = sb("sums_rest", [P, 2, TOPK * TOPK])
        best = sb("best", [P, 2, TOPK])
        best_at = sb("best_at", [P, 2, TOPK], U32)
        digits = sb("digits", [P, 2, 2, TOPK], U32)
        digits_f = sb("digits_f", [P, 2, 2, TOPK])
        match = sb("match", [P, 2, TOPK, TOPK])
        found = sb("found", [P, 2, 2 * TOPK])
        expd = sb("expd", [P, 2, TOPK])
        denom = sb("denom", [P, 2])
        cols_flat = m.cols[:].rearrange("p k n -> p (k n)")
        u_ring = [cols_flat[:, j * D:(j + 1) * D] for j in range(6)] + [u_more[:, 0, :], u_more[:, 1, :]]
        block = scope.enter_context(nc.Block(no_gpsimd_drain=True))
        groups_before = layer * TT * sections * groups
        sections_before = layer * (TT * sections + 1)

        def select(dve, section, nth):
            def rounds(values, remaining, tops, ats, n):
                for i in range(n):
                    m.select.mark(dve.max(tops[:, i, 0:8], values[:, i, :]))
                m.select.wait(dve)
                for i in range(n):
                    m.select.mark(dve.max_index(ats[:, i, 0:8], tops[:, i, 0:8], values[:, i, :]))
                    m.select.mark(dve.match_replace(remaining[:, i, :], tops[:, i, 0:8], values[:, i, :], LOWEST))
                m.select.wait(dve)
                for i in range(n):
                    m.select.mark(dve.max(tops[:, i, 8:16], remaining[:, i, :]))
                m.select.wait(dve)
                for i in range(n):
                    m.select.mark(dve.max_index(ats[:, i, 8:16], tops[:, i, 8:16], remaining[:, i, :]))
                m.select.wait(dve)

            m.select.begin(nth)
            m.select.link(dve, dve.tensor_copy(first[:].rearrange("p j k -> p (j k)"), m.scores[:, bass.ds(section, 1), :].squeeze(1)))
            rounds(first, rest, top, top_at, 4)
            m.select.mark(dve.tensor_copy(top_at_f[:], top_at[:]))
            sets = top[:].rearrange("p (h s) r -> p h s r", s=2)
            sets_at = top_at_f[:].rearrange("p (h s) r -> p h s r", s=2)
            square = [P, 2, TOPK, TOPK]
            m.select.link(dve, dve.tensor_tensor(sums[:].rearrange("p h (r s) -> p h r s", r=TOPK),
                                                 sets[:, :, 0, :].unsqueeze(3).to_broadcast(square),
                                                 sets[:, :, 1, :].unsqueeze(2).to_broadcast(square), ALU.add))
            rounds(sums, sums_rest, best, best_at, 2)
            dve.tensor_tensor(expd[:], best[:], best[:, :, 0:1].to_broadcast([P, 2, TOPK]), ALU.subtract).then_inc(m.shifted_ready, 1)
            m.select.mark(dve.tensor_single_scalar(digits[:, 0], best_at[:], 4, ALU.logical_shift_right))
            m.select.mark(dve.tensor_single_scalar(digits[:, 1], best_at[:], TOPK - 1, ALU.bitwise_and))
            m.select.wait(dve)
            m.select.link(dve, dve.tensor_copy(digits_f[:], digits[:]))
            for s in range(2):
                ranks = m.ranks[:].unsqueeze(1).unsqueeze(1).to_broadcast(square)
                m.select.link(dve, dve.tensor_tensor(match[:], digits_f[:, s].unsqueeze(3).to_broadcast(square), ranks, ALU.is_equal))
                m.select.link(dve, dve.tensor_tensor(match[:], match[:], sets_at[:, :, s, :].unsqueeze(2).to_broadcast(square), ALU.mult))
                m.select.link(dve, dve.tensor_reduce(found[:, s, :], match[:].rearrange("p h r s -> p (h r) s"), AX_X, ALU.add))
            m.select.link(dve, dve.scalar_tensor_tensor(found[:, 0, :], found[:, 0, :], float(NKEYS), found[:, 1, :], ALU.mult, ALU.add))
            m.select.mark(dve.tensor_copy(idx[:, bass.ds(section * 32, 32)], found[:, 0, :]))
            dve.wait_ge(m.exps_ready, nth)
            m.select.link(dve, dve.tensor_reduce(denom[:], expd[:], AX_X, ALU.add))
            m.select.link(dve, dve.reciprocal(denom[:], denom[:]))
            dve.tensor_tensor(gates[:, bass.ds(section * 32, 32)].rearrange("p (h r) -> p h r", h=2), expd[:],
                              denom[:].unsqueeze(2).to_broadcast([P, 2, TOPK]), ALU.mult).then_inc(m.section_selected, 1)

        @block.sync
        def _(sp):
            sp.dma_start(ln[:, 0, :], a["ln_g"][layer, 1:2, :].to_broadcast([P, D])).then_inc(m.ln_landed, 16)
            sp.dma_start(ln[:, 1, :], a["ln_b"][layer, 1:2, :].to_broadcast([P, D])).then_inc(m.ln_landed, 16)
            if layer == 1:
                for t in range(TT):
                    sp.wait_ge(m.tile_done, TT + t + 1)
                    sp.dma_start(a["out"][0, t * P:(t + 1) * P, :], m.x[:, t, :]).then_inc(m.out_stored, 16)
                sp.wait_ge(m.out_stored, 16 * TT)

        @block.gpsimd
        def _(pool):
            with pool.Fori(0, TT * sections) as s:
                pool.wait_ge(m.section_selected, sections_before + s + 1)
                for g in range(groups):
                    group = groups_before + s * groups + g
                    pool.tensor_copy(current[:, g % 2, :], idx[:, bass.ds(s * 32 + g * RING, RING)]).then_inc(m.current_ready, 1)
                    pool.wait_ge(m.dots_done, (group + 1) * RING)
                    pool.wait_ge(m.current_ready, group + 1)
                    pool.nop(nofuse=True)
                    for j in range(RING):
                        pool.indirect_dma_start(out=u_ring[j], out_offset=None, in_=u_table,
                                                in_offset=bass.IndirectOffsetOnAxis(ap=current[:, g % 2, j:j + 1], axis=0)).then_inc(m.u_landed[j], 16)
                    pool.wait_ge(m.v_used, (group + 2) * RING)
                    pool.nop(nofuse=True)
                    for j in range(RING):
                        pool.indirect_dma_start(out=v_ring[:, j, :], out_offset=None, in_=v_table,
                                                in_offset=bass.IndirectOffsetOnAxis(ap=current[:, g % 2, j:j + 1], axis=0)).then_inc(m.v_landed[j], 16)

        def norm(dve, t):
            if t == 0:
                dve.wait_ge(m.ln_landed, 32 * (2 * layer + 2))
            dve.wait_ge(m.experts_ready, layer * TT + t + 1)
            norm_tile_vector(m, dve, t, m.mod[:, 5 * D:6 * D], ln, scratch, (2 * t, 2 * t + 1), moments, stats).then_inc(m.tile_done, 1)

        @block.vector
        def _(dve):
            m.vector.mark(dve.memset(zeros[:], 0.0))
            if layer == 0:
                dve.memset(found[:], 0.0).then_inc(m.dots_done, RING)
                dve.memset(match[:], 0.0).then_inc(m.v_used, 2 * RING)
            m.vector.wait(dve)
            dve.engine_nop().then_inc(m.zeros_ready, 1)
            select(dve, 0, sections_before + 1)
            for t in range(TT):
                with dve.Fori(0, sections) as q:
                    section = t * sections + q
                    select(dve, section + 1, sections_before + section + 2)
                    for g in range(groups):
                        group = groups_before + section * groups + g
                        for j in range(RING):
                            dve.wait_ge(m.u_landed[j], (group + 1) * 16)
                            dve.tensor_tensor_reduce(out=u_ring[j], in0=u_ring[j], in1=m.xm[:, t, :], scale=1.0, scalar=0.0,
                                                     op0=ALU.mult, op1=ALU.add, accum_out=dots[:, g % 2, j:j + 1]).then_inc(m.dots_done, 1)
                        dve.wait_ge(m.acted_ready, group + 1)
                        dve.tensor_tensor(weights[:, g % 2, :], acted[:, g % 2, :], gates[:, bass.ds(section * 32 + g * RING, RING)],
                                          ALU.mult).then_inc(m.weights_ready, 1)
                if t >= 1:
                    norm(dve, t - 1)
            norm(dve, TT - 1)

        @block.scalar
        def _(act):
            def exponentials(nth):
                act.wait_ge(m.shifted_ready, nth)
                act.activation(expd[:], expd[:], ACT.Exp).then_inc(m.exps_ready, 1)

            exponentials(sections_before + 1)
            for t in range(TT):
                with act.Fori(0, sections) as q:
                    exponentials(sections_before + t * sections + q + 2)
                    for g in range(groups):
                        group = groups_before + (t * sections + q) * groups + g
                        act.wait_ge(m.dots_done, (group + 2) * RING)
                        act.activation(acted[:, g % 2, :], dots[:, g % 2, :], ACT.Gelu).then_inc(m.acted_ready, 1)
                        act.wait_ge(m.weights_ready, group + 1)
                        act.wait_ge(m.v_used, (group + 1) * RING)
                        for j in range(RING):
                            last = act.activation(diagonal[:, g % 2, j, :], m.ident[:], ACT.Copy, scale=weights[:, g % 2, j:j + 1])
                        last.then_inc(m.diagonals_ready, 1)
                if t >= 1:
                    norm_tile_scalar(m, act, moments)
            norm_tile_scalar(m, act, moments)

        @block.tensor
        def _(pe):
            pe.wait_ge(m.zeros_ready, layer + 1)
            for t in range(TT):
                for half in range(2):
                    pe.matmul(m.psum[:, 2 * t + half, :], zeros[:, 0:P], zeros[:], start=True, stop=False)
                with pe.Fori(0, sections) as q:
                    for g in range(groups):
                        group = groups_before + (t * sections + q) * groups + g
                        pe.wait_ge(m.diagonals_ready, group + 1)
                        for j in range(RING):
                            pe.wait_ge(m.v_landed[j], (group + 1) * 16)
                            for half in range(2):
                                mm = pe.matmul(m.psum[:, 2 * t + half, :], diagonal[:, g % 2, j, :],
                                               v_ring[:, j, half * HALF:(half + 1) * HALF], start=False, stop=False)
                            mm.then_inc(m.v_used, 1)
                for half in range(2):
                    mm = pe.matmul(m.psum[:, 2 * t + half, :], zeros[:, 0:P], zeros[:], start=False, stop=True)
                mm.then_inc(m.experts_ready, 1)


def sine_vector(m, dve, out, product, bias, freq, turns):
    m.vector.link(dve, dve.tensor_scalar(out, product, bias, freq, ALU.add, ALU.mult))
    m.vector.link(dve, dve.tensor_scalar(turns, out, 1 / (2 * np.pi), MAGIC, ALU.mult, ALU.add))
    m.vector.link(dve, dve.tensor_scalar_add(turns, turns, -MAGIC))
    for part in (TWO_PI_HIGH, TWO_PI_MID, TWO_PI_LOW):
        m.vector.link(dve, dve.scalar_tensor_tensor(out, turns, -part, out, ALU.mult, ALU.add))
    dve.tensor_scalar(out, out, PI_BELOW, -PI_BELOW, ALU.min, ALU.max).then_inc(m.angle_ready, 1)


def filter_spectrum(nc, m, a):
    with ExitStack() as scope:
        def sb(name, shape):
            return scope.enter_context(nc.sbuf_tensor(name, shape, F32))
        position = sb("position", [EMB, SEQ])
        w1, w2, w3 = sb("ffn_w1", [EMB, FFN]), sb("ffn_w2", [FFN, FFN]), sb("ffn_w3", [FFN, 2 * D])
        ffn = sb("ffn_vectors", [FFN, 4])
        hidden = sb("hidden", [FFN, 2, SEQ])
        turns = sb("turns", [FFN, SEQ])
        decay = sb("decay", [P, 2, D])
        fwd, bwd = sb("fwd", [P, TT, D]), sb("bwd", [P, TT, D])
        scratch = sb("filter_scratch", [P, D])
        inv_l1 = sb("inv_l1", [P, D])
        block = scope.enter_context(nc.Block(no_gpsimd_drain=True))

        @block.sync
        def _(sp):
            sp.dma_start(position[:], a["position"]).then_inc(m.ffn_landed, 16)
            sp.dma_start(w1[:], a["hy_ffn_w1"][0]).then_inc(m.ffn_landed, 16)
            sp.dma_start(w2[:], a["hy_ffn_w2"][0]).then_inc(m.ffn_landed, 16)
            sp.dma_start(w3[:], a["hy_ffn_w3"][0]).then_inc(m.ffn_landed, 16)
            sp.dma_start(ffn[:], a["ffn_vectors"]).then_inc(m.ffn_landed, 16)
            for t in range(TT):
                if t >= 2:
                    sp.wait_ge(m.filter_taken, 4 * (t - 1))
                sp.dma_start(decay[:, t % 2, :], a["decay"][t * P:(t + 1) * P, :]).then_inc(m.decay_landed[t % 2], 16)
            sp.dma_start(m.cos_in[:], a["cos_in"].rearrange("(t p) f -> p t f", p=P)).then_inc(m.dft_landed, 16)
            sp.dma_start(m.sin_in[:], a["sin_in"].rearrange("(t p) f -> p t f", p=P)).then_inc(m.dft_landed, 16)

        @block.tensor
        def _(pe):
            pe.wait_ge(m.ffn_landed, 80)
            pe.matmul(m.psum[0:FFN, 0, :], w1[:], position[:], start=True, stop=True).then_inc(m.hidden_ready, 1)
            pe.wait_ge(m.sine_ready, 1)
            pe.matmul(m.psum[0:FFN, 1, :], w2[:], hidden[:, 0, :], start=True, stop=True).then_inc(m.hidden_ready, 1)
            pe.wait_ge(m.sine_ready, 2)
            for t in range(TT):
                for n in range(4):
                    i = 4 * t + n
                    if i >= 2:
                        pe.wait_ge(m.filter_taken, i - 1)
                    pe.matmul(m.psum[:, i % 2, :], hidden[:, 1, t * P:(t + 1) * P], w3[:, n * HALF:(n + 1) * HALF],
                              start=True, stop=True).then_inc(m.filter_ready, 1)
            for t in range(TT):
                for b in range(2):
                    pe.wait_ge(m.abs_ready, 2 * t + b + 1)
                    for half in range(2):
                        mm = pe.matmul(m.psum[:, 2 + half, :], m.ones[:], scratch[:, half * HALF:(half + 1) * HALF],
                                       start=t == b == 0, stop=t == TT - 1 and b == 1)
                    mm.then_inc(m.abs_summed, 1)
            pe.wait_ge(m.parts_ready, 2 * TT)
            pe.wait_ge(m.dft_landed, 32)
            for ft in range(4):
                for half in range(2):
                    i = 2 * ft + half
                    cols = slice(half * HALF, (half + 1) * HALF)
                    if i >= 2:
                        pe.wait_ge(m.spectrum_taken, 2 * (i - 1))
                    for table, part, bank in ((m.cos_in, fwd, 4 + 2 * (i % 2)), (m.sin_in, bwd, 5 + 2 * (i % 2))):
                        for t in range(TT):
                            mm = pe.matmul(m.psum[:, bank, :], table[:, t, ft * P:(ft + 1) * P], part[:, t, cols],
                                           start=t == 0, stop=t == TT - 1)
                    mm.then_inc(m.spectrum_ready, 1)
            for half in range(2):
                for t in range(TT):
                    mm = pe.matmul(m.psum[0:1, half, :], m.sin_in[:, t, 0:1], fwd[:, t, half * HALF:(half + 1) * HALF],
                                   start=t == 0, stop=t == TT - 1)
            mm.then_inc(m.highest_ready, 1)

        @block.vector
        def _(dve):
            dve.wait_ge(m.ffn_landed, 80)
            for n in range(2):
                dve.wait_ge(m.hidden_ready, n + 1)
                sine_vector(m, dve, hidden[:, n, :], m.psum[0:FFN, n, :], ffn[:, 2 * n:2 * n + 1], ffn[:, 2 * n + 1:2 * n + 2], turns[:])
            for t in range(TT):
                dve.wait_ge(m.decay_landed[t % 2], 16 * (t // 2 + 1))
                for n in range(4):
                    dve.wait_ge(m.filter_ready, 4 * t + n + 1)
                    part, cols = (fwd if n < 2 else bwd), slice((n % 2) * HALF, (n % 2 + 1) * HALF)
                    dve.tensor_tensor(part[:, t, cols], m.psum[:, (4 * t + n) % 2, :], decay[:, t % 2, cols], ALU.mult).then_inc(m.filter_taken, 1)
            dve.wait_ge(m.filter_taken, 4 * TT)
            dve.memset(bwd[0:1, 0, :], 0.0).then_inc(m.parts_final, 1)
            dve.wait_ge(m.abs_summed, 2 * TT)
            for half in range(2):
                m.vector.mark(dve.reciprocal(inv_l1[:, half * HALF:(half + 1) * HALF], m.psum[:, 2 + half, :]))
            m.vector.wait(dve)
            for t in range(TT):
                m.vector.link(dve, dve.tensor_tensor(scratch[:], fwd[:, t, :], bwd[:, t, :], ALU.subtract))
                m.vector.link(dve, dve.tensor_tensor(fwd[:, t, :], fwd[:, t, :], bwd[:, t, :], ALU.add))
                dve.tensor_tensor(bwd[:, t, :], scratch[:], inv_l1[:], ALU.mult).then_inc(m.parts_ready, 1)
                dve.tensor_tensor(fwd[:, t, :], fwd[:, t, :], inv_l1[:], ALU.mult).then_inc(m.parts_ready, 1)
                dve.wait_ge(m.parts_ready, 2 * (t + 1))

        @block.scalar
        def _(act):
            for n in range(2):
                act.wait_ge(m.angle_ready, n + 1)
                act.activation(hidden[:, n, :], hidden[:, n, :], ACT.Sin).then_inc(m.sine_ready, 1)
            act.wait_ge(m.parts_final, 1)
            for t in range(TT):
                for b, part in enumerate((fwd, bwd)):
                    if t + b >= 1:
                        act.wait_ge(m.abs_summed, 2 * t + b)
                    act.activation(scratch[:], part[:, t, :], ACT.Abs).then_inc(m.abs_ready, 1)
            for i in range(8):
                ft, cols = i // 2, slice((i % 2) * HALF, (i % 2 + 1) * HALF)
                act.wait_ge(m.spectrum_ready, i + 1)
                act.copy(m.k_re[:, ft, cols], m.psum[:, 4 + 2 * (i % 2), :]).then_inc(m.spectrum_taken, 1)
                act.copy(m.k_im[:, ft, cols], m.psum[:, 5 + 2 * (i % 2), :]).then_inc(m.spectrum_taken, 1)
            act.wait_ge(m.spectrum_taken, 16)
            act.wait_ge(m.highest_ready, 1)
            for half in range(2):
                act.copy(m.k_im[0:1, 0, half * HALF:(half + 1) * HALF], m.psum[0:1, half, :]).then_inc(m.highest_taken, 1)


def hyena_project(nc, m, a):
    tiles = 3 * KT
    weights = a["hy_w_in"][0].rearrange("(k p) n -> p k n", p=P)
    with ExitStack() as scope:
        w = scope.enter_context(nc.sbuf_tensor("hy_w_sb", [P, 2, KT, HALF], F32))
        h = scope.enter_context(nc.sbuf_tensor("h_rows1", [P, 2, D], F32))
        z = scope.enter_context(nc.sbuf_tensor("z_padded", [P, 2, SEQ + 2], F32))
        conv = scope.enter_context(nc.sbuf_tensor("conv", [P, SEQ], F32))
        vectors = scope.enter_context(nc.sbuf_tensor("hy_vectors_sb", [P, 5, tiles], F32))
        block = scope.enter_context(nc.Block(no_gpsimd_drain=True))

        @block.sync
        def _(sp):
            sp.dma_start(vectors[:], a["hy_vectors"]).then_inc(m.hy_vectors_landed, 16)
            for n in range(tiles // 4):
                if n >= 2:
                    sp.wait_ge(m.z_ready, 4 * (n - 1))
                sp.dma_start(w[:, n % 2], weights[:, :, n * HALF:(n + 1) * HALF]).then_inc(m.hy_landed[n % 2], 16)

        @block.tensor
        def _(pe):
            for t in range(TT):
                pe.wait_ge(m.rows_ready, m.rows_before + t + 1)
                transpose_tile_tensor(m, pe, h[:, t % 2, :], t)
            pe.wait_ge(m.columns_ready, m.turned_before + 2 * TT)
            for i in range(tiles):
                n = i // 4
                pe.wait_ge(m.hy_landed[n % 2], 16 * (n // 2 + 1))
                if i >= 4:
                    pe.wait_ge(m.z_taken, i - 3)
                for k in range(KT):
                    mm = pe.matmul(m.psum[:, i % 4, :], w[:, n % 2, k, (i % 4) * P:(i % 4 + 1) * P], m.cols[:, k, 0:SEQ],
                                   start=k == 0, stop=k == KT - 1)
                mm.then_inc(m.z_ready, 1)

        @block.scalar
        def _(act):
            for t in range(TT):
                transpose_tile_scalar(m, act, t, t)
            act.wait_ge(m.hy_vectors_landed, 16)
            act.wait_ge(m.pads_ready, 1)
            for i in range(tiles):
                act.wait_ge(m.z_ready, i + 1)
                if i >= 2:
                    act.wait_ge(m.conv_done, i - 1)
                act.activation(z[:, i % 2, 1:SEQ + 1], m.psum[:, i % 4, :], ACT.Identity, bias=vectors[:, 0, i:i + 1]).then_inc(m.z_taken, 1)

        @block.vector
        def _(dve):
            dve.memset(z[:], 0.0).then_inc(m.pads_ready, 1)
            modulate_rows_vector(m, dve, h, TT)
            dve.wait_ge(m.hy_vectors_landed, 16)
            for i in range(tiles):
                dve.wait_ge(m.z_taken, i + 1)
                taps = [z[:, i % 2, j:j + SEQ] for j in range(3)]
                out = m.x0[:, i, :] if i < KT else m.v_cols[:, i - KT, :] if i < 2 * KT else conv[:]
                m.vector.link(dve, dve.tensor_scalar(out, taps[0], vectors[:, 2, i:i + 1], vectors[:, 1, i:i + 1], ALU.mult, ALU.add))
                m.vector.link(dve, dve.scalar_tensor_tensor(out, taps[1], vectors[:, 3, i:i + 1], out, ALU.mult, ALU.add))
                dve.scalar_tensor_tensor(out, taps[2], vectors[:, 4, i:i + 1], out, ALU.mult, ALU.add).then_inc(m.conv_done, 1)
                if i >= 2 * KT:
                    dve.wait_ge(m.conv_done, i + 1)
                    v = m.v_cols[:, i - 2 * KT, :]
                    m.vector.link(dve, dve.tensor_tensor(v, v, conv[:], ALU.mult))
    m.rows_before += TT
    m.turned_before += 2 * TT


def convolve(nc, m, a):
    with ExitStack() as scope:
        def sb(name, shape):
            return scope.enter_context(nc.sbuf_tensor(name, shape, F32))
        v_rows = sb("v_rows1", [P, TT, D])
        cos_out, sin_out = sb("cos_out_sb", [P, 4, SEQ]), sb("sin_out_sb", [P, 4, SEQ])
        skip = sb("skip", [P, KT])
        parts = sb("spectrum_parts", [P, 4, HALF])
        minus = sb("minus", [P, 2])
        mixed = sb("skip_mixed", [P, SEQ])
        block = scope.enter_context(nc.Block(no_gpsimd_drain=True))

        @block.sync
        def _(sp):
            sp.dma_start(skip[:], a["hy_d_t"]).then_inc(m.inverse_landed, 16)
            sp.dma_start(cos_out[:], a["cos_out"].rearrange("(f p) t -> p f t", p=P)).then_inc(m.inverse_landed, 16)
            sp.dma_start(sin_out[:], a["sin_out"].rearrange("(f p) t -> p f t", p=P)).then_inc(m.inverse_landed, 16)

        @block.tensor
        def _(pe):
            for i in range(2 * TT):
                t, half = i // 2, i % 2
                if i >= 4:
                    pe.wait_ge(m.v_rows_taken, i - 3)
                for k in range(4):
                    mm = pe.transpose(m.psum[:, 4 + i % 4, k * P:(k + 1) * P], m.v_cols[:, 4 * half + k, t * P:(t + 1) * P], m.ident[:])
                mm.then_inc(m.v_turned, 1)
            pe.wait_ge(m.v_rows_taken, 2 * TT)
            for i in range(8):
                ft, cols = i // 2, slice((i % 2) * HALF, (i % 2 + 1) * HALF)
                if i >= 2:
                    pe.wait_ge(m.spectra_used, i - 1)
                for table, bank in ((m.cos_in, 2 * (i % 2)), (m.sin_in, 2 * (i % 2) + 1)):
                    for t in range(TT):
                        mm = pe.matmul(m.psum[:, bank, :], table[:, t, ft * P:(ft + 1) * P], v_rows[:, t, cols],
                                       start=t == 0, stop=t == TT - 1)
                mm.then_inc(m.v_spectrum_ready, 1)
            pe.wait_ge(m.inverse_landed, 48)
            pe.wait_ge(m.spectra_multiplied, 8)
            for k in range(KT):
                if k >= 4:
                    pe.wait_ge(m.y_taken, k - 3)
                for n, (part, table) in enumerate(((m.k_re, cos_out), (m.k_im, sin_out))):
                    for ft in range(4):
                        mm = pe.matmul(m.psum[:, 4 + k % 4, :], part[:, ft, k * P:(k + 1) * P], table[:, ft, :],
                                       start=n == ft == 0, stop=n == 1 and ft == 3)
                mm.then_inc(m.y_ready, 1)

        @block.scalar
        def _(act):
            for i in range(2 * TT):
                act.wait_ge(m.v_turned, i + 1)
                act.copy(v_rows[:, i // 2, (i % 2) * HALF:(i % 2 + 1) * HALF], m.psum[:, 4 + i % 4, :]).then_inc(m.v_rows_taken, 1)

        @block.vector
        def _(dve):
            m.vector.mark(dve.memset(minus[:], -1.0))
            m.vector.wait(dve)
            m.vector.link(dve, dve.memset(minus[0:1, 0:1], 0.0))
            for i in range(8):
                ft, cols = i // 2, slice((i % 2) * HALF, (i % 2 + 1) * HALF)
                dve.wait_ge(m.v_spectrum_ready, i + 1)
                v_re, v_im = m.psum[:, 2 * (i % 2), :], m.psum[:, 2 * (i % 2) + 1, :]
                k_re, k_im = m.k_re[:, ft, cols], m.k_im[:, ft, cols]
                m.vector.mark(dve.tensor_tensor(parts[:, 0, :], v_re, k_re, ALU.mult))
                m.vector.mark(dve.tensor_tensor(parts[:, 1, :], v_im, k_im, ALU.mult))
                m.vector.mark(dve.tensor_tensor(parts[:, 2, :], v_re, k_im, ALU.mult))
                dve.tensor_tensor(parts[:, 3, :], v_im, k_re, ALU.mult).then_inc(m.spectra_used, 1)
                m.vector.wait(dve)
                dve.wait_ge(m.spectra_used, i + 1)
                sign = minus[:, 0:1] if ft == 0 else minus[:, 1:2]
                m.vector.mark(dve.scalar_tensor_tensor(k_re, parts[:, 1, :], sign, parts[:, 0, :], ALU.mult, ALU.add))
                m.vector.mark(dve.tensor_tensor(k_im, parts[:, 2, :], parts[:, 3, :], ALU.add))
                m.vector.wait(dve)
                if ft == 0:
                    m.vector.link(dve, dve.tensor_copy(m.k_im[0:1, 0, cols], parts[0:1, 1, :]))
                dve.engine_nop().then_inc(m.spectra_multiplied, 1)
            dve.wait_ge(m.inverse_landed, 48)
            for k in range(KT):
                dve.wait_ge(m.y_ready, k + 1)
                dve.scalar_tensor_tensor(mixed[:], m.v_cols[:, k, :], skip[:, k:k + 1], m.psum[:, 4 + k % 4, :],
                                         ALU.mult, ALU.add).then_inc(m.y_taken, 1)
                dve.wait_ge(m.y_taken, k + 1)
                m.vector.link(dve, dve.tensor_tensor(m.cols[:, k, 0:SEQ], mixed[:], m.x0[:, k, :], ALU.mult))


def program(nc, a):
    with ExitStack() as whole:
        def sem(name):
            return whole.enter_context(nc.semaphore(name))
        m = Machine()
        m.setup_landed = sem("setup_landed")
        m.silu_done = sem("silu_done")
        m.mod_row_ready = sem("mod_row_ready")
        m.mod_row_taken = sem("mod_row_taken")
        m.vector_steps = sem("vector_steps")
        m.selection_steps = sem("selection_steps")
        m.proj_ready = sem("proj_ready")
        m.proj_taken = sem("proj_taken")
        m.rows_ready = sem("rows_ready")
        m.rows_transposed = sem("rows_transposed")
        m.columns_ready = sem("columns_ready")
        m.mix_consts_landed = sem("mix_consts_landed")
        m.scores_biased = sem("scores_biased")
        m.gv_var_ready = sem("gv_var_ready")
        m.gv_std_ready = sem("gv_std_ready")
        m.gv_ready = sem("gv_ready")
        m.mixed_ready = sem("mixed_ready")
        m.mixed_taken = sem("mixed_taken")
        m.scores_ready = sem("scores_ready")
        m.probs_turned = sem("probs_turned")
        m.ctx_scores_taken = sem("ctx_scores_taken")
        m.max_ready = sem("max_ready")
        m.probs_ready = sem("probs_ready")
        m.turned_taken_vector = sem("turned_taken_vector")
        m.turned_taken_scalar = sem("turned_taken_scalar")
        m.heads_out_ready = sem("heads_out_ready")
        m.heads_out_taken = sem("heads_out_taken")
        m.var_ready = sem("var_ready")
        m.std_ready = sem("std_ready")
        m.out_landed = sem("out_landed")
        m.ln_landed = sem("ln_landed")
        m.mix_out_ready = sem("mix_out_ready")
        m.tile_modulated = sem("tile_modulated")
        m.query_ready = sem("query_ready")
        m.query_taken = sem("query_taken")
        m.keys_landed = sem("keys_landed")
        m.key_scores_ready = sem("key_scores_ready")
        m.key_scores_taken = sem("key_scores_taken")
        m.section_selected = sem("section_selected")
        m.shifted_ready = sem("shifted_ready")
        m.exps_ready = sem("exps_ready")
        m.current_ready = sem("current_ready")
        m.dots_done = sem("dots_done")
        m.v_used = sem("v_used")
        m.acted_ready = sem("acted_ready")
        m.weights_ready = sem("weights_ready")
        m.diagonals_ready = sem("diagonals_ready")
        m.zeros_ready = sem("zeros_ready")
        m.experts_ready = sem("experts_ready")
        m.tile_done = sem("tile_done")
        m.out_stored = sem("out_stored")
        m.ffn_landed = sem("ffn_landed")
        m.hidden_ready = sem("hidden_ready")
        m.angle_ready = sem("angle_ready")
        m.sine_ready = sem("sine_ready")
        m.filter_ready = sem("filter_ready")
        m.filter_taken = sem("filter_taken")
        m.parts_final = sem("parts_final")
        m.abs_ready = sem("abs_ready")
        m.abs_summed = sem("abs_summed")
        m.parts_ready = sem("parts_ready")
        m.dft_landed = sem("dft_landed")
        m.spectrum_ready = sem("spectrum_ready")
        m.spectrum_taken = sem("spectrum_taken")
        m.highest_ready = sem("highest_ready")
        m.highest_taken = sem("highest_taken")
        m.hy_vectors_landed = sem("hy_vectors_landed")
        m.z_ready = sem("z_ready")
        m.z_taken = sem("z_taken")
        m.pads_ready = sem("pads_ready")
        m.conv_done = sem("conv_done")
        m.inverse_landed = sem("inverse_landed")
        m.v_turned = sem("v_turned")
        m.v_rows_taken = sem("v_rows_taken")
        m.v_spectrum_ready = sem("v_spectrum_ready")
        m.spectra_used = sem("spectra_used")
        m.spectra_multiplied = sem("spectra_multiplied")
        m.y_ready = sem("y_ready")
        m.y_taken = sem("y_taken")
        m.mod_landed = [sem(f"mod_landed{slot}") for slot in range(3)]
        m.proj_landed = [sem(f"proj_landed{slot}") for slot in range(2)]
        m.table_landed = [sem(f"table_landed{slot}") for slot in range(2)]
        m.wq_landed = [sem(f"wq_landed{slot}") for slot in range(2)]
        m.decay_landed = [sem(f"decay_landed{slot}") for slot in range(2)]
        m.hy_landed = [sem(f"hy_landed{slot}") for slot in range(2)]
        m.u_landed = [sem(f"u_landed{slot}") for slot in range(RING)]
        m.v_landed = [sem(f"v_landed{slot}") for slot in range(RING)]
        m.vector = Chain(m.vector_steps)
        m.select = SelectionChain(m.selection_steps)
        m.rows_before = m.turned_before = m.norms = m.roots = 0

        def sb(scope, name, shape):
            return scope.enter_context(nc.sbuf_tensor(name, shape, F32))
        m.psum = whole.enter_context(nc.psum_tensor("psum", [P, 8, HALF], F32))
        m.x = sb(whole, "x_rows", [P, TT, D])
        m.xm = sb(whole, "xm_rows", [P, TT, D])
        m.mod = sb(whole, "mod_rows", [P, 6 * D])
        m.cols = sb(whole, "cols", [P, KT, KEYS_ALL])
        m.ident = sb(whole, "ident_sb", [P, P])
        m.ones = sb(whole, "ones", [P, P])
        m.ranks = sb(whole, "ranks_sb", [P, TOPK])
        m.cond_wide = sb(whole, "cond_wide", [P, 2, KT, P])
        m.x0 = m.xm[:].rearrange("p t (a n) -> p (t a) n", n=SEQ)
        setup(nc, m, a)
        modulation(nc, m, a, 0)
        with ExitStack() as scope:
            m.q_cols = sb(scope, "q_cols", [P, 4, SEQ])
            m.k_cols = sb(scope, "k_cols", [P, 4, KEYS_ALL])
            m.v_rows = sb(scope, "v_rows0", [P, TT + CT, NA_DIM])
            m.gate_rows = sb(scope, "gate_rows", [P, TT, D])
            project(nc, m, a)
            mix(nc, m, a)
        residual(nc, m, a, 0)
        with ExitStack() as scope:
            m.scores = sb(scope, "scores0", [P, 4 * TT + 1, 4 * NKEYS])
            score_keys(nc, m, a, 0)
            experts(nc, m, a, 0)
        modulation(nc, m, a, 1)
        with ExitStack() as scope:
            m.k_re, m.k_im = sb(scope, "k_re", [P, 4, D]), sb(scope, "k_im", [P, 4, D])
            m.cos_in, m.sin_in = sb(scope, "cos_in_sb", [P, TT, SEQ]), sb(scope, "sin_in_sb", [P, TT, SEQ])
            filter_spectrum(nc, m, a)
            m.v_cols = sb(scope, "v_cols", [P, KT, SEQ])
            hyena_project(nc, m, a)
            convolve(nc, m, a)
        residual(nc, m, a, 1)
        with ExitStack() as scope:
            m.scores = sb(scope, "scores1", [P, 4 * TT + 1, 4 * NKEYS])
            score_keys(nc, m, a, 1)
            experts(nc, m, a, 1)


def constants():
    f = np.float32
    col = np.arange(GRID_W)
    first = np.clip(col - WIN_COLS // 2, 0, GRID_W - WIN_COLS)
    inside = (col[None, :] >= first[:, None]) & (col[None, :] < first[:, None] + WIN_COLS)
    window = np.where(inside, 0.0, MASKED).astype(f)
    t = np.linspace(0.0, 1.0, SEQ, dtype=f)
    angle = (f(2.0 * np.pi) * np.arange(SEQ, dtype=f) / f(SEQ))[:, None]
    bands = np.linspace(1e-4, (EMB - 1) // 2 - 1, (EMB - 1) // 2, dtype=f)[None, :]
    position = np.concatenate([t[:, None], np.cos(bands * angle), np.sin(-bands * angle)], axis=1)
    deltas = np.abs(np.linspace(np.log(1e-2) / 1.5, np.log(1e-2) / 0.3, D, dtype=f))
    n = np.arange(SEQ)
    turn = 2 * np.pi * (np.outer(n, n) % NFFT) / NFFT
    alternating = 1.0 - 2.0 * (n % 2)
    cos_in, sin_in = np.cos(turn), np.sin(turn)
    weight = np.where(n == 0, 1.0, 2.0)[:, None] / NFFT
    cos_out, sin_out = weight * cos_in, weight * sin_in
    sin_in[:, 0] = alternating
    sin_out[0, :] = alternating / NFFT
    return {
        "ident": np.eye(P, dtype=f), "ranks": np.tile(np.arange(TOPK, dtype=f), (P, 1)),
        "window": np.concatenate([window, window]), "position": np.ascontiguousarray(position.T.astype(f)),
        "decay": np.exp(-t[:, None] * deltas[None, :]).astype(f),
        "cos_in": cos_in.astype(f), "sin_in": sin_in.astype(f), "cos_out": cos_out.astype(f), "sin_out": sin_out.astype(f),
    }


AS_THEY_COME = ("x", "c", "ctx", "c_ctx", "mod_w", "mod_b", "ln_g", "ln_b", "ab_w_in", "ab_w_out", "hy_w_in",
                "hy_ffn_w1", "hy_ffn_w2", "hy_ffn_w3", "hy_w_out", "peer_wq")


def laid_out(inputs):
    g = {name: np.asarray(value) for name, value in inputs.items()}
    arrays = {name: g[name] for name in AS_THEY_COME}
    for layer in range(2):
        arrays[f"peer_u{layer}"], arrays[f"peer_v{layer}"] = g["peer_u"][layer], g["peer_v"][layer]
    padded = np.pad(g["na_rpb"][0], ((0, 0), (0, 0), (GRID_W - WIN_COLS, GRID_W - WIN_COLS)))
    column = np.arange(GRID_W)
    shifted = padded[:, :, (GRID_W - 1 - column)[:, None] + column[None, :]]
    arrays["rpb_shifted"] = shifted.transpose(0, 2, 1, 3)
    arrays["gm_w_s_t"] = g["gm_w_s"][0].transpose(0, 2, 1)
    arrays["gm_b_s_t"] = g["gm_b_s"][0].T
    arrays["peer_keys_t"] = g["peer_keys"].transpose(0, 1, 2, 4, 3).reshape(2, HP, P, NKEYS)
    arrays["ffn_vectors"] = np.stack([g["hy_ffn_b1"][0], g["hy_ffn_f1"][0], g["hy_ffn_b2"][0], g["hy_ffn_f2"][0]], axis=1)
    per_feature = np.concatenate([g["hy_b_in"], g["hy_conv_b"], g["hy_conv_w"][0]])
    arrays["hy_vectors"] = per_feature.reshape(5, 3 * KT, P).transpose(2, 0, 1)
    arrays["hy_d_t"] = g["hy_d"][0].reshape(KT, P).T
    return {name: np.ascontiguousarray(value) for name, value in arrays.items()} | constants()


def kernel(**inputs):
    import concourse.bacc as bacc
    from concourse.bass_utils import run_bass_kernel_spmd

    nc = bacc.Bacc("TRN2", target_bir_lowering=False, num_devices=1)
    arrays = laid_out(inputs)
    a = {name: nc.dram_tensor(f"in_{name}", value.shape, mybir.dt.from_np(value.dtype), kind="ExternalInput").ap()
         for name, value in arrays.items()}
    a["out"] = nc.dram_tensor("out_x", (1, SEQ, D), F32, kind="ExternalOutput").ap()
    program(nc, a)
    result = run_bass_kernel_spmd(nc, [{f"in_{name}": value for name, value in arrays.items()}], core_ids=[0])
    return result.results[0]["out_x"]
```

```python
from contextlib import ExitStack

import numpy as np

import concourse.bass as bass
from concourse import mybir

F32 = mybir.dt.float32
U32 = mybir.dt.uint32
ALU = mybir.AluOpType
ACT = mybir.ActivationFunctionType
AX_X = mybir.AxisListType.X

P = 128
D = 1024
SEQ = 512
CTX = 256
KT = D // P
TT = SEQ // P
CT = CTX // P
HALF = 512
ALPHA = 4 ** 0.25
EPS = 1e-5

HEADS = 8
HEAD_DIM = 64
GRID_W = 64
GRID_ROWS = SEQ // GRID_W
WIN_COLS = 16
NA_DIM = HEADS * HEAD_DIM
KEYS_ALL = SEQ + CTX
RPB_ROWS = 2 * 8 - 1
TAB = RPB_ROWS - 1
MASKED = -1e30

GROUPS = 4
PEER_HEADS = 8
NKEYS = 128
TOPK = 16
SLOTS = PEER_HEADS * TOPK
HP = 2 * PEER_HEADS
RING = 8
LOWEST = -3.4e38

NFFT = 2 * SEQ
EMB = 33
FFN = 64
MAGIC = 1.5 * 2 ** 23
TWO_PI_HIGH = 6.28125
TWO_PI_MID = float(np.floor((2 * np.pi - TWO_PI_HIGH) * 2 ** 21) / 2 ** 21)
TWO_PI_LOW = float(2 * np.pi - TWO_PI_HIGH - TWO_PI_MID)
PI_BELOW = float(np.nextafter(np.float32(np.pi), np.float32(0)))


class Machine:
    pass


class Chain:

    def __init__(self, semaphore):
        self.semaphore, self.count = semaphore, 0

    def mark(self, instruction):
        instruction.then_inc(self.semaphore, 1)
        self.count += 1

    def wait(self, engine):
        engine.wait_ge(self.semaphore, self.count)

    def link(self, engine, instruction):
        self.mark(instruction)
        self.wait(engine)


class SelectionChain(Chain):

    def __init__(self, semaphore):
        super().__init__(semaphore)
        self.each, self.before = None, 0

    def begin(self, nth):
        if self.each is None and self.count:
            self.each = self.count
        self.before = (nth - 1) * self.each if self.each else 0
        self.count = 0

    def wait(self, engine):
        engine.wait_ge(self.semaphore, self.before + self.count)
        engine.nop(nofuse=True)


MOD_FIRST = (0, 23)
PROJECT_FIRST = 12
RESIDUAL_FIRST = (17, 41)
SCORES_FIRST = (19, 43)
HYENA_FIRST = 35


def block_of(weights, n):
    return weights[:, :, n * HALF:(n + 1) * HALF]


def load_block(m, sp, number, source):
    sp.dma_start(m.ring[:, number % 2], source).then_inc(m.ring_landed[number % 2], 16)


def wait_block(m, pe, number):
    pe.wait_ge(m.ring_landed[number % 2], 16 * (number // 2 + 1))
    return m.ring[:, number % 2]


def feature_major(weights):
    return weights.rearrange("(k p) n -> p k n", p=P)


def setup(nc, m, a):
    with ExitStack() as scope:
        cond = scope.enter_context(nc.sbuf_tensor("cond", [P, 2, KT], F32))
        block = scope.enter_context(nc.Block(no_gpsimd_drain=True))

        @block.sync
        def _(sp):
            sp.dma_start(cond[:, 0, :], a["c"].rearrange("a (p k) -> p (a k)", k=KT)).then_inc(m.setup_landed, 16)
            sp.dma_start(cond[:, 1, :], a["c_ctx"].rearrange("(p k) -> p k", k=KT)).then_inc(m.setup_landed, 16)
            sp.dma_start(m.ident[:], a["ident"]).then_inc(m.setup_landed, 16)
            sp.dma_start(m.picks[:], a["picks"]).then_inc(m.setup_landed, 16)
            sp.dma_start(m.ranks[:], a["ranks"]).then_inc(m.setup_landed, 16)
            sp.dma_start(m.x[:], a["x"][0].rearrange("(t p) d -> p t d", p=P)).then_inc(m.setup_landed, 16)
            sp.dma_start(m.xm[:, 0:CT, :], a["ctx"][0].rearrange("(t p) d -> p t d", p=P)).then_inc(m.setup_landed, 16)

        @block.scalar
        def _(act):
            act.wait_ge(m.setup_landed, 112)
            act.activation(m.cond_silu[:].rearrange("p k c -> p c k"), cond[:], ACT.Silu).then_inc(m.silu_done, 1)

        @block.vector
        def _(dve):
            m.vector.mark(dve.memset(m.ones[:], 1.0))


def modulation_weights(a, layer):
    return a["mod_w"][layer].rearrange("(p k) n -> p k n", k=KT)


def modulation(nc, m, a, layer):
    blocks = 6 * D // HALF
    ctx_blocks = 2 * D // HALF if layer == 0 else 0
    weights, first = modulation_weights(a, layer), MOD_FIRST[layer]
    wide = [(n, who) for n in range(blocks) for who in range(2 if n < ctx_blocks else 1)]
    pairs_before, wide_before = layer * blocks, layer * (blocks + 2 * D // HALF)
    with ExitStack() as scope:
        rows = scope.enter_context(nc.sbuf_tensor(f"mod_pairs{layer}", [3, 6 * D], F32))
        block = scope.enter_context(nc.Block(no_gpsimd_drain=True))

        @block.sync
        def _(sp):
            if layer == 0:
                for n in range(2):
                    load_block(m, sp, first + n, block_of(weights, n))
            sp.dma_start(rows[2:3, :], a["mod_b"][layer:layer + 1, :]).then_inc(m.mod_bias_landed, 16)
            for n in range(2, blocks):
                sp.wait_ge(m.mod_pair_ready, pairs_before + n - 1)
                load_block(m, sp, first + n, block_of(weights, n))
            for n in range(2):
                sp.wait_ge(m.mod_pair_ready, pairs_before + blocks - 1 + n)
                if layer == 0:
                    load_block(m, sp, PROJECT_FIRST + n, block_of(feature_major(a["ab_w_in"][0]), n))
                else:
                    load_block(m, sp, HYENA_FIRST + n, block_of(feature_major(a["hy_w_in"][0]), n))

        @block.tensor
        def _(pe):
            pe.wait_ge(m.mod_bias_landed, 16 * (layer + 1))

            def repeat(i):
                n, who = wide[i]
                pe.wait_ge(m.mod_pair_taken, pairs_before + n + 1)
                if i >= 2:
                    pe.wait_ge(m.mod_row_taken, wide_before + i - 1)
                pe.matmul(m.psum[:, 2 + i % 2, :], m.picks[0:3, who, :], rows[:, n * HALF:(n + 1) * HALF],
                          start=True, stop=True).then_inc(m.mod_row_ready, 1)

            for n in range(blocks + 1):
                if n < blocks:
                    w = wait_block(m, pe, first + n)
                    if n >= 2:
                        pe.wait_ge(m.mod_pair_taken, pairs_before + n - 1)
                    for k in range(KT):
                        mm = pe.matmul(m.psum[0:2, n % 2, :], m.cond_silu[:, k, :], w[:, k, :], start=k == 0, stop=k == KT - 1)
                    mm.then_inc(m.mod_pair_ready, 1)
                for i in range(len(wide)):
                    if wide[i][0] == n - 1:
                        repeat(i)

        @block.vector
        def _(dve):
            for n in range(blocks + 1):
                if n < blocks:
                    dve.wait_ge(m.mod_pair_ready, pairs_before + n + 1)
                    dve.tensor_copy(rows[0:2, n * HALF:(n + 1) * HALF], m.psum[0:2, n % 2, :]).then_inc(m.mod_pair_taken, 1)
                for i, (row_n, who) in enumerate(wide):
                    if row_n == n - 1:
                        dve.wait_ge(m.mod_row_ready, wide_before + i + 1)
                        is_scale = row_n * HALF // D in (1, 4)
                        cols = slice(row_n * HALF, (row_n + 1) * HALF)
                        out = m.mod[:, cols] if who == 0 else m.xm[:, 2:4, :].rearrange("p t d -> p (t d)")[:, cols]
                        dve.tensor_scalar_add(out, m.psum[:, 2 + i % 2, :], 1.0 if is_scale else 0.0).then_inc(m.mod_row_taken, 1)


def project(nc, m, a):
    blocks = 5
    weights = feature_major(a["ab_w_in"][0])
    products = [(0, "q", f) for f in range(4)] + [(1, part, f) for f in range(4) for part in ("k", "kc")]
    products += [(2, "v", t) for t in range(TT + CT)] + [(3, "u", t) for t in range(TT)] + [(4, "g", t) for t in range(TT)]
    with ExitStack() as scope:
        h = scope.enter_context(nc.sbuf_tensor("h_rows0", [P, 2, D], F32))
        block = scope.enter_context(nc.Block(no_gpsimd_drain=True))

        @block.sync
        def _(sp):
            for n in range(2, blocks + 2):
                last = max(i for i, product in enumerate(products) if product[0] == n - 2)
                sp.wait_ge(m.proj_ready, last + 1)
                if n < blocks:
                    load_block(m, sp, PROJECT_FIRST + n, block_of(weights, n))
                else:
                    load_block(m, sp, RESIDUAL_FIRST[0] + n - blocks, block_of(feature_major(a["ab_w_out"][0]), n - blocks))

        @block.vector
        def _(dve):
            modulate_rows_vector(m, dve, h, TT + CT)

        @block.tensor
        def _(pe):
            for t in range(TT + CT):
                pe.wait_ge(m.rows_ready, m.rows_before + t + 1)
                transpose_tile_tensor(m, pe, h[:, t % 2, :], t)
            pe.wait_ge(m.columns_ready, m.turned_before + 2 * (TT + CT))
            for i, (n, what, j) in enumerate(products):
                w = wait_block(m, pe, PROJECT_FIRST + n)
                if i >= 4:
                    pe.wait_ge(m.proj_taken, i - 3)
                for k in range(KT):
                    if what == "q":
                        out, left, right = m.psum[:, i % 4, :], w[:, k, j * P:(j + 1) * P], m.cols[:, k, 0:SEQ]
                    elif what == "k":
                        out, left, right = m.psum[:, i % 4, :], w[:, k, j * P:(j + 1) * P], m.cols[:, k, 0:SEQ]
                    elif what == "kc":
                        out, left, right = m.psum[:, i % 4, 0:CTX], w[:, k, j * P:(j + 1) * P], m.cols[:, k, SEQ:KEYS_ALL]
                    else:
                        out, left, right = m.psum[:, i % 4, :], m.cols[:, k, j * P:(j + 1) * P], w[:, k, :]
                    mm = pe.matmul(out, left, right, start=k == 0, stop=k == KT - 1)
                mm.then_inc(m.proj_ready, 1)

        @block.scalar
        def _(act):
            for t in range(TT + CT):
                transpose_tile_scalar(m, act, t, t)
            for i, (n, what, j) in enumerate(products):
                act.wait_ge(m.proj_ready, i + 1)
                bank = m.psum[:, i % 4, :]
                if what == "q":
                    act.mul(m.q_cols[:, j, :], bank, HEAD_DIM ** -0.5).then_inc(m.proj_taken, 1)
                elif what == "k":
                    act.copy(m.k_cols[:, j, 0:SEQ], bank).then_inc(m.proj_taken, 1)
                elif what == "kc":
                    act.copy(m.k_cols[:, j, SEQ:KEYS_ALL], bank[:, 0:CTX]).then_inc(m.proj_taken, 1)
                elif what == "v":
                    act.copy(m.v_rows[:, j, :], bank).then_inc(m.proj_taken, 1)
                else:
                    half = m.gate_rows[:, j, (0 if what == "u" else HALF):(HALF if what == "u" else D)]
                    act.activation(half, bank, ACT.Gelu).then_inc(m.proj_taken, 1)
    m.rows_before += TT + CT
    m.turned_before += 2 * (TT + CT)


def modulate_rows_vector(m, dve, h, tiles):
    for t in range(tiles):
        if t >= 2:
            dve.wait_ge(m.rows_transposed, m.turned_before + 2 * (t - 1))
        if t < TT:
            rows, shift, scale = m.x[:, t, :], m.mod[:, 0:D], m.mod[:, D:2 * D]
        else:
            rows, shift, scale = m.xm[:, t - TT, :], m.xm[:, 2, :], m.xm[:, 3, :]
        m.vector.link(dve, dve.tensor_tensor(h[:, t % 2, :], rows, scale, ALU.mult))
        dve.tensor_tensor(h[:, t % 2, :], h[:, t % 2, :], shift, ALU.add).then_inc(m.rows_ready, 1)


def transpose_tile_tensor(m, pe, rows, i):
    for half in range(2):
        n = 2 * i + half
        if n >= 4:
            pe.wait_ge(m.columns_ready, m.turned_before + n - 3)
        for k in range(4):
            tile = rows[:, (4 * half + k) * P:(4 * half + k + 1) * P]
            mm = pe.transpose(m.psum[:, 4 + n % 4, k * P:(k + 1) * P], tile, m.ident[:])
        mm.then_inc(m.rows_transposed, 1)


def transpose_tile_scalar(m, act, t, i):
    for half in range(2):
        n = 2 * i + half
        act.wait_ge(m.rows_transposed, m.turned_before + n + 1)
        bank = m.psum[:, 4 + n % 4, :].rearrange("p (k n) -> p k n", k=4)
        act.copy(m.cols[:, 4 * half:4 * half + 4, t * P:(t + 1) * P], bank).then_inc(m.columns_ready, 1)


def mix(nc, m, a):
    items = [(head, t) for head in range(HEADS) for t in range(TT)]
    with ExitStack() as scope:
        table = scope.enter_context(nc.sbuf_tensor("bias_table", [P, 2, TAB, GRID_W], F32))
        window = scope.enter_context(nc.sbuf_tensor("window", [P, GRID_W], F32))
        w_s = scope.enter_context(nc.sbuf_tensor("w_s_sb", [P, GROUPS, P], F32))
        b_s = scope.enter_context(nc.sbuf_tensor("b_s_sb", [P, GROUPS], F32))
        logits = scope.enter_context(nc.sbuf_tensor("logits", [P, 3, KEYS_ALL], F32))
        probs_t = scope.enter_context(nc.sbuf_tensor("probs_t", [P, 2, KEYS_ALL], F32))
        neg_max = scope.enter_context(nc.sbuf_tensor("neg_max", [P, 3], F32))
        row_sum = scope.enter_context(nc.sbuf_tensor("row_sum", [P, 3], F32))
        inv_sum = scope.enter_context(nc.sbuf_tensor("inv_sum", [P, 2], F32))
        stats = scope.enter_context(nc.sbuf_tensor("gv_stats", [P, TT, 6], F32))
        moments = scope.enter_context(nc.sbuf_tensor("gv_moments", [P, TT, 2], F32))
        block = scope.enter_context(nc.Block(no_gpsimd_drain=True))
        ctx_scores = [m.psum[:, 3, 0:CTX], m.psum[:, 4, 0:CTX]]
        turn_bank, out_bank, mixed_bank = (5, 6), 7, 7

        @block.sync
        def _(sp):
            sp.dma_start(window[:], a["window"]).then_inc(m.mix_consts_landed, 16)
            sp.dma_start(w_s[:], a["gm_w_s_t"].rearrange("g q p -> q g p")).then_inc(m.mix_consts_landed, 16)
            sp.dma_start(b_s[:], a["gm_b_s_t"]).then_inc(m.mix_consts_landed, 16)
            for head in range(HEADS):
                if head >= 2:
                    sp.wait_ge(m.scores_biased, TT * (head - 1))
                for r2 in range(2):
                    source = a["rpb_shifted"][head, :, 1 - r2:1 - r2 + TAB, :]
                    sp.dma_start(table[r2 * GRID_W:(r2 + 1) * GRID_W, head % 2], source).then_inc(m.table_landed[head % 2], 16)

        @block.vector
        def _(dve):
            for t in range(TT):
                m.vector.mark(dve.bn_stats(stats[:, t, :], m.gate_rows[:, t, HALF:D]))
            m.vector.wait(dve)
            for t in range(TT):
                m.vector.mark(dve.bn_aggr(moments[:, t, :], stats[:, t, :]))
            m.vector.wait(dve)
            dve.tensor_scalar_add(moments[:, :, 1], moments[:, :, 1], EPS).then_inc(m.gv_var_ready, 1)
            dve.wait_ge(m.gv_std_ready, 1)
            m.vector.link(dve, dve.reciprocal(moments[:, :, 1], moments[:, :, 1]))
            for t in range(TT):
                gv = m.gate_rows[:, t, HALF:D]
                dve.tensor_scalar(gv, gv, moments[:, t, 0:1], moments[:, t, 1:2], ALU.subtract, ALU.mult).then_inc(m.gv_ready, 1)
            dve.wait_ge(m.mix_consts_landed, 48)

            def gate(t):
                dve.wait_ge(m.mixed_ready, t + 1)
                for g in range(GROUPS):
                    cols = slice(g * P, (g + 1) * P)
                    last = dve.scalar_tensor_tensor(m.xm[:, t, HALF + g * P:HALF + (g + 1) * P], m.psum[:, mixed_bank, cols],
                                                    b_s[:, g:g + 1], m.gate_rows[:, t, cols], ALU.add, ALU.mult)
                last.then_inc(m.mixed_taken, 1)

            def bias_scores(i):
                head, t = items[i]
                if t == 0:
                    dve.wait_ge(m.table_landed[head % 2], 32 * (head // 2 + 1))
                    mask = window[:].unsqueeze(1).to_broadcast([P, TAB, GRID_W])
                    m.vector.link(dve, dve.tensor_tensor(table[:, head % 2], table[:, head % 2], mask, ALU.add))
                dve.wait_ge(m.scores_ready, i + 1)
                if i >= 3:
                    dve.wait_ge(m.probs_turned, 2 * (i - 2))
                j = 2 * (TT - 1 - t)
                rows = table[:, head % 2, j:j + GRID_ROWS, :].rearrange("p r c -> p (r c)")
                dve.tensor_tensor(logits[:, i % 3, 0:SEQ], m.psum[:, i % 3, :], rows, ALU.add).then_inc(m.scores_biased, 1)
                dve.wait_ge(m.scores_biased, i + 1)
                dve.wait_ge(m.ctx_scores_taken, i + 1)
                m.vector.link(dve, dve.reduce_max(neg_max[:, i % 3:i % 3 + 1], logits[:, i % 3, :], AX_X))
                dve.tensor_scalar_mul(neg_max[:, i % 3:i % 3 + 1], neg_max[:, i % 3:i % 3 + 1], -1.0).then_inc(m.max_ready, 1)

            def take_turned(i):
                dve.wait_ge(m.probs_turned, 2 * i + 1)
                if i >= 2:
                    dve.wait_ge(m.heads_out_ready, i - 1)
                dve.tensor_copy(probs_t[:, i % 2, 0:HALF], m.psum[:, turn_bank[0], :]).then_inc(m.turned_taken_vector, 1)
                dve.wait_ge(m.probs_ready, i + 1)
                m.vector.mark(dve.reciprocal(inv_sum[:, i % 2:i % 2 + 1], row_sum[:, i % 3:i % 3 + 1]))

            def take_out(i):
                head, t = items[i]
                dve.wait_ge(m.heads_out_ready, i + 1)
                dve.tensor_scalar(m.xm[:, t, head * HEAD_DIM:(head + 1) * HEAD_DIM],
                                  m.psum[:, out_bank, 0:HEAD_DIM],
                                  inv_sum[:, i % 2:i % 2 + 1], None, ALU.mult).then_inc(m.heads_out_taken, 1)

            bias_scores(0)
            bias_scores(1)
            for t in range(TT):
                gate(t)
            for i in range(len(items) + 1):
                if i + 2 < len(items):
                    bias_scores(i + 2)
                if i >= 1:
                    m.vector.wait(dve)
                    take_out(i - 1)
                if i < len(items):
                    take_turned(i)

        @block.scalar
        def _(act):
            act.wait_ge(m.gv_var_ready, 1)
            act.activation(moments[:, :, 1], moments[:, :, 1], ACT.Sqrt).then_inc(m.gv_std_ready, 1)

            def take_ctx(i):
                act.wait_ge(m.scores_ready, i + 1)
                if i >= 3:
                    act.wait_ge(m.probs_turned, 2 * (i - 2))
                act.copy(logits[:, i % 3, SEQ:KEYS_ALL], ctx_scores[i % 2]).then_inc(m.ctx_scores_taken, 1)

            def exponentials(i):
                act.wait_ge(m.max_ready, i + 1)
                if i >= 3:
                    act.wait_ge(m.heads_out_taken, i - 2)
                act.activation(logits[:, i % 3, :], logits[:, i % 3, :], ACT.Exp, bias=neg_max[:, i % 3:i % 3 + 1],
                               accum_out=row_sum[:, i % 3:i % 3 + 1]).then_inc(m.probs_ready, 1)

            def take_turned(i):
                act.wait_ge(m.probs_turned, 2 * i + 2)
                if i >= 2:
                    act.wait_ge(m.heads_out_ready, i - 1)
                act.copy(probs_t[:, i % 2, HALF:KEYS_ALL], m.psum[:, turn_bank[1], 0:CTX]).then_inc(m.turned_taken_scalar, 1)

            take_ctx(0)
            take_ctx(1)
            exponentials(0)
            for i in range(len(items)):
                if i + 2 < len(items):
                    take_ctx(i + 2)
                if i + 1 < len(items):
                    exponentials(i + 1)
                take_turned(i)

        def scores(pe, i):
            head, t = items[i]
            part = slice((head % 2) * HEAD_DIM, (head % 2 + 1) * HEAD_DIM)
            if i >= 3:
                pe.wait_ge(m.scores_biased, i - 2)
            if i >= 2:
                pe.wait_ge(m.ctx_scores_taken, i - 1)
            q = m.q_cols[part, head // 2, t * P:(t + 1) * P]
            pe.matmul(m.psum[:, i % 3, :], q, m.k_cols[part, head // 2, 0:SEQ], start=True, stop=True)
            pe.matmul(ctx_scores[i % 2], q, m.k_cols[part, head // 2, SEQ:KEYS_ALL], start=True, stop=True).then_inc(m.scores_ready, 1)

        def weighted_values(pe, i):
            head, t = items[i]
            pe.wait_ge(m.turned_taken_vector, i + 1)
            pe.wait_ge(m.turned_taken_scalar, i + 1)
            if i == 0:
                pe.wait_ge(m.mixed_taken, TT)
            if i >= 1:
                pe.wait_ge(m.heads_out_taken, i)
            for c in range(KEYS_ALL // P):
                mm = pe.matmul(m.psum[:, out_bank, 0:HEAD_DIM],
                               probs_t[:, i % 2, c * P:(c + 1) * P], m.v_rows[:, c, head * HEAD_DIM:(head + 1) * HEAD_DIM],
                               start=c == 0, stop=c == KEYS_ALL // P - 1)
            mm.then_inc(m.heads_out_ready, 1)

        @block.tensor
        def _(pe):
            pe.wait_ge(m.mix_consts_landed, 48)
            for t in range(TT):
                pe.wait_ge(m.gv_ready, t + 1)
                if t >= 1:
                    pe.wait_ge(m.mixed_taken, t)
                for g in range(GROUPS):
                    mm = pe.matmul(m.psum[:, mixed_bank, g * P:(g + 1) * P], w_s[:, g, :],
                                   m.gate_rows[:, t, HALF + g * P:HALF + (g + 1) * P], start=True, stop=True)
                mm.then_inc(m.mixed_ready, 1)
                if t == 0:
                    scores(pe, 0)
                    scores(pe, 1)
            for i in range(len(items) + 1):
                if i + 2 < len(items):
                    scores(pe, i + 2)
                if i < len(items):
                    pe.wait_ge(m.probs_ready, i + 1)
                    if i >= 1:
                        pe.wait_ge(m.turned_taken_vector, i)
                        pe.wait_ge(m.turned_taken_scalar, i)
                    for c in range(KEYS_ALL // P):
                        mm = pe.transpose(m.psum[:, turn_bank[c // 4], (c % 4) * P:(c % 4 + 1) * P],
                                          logits[:, i % 3, c * P:(c + 1) * P], m.ident[:])
                        if c == 3 or c == 5:
                            mm.then_inc(m.probs_turned, 1)
                if i >= 1:
                    weighted_values(pe, i - 1)


def norm_tile_vector(m, dve, t, gate_row, ln, scratch, banks, moments, stats):
    x = m.x[:, t, :]
    for half in range(2):
        cols = slice(half * HALF, (half + 1) * HALF)
        m.vector.mark(dve.tensor_tensor(scratch[:, cols], m.psum[:, banks[half], :], gate_row[:, cols], ALU.mult))
    m.vector.wait(dve)
    m.vector.link(dve, dve.scalar_tensor_tensor(x, x, ALPHA, scratch[:], ALU.mult, ALU.add))
    for half in range(2):
        m.vector.mark(dve.bn_stats(stats[:, half, :], m.x[:, t, half * HALF:(half + 1) * HALF]))
    m.vector.wait(dve)
    m.vector.link(dve, dve.bn_aggr(moments[:], stats[:]))
    dve.tensor_scalar_add(moments[:, 1:2], moments[:, 1:2], EPS).then_inc(m.var_ready, 1)
    m.norms += 1
    dve.wait_ge(m.std_ready, m.norms)
    m.vector.link(dve, dve.reciprocal(moments[:, 1:2], moments[:, 1:2]))
    m.vector.link(dve, dve.tensor_scalar(x, x, moments[:, 0:1], moments[:, 1:2], ALU.subtract, ALU.mult))
    m.vector.link(dve, dve.tensor_tensor(x, x, ln[:, 0, :], ALU.mult))
    return dve.tensor_tensor(x, x, ln[:, 1, :], ALU.add)


def norm_tile_scalar(m, act, moments):
    m.roots += 1
    act.wait_ge(m.var_ready, m.roots)
    act.activation(moments[:, 1:2], moments[:, 1:2], ACT.Sqrt).then_inc(m.std_ready, 1)


def residual(nc, m, a, layer):
    turned_first = TT if layer == 0 else 0
    with ExitStack() as scope:
        ln = scope.enter_context(nc.sbuf_tensor(f"ln_mix{layer}", [P, 2, D], F32))
        scratch = scope.enter_context(nc.sbuf_tensor(f"scratch_mix{layer}", [P, D], F32))
        stats = scope.enter_context(nc.sbuf_tensor(f"stats_mix{layer}", [P, 2, 6], F32))
        moments = scope.enter_context(nc.sbuf_tensor(f"moments_mix{layer}", [P, 2], F32))
        block = scope.enter_context(nc.Block(no_gpsimd_drain=True))

        @block.sync
        def _(sp):
            sp.dma_start(ln[:, 0, :], a["ln_g"][layer, 0:1, :].to_broadcast([P, D])).then_inc(m.ln_landed, 16)
            sp.dma_start(ln[:, 1, :], a["ln_b"][layer, 0:1, :].to_broadcast([P, D])).then_inc(m.ln_landed, 16)
            sp.wait_ge(m.mix_out_ready, (layer + 1) * TT)
            for n in range(2):
                load_block(m, sp, SCORES_FIRST[layer] + n, block_of(feature_major(a["peer_wq"][layer]), n))

        @block.tensor
        def _(pe):
            for t in range(turned_first):
                transpose_tile_tensor(m, pe, m.xm[:, t, :], t)
            w = [wait_block(m, pe, RESIDUAL_FIRST[layer] + half) for half in range(2)]
            for t in range(TT + 1):
                if t < TT:
                    if layer == 0:
                        pe.wait_ge(m.columns_ready, m.turned_before + 2 * (t + 1))
                    if t >= 2:
                        pe.wait_ge(m.tile_modulated, layer * TT + t - 1)
                    for half in range(2):
                        for k in range(KT):
                            mm = pe.matmul(m.psum[:, 2 * (t % 2) + half, :], m.cols[:, k, t * P:(t + 1) * P],
                                           w[half][:, k, :], start=k == 0, stop=k == KT - 1)
                    mm.then_inc(m.mix_out_ready, 1)
                if t >= 1:
                    pe.wait_ge(m.tile_modulated, layer * TT + t)
                    transpose_tile_tensor(m, pe, m.xm[:, t - 1, :], turned_first + t - 1)

        @block.vector
        def _(dve):
            dve.wait_ge(m.ln_landed, 32 * (2 * layer + 1))
            for t in range(TT):
                dve.wait_ge(m.mix_out_ready, layer * TT + t + 1)
                m.vector.link(dve, norm_tile_vector(m, dve, t, m.mod[:, 2 * D:3 * D], ln, scratch,
                                                    (2 * (t % 2), 2 * (t % 2) + 1), moments, stats))
                m.vector.link(dve, dve.tensor_tensor(m.xm[:, t, :], m.x[:, t, :], m.mod[:, 4 * D:5 * D], ALU.mult))
                dve.tensor_tensor(m.xm[:, t, :], m.xm[:, t, :], m.mod[:, 3 * D:4 * D], ALU.add).then_inc(m.tile_modulated, 1)

        @block.scalar
        def _(act):
            for t in range(turned_first):
                transpose_tile_scalar(m, act, t, t)
            for t in range(TT):
                norm_tile_scalar(m, act, moments)
                transpose_tile_scalar(m, act, t, turned_first + t)
    m.turned_before += 2 * (turned_first + TT)


def score_keys(nc, m, a, layer):
    weights = feature_major(a["peer_wq"][layer])
    blocks = HP * P // HALF
    with ExitStack() as scope:
        keys = scope.enter_context(nc.sbuf_tensor(f"keys{layer}", [P, HP, NKEYS], F32))
        query = scope.enter_context(nc.sbuf_tensor(f"query{layer}", [P, 2, SEQ], F32))
        block = scope.enter_context(nc.Block(no_gpsimd_drain=True))
        done = layer * HP

        @block.sync
        def _(sp):
            sp.dma_start(keys[:], a["peer_keys_t"][layer].rearrange("h d k -> d h k")).then_inc(m.keys_landed, 16)
            for n in range(2, blocks):
                sp.wait_ge(m.query_ready, done + 4 * (n - 1))
                load_block(m, sp, SCORES_FIRST[layer] + n, block_of(weights, n))

        @block.tensor
        def _(pe):
            for i in range(HP + 1):
                if i < HP:
                    w = wait_block(m, pe, SCORES_FIRST[layer] + i // 4)
                    if i >= 2:
                        pe.wait_ge(m.query_taken, done + i - 1)
                    for k in range(KT):
                        mm = pe.matmul(m.psum[:, i % 2, :], w[:, k, (i % 4) * P:(i % 4 + 1) * P],
                                       m.cols[:, k, 0:SEQ], start=k == 0, stop=k == KT - 1)
                    mm.then_inc(m.query_ready, 1)
                if i >= 1:
                    j = i - 1
                    if j == 0:
                        pe.wait_ge(m.keys_landed, 16 * (layer + 1))
                    pe.wait_ge(m.query_taken, done + j + 1)
                    if j >= 2:
                        pe.wait_ge(m.key_scores_taken, done + j - 1)
                    for t in range(TT):
                        mm = pe.matmul(m.psum[:, 2 + j % 2, t * P:(t + 1) * P], query[:, j % 2, t * P:(t + 1) * P],
                                       keys[:, j, :], start=True, stop=True)
                    mm.then_inc(m.key_scores_ready, 1)

        @block.scalar
        def _(act):
            for i in range(HP):
                act.wait_ge(m.query_ready, done + i + 1)
                if i >= 2:
                    act.wait_ge(m.key_scores_ready, done + i - 1)
                act.copy(query[:, i % 2, :], m.psum[:, i % 2, :]).then_inc(m.query_taken, 1)

        @block.vector
        def _(dve):
            m.vector.mark(dve.memset(m.scores[:, TT * 4, :], 0.0))
            by_tile = m.scores[:, 0:TT * 4, :].rearrange("p (t q) (j k) -> p t q j k", t=TT, j=4)
            for i in range(HP):
                dve.wait_ge(m.key_scores_ready, done + i + 1)
                dve.tensor_copy(by_tile[:, :, i // 4, i % 4, :],
                                m.psum[:, 2 + i % 2, :].rearrange("p (t k) -> p t k", t=TT)).then_inc(m.key_scores_taken, 1)


def experts(nc, m, a, layer):
    sections = SLOTS // 32
    groups = 32 // RING
    u_table, v_table = a[f"peer_u{layer}"], a[f"peer_v{layer}"]
    with ExitStack() as scope:
        def sb(name, shape, dtype=F32):
            return scope.enter_context(nc.sbuf_tensor(f"{name}{layer}", shape, dtype))
        idx = sb("idx", [P, (4 * TT + 1) * 32], U32)
        gates = sb("gates", [P, (4 * TT + 1) * 32])
        v_ring = sb("v_ring", [P, RING, D])
        current = sb("current", [P, 2, RING], U32)
        dots = sb("dots", [P, 2, RING])
        acted = sb("acted", [P, 2, RING])
        weights = sb("weights", [P, 2, RING])
        columns = m.cols[:].rearrange("p k n -> p (k n)")
        ln = columns[:, 0:2 * D].rearrange("p (g d) -> p g d", g=2)
        diagonal = columns[:, 2 * D:4 * D].rearrange("p (g j k) -> p g j k", g=2, j=RING)
        scratch = columns[:, 4 * D:5 * D]
        first = columns[:, 5 * D:5 * D + HALF].rearrange("p (j k) -> p j k", j=4)
        rest = columns[:, 5 * D + HALF:6 * D].rearrange("p (j k) -> p j k", j=4)
        zeros = sb("zeros", [1, HALF])
        stats = sb("stats_peer", [P, 2, 6])
        moments = sb("moments_peer", [P, 2])
        top = sb("top", [P, 4, TOPK])
        top_at = sb("top_at", [P, 4, TOPK], U32)
        top_at_f = sb("top_at_f", [P, 4, TOPK])
        sums = sb("sums", [P, 2, TOPK * TOPK])
        sums_rest = sb("sums_rest", [P, 2, TOPK * TOPK])
        best = sb("best", [P, 2, TOPK])
        best_at = sb("best_at", [P, 2, TOPK], U32)
        digits = sb("digits", [P, 2, 2, TOPK], U32)
        digits_f = sb("digits_f", [P, 2, 2, TOPK])
        match = sb("match", [P, 2, TOPK, TOPK])
        found = sb("found", [P, 2, 2 * TOPK])
        expd = sb("expd", [P, 2, TOPK])
        denom = sb("denom", [P, 2])
        u_ring = [m.ring[:, j // 4, 2 * (j % 4):2 * (j % 4) + 2, :].rearrange("p k n -> p (k n)") for j in range(RING)]
        block = scope.enter_context(nc.Block(no_gpsimd_drain=True))
        groups_before = layer * TT * sections * groups
        sections_before = layer * (TT * sections + 1)

        def rounds(dve, values, remaining, tops, ats, n):
            for i in range(n):
                m.select.mark(dve.max(tops[:, i, 0:8], values[:, i, :]))
            m.select.wait(dve)
            for i in range(n):
                m.select.mark(dve.max_index(ats[:, i, 0:8], tops[:, i, 0:8], values[:, i, :]))
                m.select.mark(dve.match_replace(remaining[:, i, :], tops[:, i, 0:8], values[:, i, :], LOWEST))
            m.select.wait(dve)
            for i in range(n):
                m.select.mark(dve.max(tops[:, i, 8:16], remaining[:, i, :]))
            m.select.wait(dve)
            for i in range(n):
                m.select.mark(dve.max_index(ats[:, i, 8:16], tops[:, i, 8:16], remaining[:, i, :]))
            m.select.wait(dve)

        def select(dve, section, nth):
            m.select.begin(nth)
            select_keys(dve, section)
            select_experts(dve, section, nth)

        def select_keys(dve, section):
            m.select.link(dve, dve.tensor_copy(columns[:, 5 * D:5 * D + HALF], m.scores[:, bass.ds(section, 1), :].squeeze(1)))
            rounds(dve, first, rest, top, top_at, 4)

        def select_experts(dve, section, nth):
            m.select.mark(dve.tensor_copy(top_at_f[:], top_at[:]))
            sets = top[:].rearrange("p (h s) r -> p h s r", s=2)
            sets_at = top_at_f[:].rearrange("p (h s) r -> p h s r", s=2)
            square = [P, 2, TOPK, TOPK]
            m.select.link(dve, dve.tensor_tensor(sums[:].rearrange("p h (r s) -> p h r s", r=TOPK),
                                                 sets[:, :, 0, :].unsqueeze(3).to_broadcast(square),
                                                 sets[:, :, 1, :].unsqueeze(2).to_broadcast(square), ALU.add))
            rounds(dve, sums, sums_rest, best, best_at, 2)
            dve.tensor_tensor(expd[:], best[:], best[:, :, 0:1].to_broadcast([P, 2, TOPK]), ALU.subtract).then_inc(m.shifted_ready, 1)
            m.select.mark(dve.tensor_single_scalar(digits[:, 0], best_at[:], 4, ALU.logical_shift_right))
            m.select.mark(dve.tensor_single_scalar(digits[:, 1], best_at[:], TOPK - 1, ALU.bitwise_and))
            m.select.wait(dve)
            m.select.link(dve, dve.tensor_copy(digits_f[:], digits[:]))
            for s in range(2):
                ranks = m.ranks[:].unsqueeze(1).unsqueeze(1).to_broadcast(square)
                m.select.link(dve, dve.tensor_tensor(match[:], digits_f[:, s].unsqueeze(3).to_broadcast(square), ranks, ALU.is_equal))
                m.select.link(dve, dve.tensor_tensor(match[:], match[:], sets_at[:, :, s, :].unsqueeze(2).to_broadcast(square), ALU.mult))
                m.select.link(dve, dve.tensor_reduce(found[:, s, :], match[:].rearrange("p h r s -> p (h r) s"), AX_X, ALU.add))
            m.select.link(dve, dve.scalar_tensor_tensor(found[:, 0, :], found[:, 0, :], float(NKEYS), found[:, 1, :], ALU.mult, ALU.add))
            m.select.mark(dve.tensor_copy(idx[:, bass.ds(section * 32, 32)], found[:, 0, :]))
            dve.wait_ge(m.exps_ready, nth)
            m.select.link(dve, dve.tensor_reduce(denom[:], expd[:], AX_X, ALU.add))
            m.select.link(dve, dve.reciprocal(denom[:], denom[:]))
            dve.tensor_tensor(gates[:, bass.ds(section * 32, 32)].rearrange("p (h r) -> p h r", h=2), expd[:],
                              denom[:].unsqueeze(2).to_broadcast([P, 2, TOPK]), ALU.mult).then_inc(m.section_selected, 1)

        @block.sync
        def _(sp):
            sp.dma_start(ln[:, 0, :], a["ln_g"][layer, 1:2, :].to_broadcast([P, D])).then_inc(m.ln_landed, 16)
            sp.dma_start(ln[:, 1, :], a["ln_b"][layer, 1:2, :].to_broadcast([P, D])).then_inc(m.ln_landed, 16)
            if layer == 0:
                sp.wait_ge(m.dots_done, (TT * sections * groups + 1) * RING)
                for n in range(2):
                    load_block(m, sp, MOD_FIRST[1] + n, block_of(modulation_weights(a, 1), n))
            if layer == 1:
                for t in range(TT):
                    sp.wait_ge(m.tile_done, TT + t + 1)
                    sp.dma_start(a["out"][0, t * P:(t + 1) * P, :], m.x[:, t, :]).then_inc(m.out_stored, 16)
                sp.wait_ge(m.out_stored, 16 * TT)

        @block.gpsimd
        def _(pool):
            with pool.Fori(0, TT * sections) as s:
                pool.wait_ge(m.section_selected, sections_before + s + 1)
                for g in range(groups):
                    group = groups_before + s * groups + g
                    pool.tensor_copy(current[:, g % 2, :], idx[:, bass.ds(s * 32 + g * RING, RING)]).then_inc(m.current_ready, 1)
                    pool.wait_ge(m.dots_done, (group + 1) * RING)
                    pool.wait_ge(m.current_ready, group + 1)
                    pool.nop(nofuse=True)
                    for j in range(RING):
                        pool.indirect_dma_start(out=u_ring[j], out_offset=None, in_=u_table,
                                                in_offset=bass.IndirectOffsetOnAxis(ap=current[:, g % 2, j:j + 1], axis=0)).then_inc(m.u_landed[j], 16)
                    pool.wait_ge(m.v_used, (group + 2) * RING)
                    pool.nop(nofuse=True)
                    for j in range(RING):
                        pool.indirect_dma_start(out=v_ring[:, j, :], out_offset=None, in_=v_table,
                                                in_offset=bass.IndirectOffsetOnAxis(ap=current[:, g % 2, j:j + 1], axis=0)).then_inc(m.v_landed[j], 16)

        def norm(dve, t):
            if t == 0:
                dve.wait_ge(m.ln_landed, 32 * (2 * layer + 2))
            dve.wait_ge(m.experts_ready, layer * TT + t + 1)
            norm_tile_vector(m, dve, t, m.mod[:, 5 * D:6 * D], ln, scratch, (2 * t, 2 * t + 1), moments, stats).then_inc(m.tile_done, 1)

        @block.vector
        def _(dve):
            m.vector.mark(dve.memset(zeros[:], 0.0))
            if layer == 0:
                dve.memset(found[:], 0.0).then_inc(m.dots_done, RING)
                dve.memset(match[:], 0.0).then_inc(m.v_used, 2 * RING)
            m.vector.wait(dve)
            dve.engine_nop().then_inc(m.zeros_ready, 1)
            select(dve, 0, sections_before + 1)
            for t in range(TT):
                with dve.Fori(0, sections) as q:
                    section = t * sections + q
                    for g in range(groups):
                        group = groups_before + section * groups + g
                        for j in range(RING):
                            dve.wait_ge(m.u_landed[j], (group + 1) * 16)
                            dve.tensor_tensor_reduce(out=u_ring[j], in0=u_ring[j], in1=m.xm[:, t, :], scale=1.0, scalar=0.0,
                                                     op0=ALU.mult, op1=ALU.add, accum_out=dots[:, g % 2, j:j + 1]).then_inc(m.dots_done, 1)
                        dve.wait_ge(m.acted_ready, group + 1)
                        dve.tensor_tensor(weights[:, g % 2, :], acted[:, g % 2, :], gates[:, bass.ds(section * 32 + g * RING, RING)],
                                          ALU.mult).then_inc(m.weights_ready, 1)
                        if g == 0:
                            m.select.begin(sections_before + section + 2)
                            select_keys(dve, section + 1)
                        if g == 1:
                            select_experts(dve, section + 1, sections_before + section + 2)
                if t >= 1:
                    norm(dve, t - 1)
            norm(dve, TT - 1)

        @block.scalar
        def _(act):
            def exponentials(nth):
                act.wait_ge(m.shifted_ready, nth)
                act.activation(expd[:], expd[:], ACT.Exp).then_inc(m.exps_ready, 1)

            exponentials(sections_before + 1)
            for t in range(TT):
                with act.Fori(0, sections) as q:
                    for g in range(groups):
                        group = groups_before + (t * sections + q) * groups + g
                        act.wait_ge(m.dots_done, (group + 2) * RING)
                        act.activation(acted[:, g % 2, :], dots[:, g % 2, :], ACT.Gelu).then_inc(m.acted_ready, 1)
                        act.wait_ge(m.weights_ready, group + 1)
                        act.wait_ge(m.v_used, (group + 1) * RING)
                        for j in range(RING):
                            last = act.activation(diagonal[:, g % 2, j, :], m.ident[:], ACT.Copy, scale=weights[:, g % 2, j:j + 1])
                        last.then_inc(m.diagonals_ready, 1)
                        if g == 1:
                            exponentials(sections_before + t * sections + q + 2)
                if t >= 1:
                    norm_tile_scalar(m, act, moments)
            norm_tile_scalar(m, act, moments)

        @block.tensor
        def _(pe):
            pe.wait_ge(m.zeros_ready, layer + 1)
            for t in range(TT):
                for half in range(2):
                    pe.matmul(m.psum[:, 2 * t + half, :], zeros[:, 0:P], zeros[:], start=True, stop=False)
                with pe.Fori(0, sections) as q:
                    for g in range(groups):
                        group = groups_before + (t * sections + q) * groups + g
                        pe.wait_ge(m.diagonals_ready, group + 1)
                        for j in range(RING):
                            pe.wait_ge(m.v_landed[j], (group + 1) * 16)
                            for half in range(2):
                                mm = pe.matmul(m.psum[:, 2 * t + half, :], diagonal[:, g % 2, j, :],
                                               v_ring[:, j, half * HALF:(half + 1) * HALF], start=False, stop=False)
                            mm.then_inc(m.v_used, 1)
                for half in range(2):
                    mm = pe.matmul(m.psum[:, 2 * t + half, :], zeros[:, 0:P], zeros[:], start=False, stop=True)
                mm.then_inc(m.experts_ready, 1)


def sine_vector(m, dve, out, product, bias, freq, turns):
    m.vector.link(dve, dve.tensor_scalar(out, product, bias, freq, ALU.add, ALU.mult))
    m.vector.link(dve, dve.tensor_scalar(turns, out, 1 / (2 * np.pi), MAGIC, ALU.mult, ALU.add))
    m.vector.link(dve, dve.tensor_scalar_add(turns, turns, -MAGIC))
    for part in (TWO_PI_HIGH, TWO_PI_MID, TWO_PI_LOW):
        m.vector.link(dve, dve.scalar_tensor_tensor(out, turns, -part, out, ALU.mult, ALU.add))
    dve.tensor_scalar(out, out, PI_BELOW, -PI_BELOW, ALU.min, ALU.max).then_inc(m.angle_ready, 1)


def filter_spectrum(nc, m, a):
    with ExitStack() as scope:
        def sb(name, shape):
            return scope.enter_context(nc.sbuf_tensor(name, shape, F32))
        fwd, bwd = sb("fwd", [P, TT, D]), sb("bwd", [P, TT, D])
        w1, w2, ffn = sb("ffn_w1", [EMB, FFN]), sb("ffn_w2", [FFN, FFN]), sb("ffn_vectors", [FFN, 4])
        free = m.cols[:].rearrange("p k n -> p (k n)")
        decay = free[:, 0:2 * D].rearrange("p (s d) -> p s d", s=2)
        w3 = free[0:FFN, 2 * D:4 * D]
        scratch, inv_l1 = free[:, 4 * D:5 * D], free[:, 5 * D:6 * D]
        hidden = m.xm[0:FFN, 0, :].rearrange("p (s n) -> p s n", s=2)
        turns, position = m.xm[0:FFN, 1, 0:SEQ], m.xm[0:EMB, 1, SEQ:2 * SEQ]
        block = scope.enter_context(nc.Block(no_gpsimd_drain=True))

        @block.sync
        def _(sp):
            sp.dma_start(position, a["position"]).then_inc(m.ffn_landed, 16)
            sp.dma_start(w1[:], a["hy_ffn_w1"][0]).then_inc(m.ffn_landed, 16)
            sp.dma_start(w2[:], a["hy_ffn_w2"][0]).then_inc(m.ffn_landed, 16)
            sp.dma_start(w3, a["hy_ffn_w3"][0]).then_inc(m.ffn_landed, 16)
            sp.dma_start(ffn[:], a["ffn_vectors"]).then_inc(m.ffn_landed, 16)
            for t in range(TT):
                if t >= 2:
                    sp.wait_ge(m.filter_taken, 4 * (t - 1))
                sp.dma_start(decay[:, t % 2, :], a["decay"][t * P:(t + 1) * P, :]).then_inc(m.decay_landed[t % 2], 16)
            sp.dma_start(m.cos_in[:], a["cos_in"].rearrange("(t p) f -> p t f", p=P)).then_inc(m.dft_landed, 16)
            sp.dma_start(m.sin_in[:], a["sin_in"].rearrange("(t p) f -> p t f", p=P)).then_inc(m.dft_landed, 16)

        @block.tensor
        def _(pe):
            pe.wait_ge(m.ffn_landed, 80)
            pe.matmul(m.psum[0:FFN, 0, :], w1[:], position, start=True, stop=True).then_inc(m.hidden_ready, 1)
            pe.wait_ge(m.sine_ready, 1)
            pe.matmul(m.psum[0:FFN, 1, :], w2[:], hidden[:, 0, :], start=True, stop=True).then_inc(m.hidden_ready, 1)
            pe.wait_ge(m.sine_ready, 2)
            for t in range(TT):
                for n in range(4):
                    i = 4 * t + n
                    if i >= 2:
                        pe.wait_ge(m.filter_taken, i - 1)
                    pe.matmul(m.psum[:, i % 2, :], hidden[:, 1, t * P:(t + 1) * P], w3[:, n * HALF:(n + 1) * HALF],
                              start=True, stop=True).then_inc(m.filter_ready, 1)
            for t in range(TT):
                for b in range(2):
                    pe.wait_ge(m.abs_ready, 2 * t + b + 1)
                    for half in range(2):
                        mm = pe.matmul(m.psum[:, 2 + half, :], m.ones[:], scratch[:, half * HALF:(half + 1) * HALF],
                                       start=t == b == 0, stop=t == TT - 1 and b == 1)
                    mm.then_inc(m.abs_summed, 1)
            pe.wait_ge(m.parts_ready, 2 * TT)
            pe.wait_ge(m.dft_landed, 32)
            for ft in range(4):
                for half in range(2):
                    i = 2 * ft + half
                    cols = slice(half * HALF, (half + 1) * HALF)
                    if i >= 2:
                        pe.wait_ge(m.spectrum_taken, 2 * (i - 1))
                    for table, part, bank in ((m.cos_in, fwd, 4 + 2 * (i % 2)), (m.sin_in, bwd, 5 + 2 * (i % 2))):
                        for t in range(TT):
                            mm = pe.matmul(m.psum[:, bank, :], table[:, t, ft * P:(ft + 1) * P], part[:, t, cols],
                                           start=t == 0, stop=t == TT - 1)
                    mm.then_inc(m.spectrum_ready, 1)
            for half in range(2):
                for t in range(TT):
                    mm = pe.matmul(m.psum[0:1, half, :], m.sin_in[:, t, 0:1], fwd[:, t, half * HALF:(half + 1) * HALF],
                                   start=t == 0, stop=t == TT - 1)
            mm.then_inc(m.highest_ready, 1)

        @block.vector
        def _(dve):
            dve.wait_ge(m.ffn_landed, 80)
            for n in range(2):
                dve.wait_ge(m.hidden_ready, n + 1)
                sine_vector(m, dve, hidden[:, n, :], m.psum[0:FFN, n, :], ffn[:, 2 * n:2 * n + 1], ffn[:, 2 * n + 1:2 * n + 2], turns)
            for t in range(TT):
                dve.wait_ge(m.decay_landed[t % 2], 16 * (t // 2 + 1))
                for n in range(4):
                    dve.wait_ge(m.filter_ready, 4 * t + n + 1)
                    part, cols = (fwd if n < 2 else bwd), slice((n % 2) * HALF, (n % 2 + 1) * HALF)
                    dve.tensor_tensor(part[:, t, cols], m.psum[:, (4 * t + n) % 2, :], decay[:, t % 2, cols], ALU.mult).then_inc(m.filter_taken, 1)
            dve.wait_ge(m.filter_taken, 4 * TT)
            dve.memset(bwd[0:1, 0, :], 0.0).then_inc(m.parts_final, 1)
            dve.wait_ge(m.abs_summed, 2 * TT)
            for half in range(2):
                m.vector.mark(dve.reciprocal(inv_l1[:, half * HALF:(half + 1) * HALF], m.psum[:, 2 + half, :]))
            m.vector.wait(dve)
            for t in range(TT):
                m.vector.link(dve, dve.tensor_tensor(scratch, fwd[:, t, :], bwd[:, t, :], ALU.subtract))
                m.vector.link(dve, dve.tensor_tensor(fwd[:, t, :], fwd[:, t, :], bwd[:, t, :], ALU.add))
                dve.tensor_tensor(bwd[:, t, :], scratch, inv_l1, ALU.mult).then_inc(m.parts_ready, 1)
                dve.tensor_tensor(fwd[:, t, :], fwd[:, t, :], inv_l1, ALU.mult).then_inc(m.parts_ready, 1)
                dve.wait_ge(m.parts_ready, 2 * (t + 1))

        @block.scalar
        def _(act):
            for n in range(2):
                act.wait_ge(m.angle_ready, n + 1)
                act.activation(hidden[:, n, :], hidden[:, n, :], ACT.Sin).then_inc(m.sine_ready, 1)
            act.wait_ge(m.parts_final, 1)
            for t in range(TT):
                for b, part in enumerate((fwd, bwd)):
                    if t + b >= 1:
                        act.wait_ge(m.abs_summed, 2 * t + b)
                    act.activation(scratch, part[:, t, :], ACT.Abs).then_inc(m.abs_ready, 1)
            for i in range(8):
                ft, cols = i // 2, slice((i % 2) * HALF, (i % 2 + 1) * HALF)
                act.wait_ge(m.spectrum_ready, i + 1)
                act.copy(m.k_re[:, ft, cols], m.psum[:, 4 + 2 * (i % 2), :]).then_inc(m.spectrum_taken, 1)
                act.copy(m.k_im[:, ft, cols], m.psum[:, 5 + 2 * (i % 2), :]).then_inc(m.spectrum_taken, 1)
            act.wait_ge(m.spectrum_taken, 16)
            act.wait_ge(m.highest_ready, 1)
            for half in range(2):
                act.copy(m.k_im[0:1, 0, half * HALF:(half + 1) * HALF], m.psum[0:1, half, :]).then_inc(m.highest_taken, 1)


def hyena_project(nc, m, a):
    tiles = 3 * KT
    weights = feature_major(a["hy_w_in"][0])
    with ExitStack() as scope:
        h = scope.enter_context(nc.sbuf_tensor("h_rows1", [P, 2, D], F32))
        z = scope.enter_context(nc.sbuf_tensor("z_padded", [P, 2, SEQ + 2], F32))
        conv = scope.enter_context(nc.sbuf_tensor("conv", [P, SEQ], F32))
        vectors = scope.enter_context(nc.sbuf_tensor("hy_vectors_sb", [P, 5, tiles], F32))
        block = scope.enter_context(nc.Block(no_gpsimd_drain=True))

        @block.sync
        def _(sp):
            sp.dma_start(vectors[:], a["hy_vectors"]).then_inc(m.hy_vectors_landed, 16)
            for n in range(2, tiles // 4):
                sp.wait_ge(m.z_ready, 4 * (n - 1))
                load_block(m, sp, HYENA_FIRST + n, block_of(weights, n))

        @block.tensor
        def _(pe):
            for t in range(TT):
                pe.wait_ge(m.rows_ready, m.rows_before + t + 1)
                transpose_tile_tensor(m, pe, h[:, t % 2, :], t)
            pe.wait_ge(m.columns_ready, m.turned_before + 2 * TT)
            for i in range(tiles):
                w = wait_block(m, pe, HYENA_FIRST + i // 4)
                if i >= 4:
                    pe.wait_ge(m.z_taken, i - 3)
                for k in range(KT):
                    mm = pe.matmul(m.psum[:, i % 4, :], w[:, k, (i % 4) * P:(i % 4 + 1) * P], m.cols[:, k, 0:SEQ],
                                   start=k == 0, stop=k == KT - 1)
                mm.then_inc(m.z_ready, 1)

        @block.scalar
        def _(act):
            for t in range(TT):
                transpose_tile_scalar(m, act, t, t)
            act.wait_ge(m.hy_vectors_landed, 16)
            act.wait_ge(m.pads_ready, 1)
            for i in range(tiles):
                act.wait_ge(m.z_ready, i + 1)
                if i >= 2:
                    act.wait_ge(m.conv_done, i - 1)
                act.activation(z[:, i % 2, 1:SEQ + 1], m.psum[:, i % 4, :], ACT.Identity, bias=vectors[:, 0, i:i + 1]).then_inc(m.z_taken, 1)

        @block.vector
        def _(dve):
            dve.memset(z[:], 0.0).then_inc(m.pads_ready, 1)
            modulate_rows_vector(m, dve, h, TT)
            dve.wait_ge(m.hy_vectors_landed, 16)
            for i in range(tiles):
                dve.wait_ge(m.z_taken, i + 1)
                taps = [z[:, i % 2, j:j + SEQ] for j in range(3)]
                out = m.x0[:, i, :] if i < KT else m.v_cols[:, i - KT, :] if i < 2 * KT else conv[:]
                m.vector.link(dve, dve.tensor_scalar(out, taps[0], vectors[:, 2, i:i + 1], vectors[:, 1, i:i + 1], ALU.mult, ALU.add))
                m.vector.link(dve, dve.scalar_tensor_tensor(out, taps[1], vectors[:, 3, i:i + 1], out, ALU.mult, ALU.add))
                dve.scalar_tensor_tensor(out, taps[2], vectors[:, 4, i:i + 1], out, ALU.mult, ALU.add).then_inc(m.conv_done, 1)
                if i >= 2 * KT:
                    dve.wait_ge(m.conv_done, i + 1)
                    v = m.v_cols[:, i - 2 * KT, :]
                    m.vector.link(dve, dve.tensor_tensor(v, v, conv[:], ALU.mult))
    m.rows_before += TT
    m.turned_before += 2 * TT


def convolve(nc, m, a):
    with ExitStack() as scope:
        def sb(name, shape):
            return scope.enter_context(nc.sbuf_tensor(name, shape, F32))
        slot = (RESIDUAL_FIRST[1] + 1) % 2
        v_rows = m.ring[:, slot].rearrange("p (t a) n -> p t (a n)", t=TT)
        cos_out, sin_out = sb("cos_out_sb", [P, 4, SEQ]), sb("sin_out_sb", [P, 4, SEQ])
        skip = sb("skip", [P, KT])
        parts = m.mod[:, 0:2 * D].rearrange("p (s n) -> p s n", s=4)
        minus = sb("minus", [P, 2])
        mixed = sb("skip_mixed", [P, SEQ])
        block = scope.enter_context(nc.Block(no_gpsimd_drain=True))

        @block.sync
        def _(sp):
            weights = feature_major(a["hy_w_out"][0])
            load_block(m, sp, RESIDUAL_FIRST[1], block_of(weights, 0))
            sp.dma_start(skip[:], a["hy_d_t"]).then_inc(m.inverse_landed, 16)
            sp.dma_start(cos_out[:], a["cos_out"].rearrange("(f p) t -> p f t", p=P)).then_inc(m.inverse_landed, 16)
            sp.dma_start(sin_out[:], a["sin_out"].rearrange("(f p) t -> p f t", p=P)).then_inc(m.inverse_landed, 16)
            sp.wait_ge(m.v_spectrum_ready, 8)
            load_block(m, sp, RESIDUAL_FIRST[1] + 1, block_of(weights, 1))

        @block.tensor
        def _(pe):
            for i in range(2 * TT):
                t, half = i // 2, i % 2
                if i >= 4:
                    pe.wait_ge(m.v_rows_taken, i - 3)
                for k in range(4):
                    mm = pe.transpose(m.psum[:, 4 + i % 4, k * P:(k + 1) * P], m.v_cols[:, 4 * half + k, t * P:(t + 1) * P], m.ident[:])
                mm.then_inc(m.v_turned, 1)
            pe.wait_ge(m.v_rows_taken, 2 * TT)
            for i in range(8):
                ft, cols = i // 2, slice((i % 2) * HALF, (i % 2 + 1) * HALF)
                if i >= 2:
                    pe.wait_ge(m.spectra_used, i - 1)
                for table, bank in ((m.cos_in, 2 * (i % 2)), (m.sin_in, 2 * (i % 2) + 1)):
                    for t in range(TT):
                        mm = pe.matmul(m.psum[:, bank, :], table[:, t, ft * P:(ft + 1) * P], v_rows[:, t, cols],
                                       start=t == 0, stop=t == TT - 1)
                mm.then_inc(m.v_spectrum_ready, 1)
            pe.wait_ge(m.inverse_landed, 48)
            pe.wait_ge(m.spectra_multiplied, 8)
            for k in range(KT):
                if k >= 4:
                    pe.wait_ge(m.y_taken, k - 3)
                for n, (part, table) in enumerate(((m.k_re, cos_out), (m.k_im, sin_out))):
                    for ft in range(4):
                        mm = pe.matmul(m.psum[:, 4 + k % 4, :], part[:, ft, k * P:(k + 1) * P], table[:, ft, :],
                                       start=n == ft == 0, stop=n == 1 and ft == 3)
                mm.then_inc(m.y_ready, 1)

        @block.scalar
        def _(act):
            for i in range(2 * TT):
                act.wait_ge(m.v_turned, i + 1)
                act.copy(v_rows[:, i // 2, (i % 2) * HALF:(i % 2 + 1) * HALF], m.psum[:, 4 + i % 4, :]).then_inc(m.v_rows_taken, 1)

        @block.vector
        def _(dve):
            m.vector.mark(dve.memset(minus[:], -1.0))
            m.vector.wait(dve)
            m.vector.link(dve, dve.memset(minus[0:1, 0:1], 0.0))
            for i in range(8):
                ft, cols = i // 2, slice((i % 2) * HALF, (i % 2 + 1) * HALF)
                dve.wait_ge(m.v_spectrum_ready, i + 1)
                v_re, v_im = m.psum[:, 2 * (i % 2), :], m.psum[:, 2 * (i % 2) + 1, :]
                k_re, k_im = m.k_re[:, ft, cols], m.k_im[:, ft, cols]
                m.vector.mark(dve.tensor_tensor(parts[:, 0, :], v_re, k_re, ALU.mult))
                m.vector.mark(dve.tensor_tensor(parts[:, 1, :], v_im, k_im, ALU.mult))
                m.vector.mark(dve.tensor_tensor(parts[:, 2, :], v_re, k_im, ALU.mult))
                dve.tensor_tensor(parts[:, 3, :], v_im, k_re, ALU.mult).then_inc(m.spectra_used, 1)
                m.vector.wait(dve)
                dve.wait_ge(m.spectra_used, i + 1)
                sign = minus[:, 0:1] if ft == 0 else minus[:, 1:2]
                m.vector.mark(dve.scalar_tensor_tensor(k_re, parts[:, 1, :], sign, parts[:, 0, :], ALU.mult, ALU.add))
                m.vector.mark(dve.tensor_tensor(k_im, parts[:, 2, :], parts[:, 3, :], ALU.add))
                m.vector.wait(dve)
                if ft == 0:
                    m.vector.link(dve, dve.tensor_copy(m.k_im[0:1, 0, cols], parts[0:1, 1, :]))
                dve.engine_nop().then_inc(m.spectra_multiplied, 1)
            dve.wait_ge(m.inverse_landed, 48)
            for k in range(KT):
                dve.wait_ge(m.y_ready, k + 1)
                dve.scalar_tensor_tensor(mixed[:], m.v_cols[:, k, :], skip[:, k:k + 1], m.psum[:, 4 + k % 4, :],
                                         ALU.mult, ALU.add).then_inc(m.y_taken, 1)
                dve.wait_ge(m.y_taken, k + 1)
                m.vector.link(dve, dve.tensor_tensor(m.cols[:, k, 0:SEQ], mixed[:], m.x0[:, k, :], ALU.mult))


def program(nc, a):
    with ExitStack() as whole:
        def sem(name):
            return whole.enter_context(nc.semaphore(name))
        m = Machine()
        m.setup_landed = sem("setup_landed")
        m.silu_done = sem("silu_done")
        m.mod_bias_landed = sem("mod_bias_landed")
        m.mod_pair_ready = sem("mod_pair_ready")
        m.mod_pair_taken = sem("mod_pair_taken")
        m.mod_row_ready = sem("mod_row_ready")
        m.mod_row_taken = sem("mod_row_taken")
        m.vector_steps = sem("vector_steps")
        m.selection_steps = sem("selection_steps")
        m.proj_ready = sem("proj_ready")
        m.proj_taken = sem("proj_taken")
        m.rows_ready = sem("rows_ready")
        m.rows_transposed = sem("rows_transposed")
        m.columns_ready = sem("columns_ready")
        m.mix_consts_landed = sem("mix_consts_landed")
        m.scores_biased = sem("scores_biased")
        m.gv_var_ready = sem("gv_var_ready")
        m.gv_std_ready = sem("gv_std_ready")
        m.gv_ready = sem("gv_ready")
        m.mixed_ready = sem("mixed_ready")
        m.mixed_taken = sem("mixed_taken")
        m.scores_ready = sem("scores_ready")
        m.probs_turned = sem("probs_turned")
        m.ctx_scores_taken = sem("ctx_scores_taken")
        m.max_ready = sem("max_ready")
        m.probs_ready = sem("probs_ready")
        m.turned_taken_vector = sem("turned_taken_vector")
        m.turned_taken_scalar = sem("turned_taken_scalar")
        m.heads_out_ready = sem("heads_out_ready")
        m.heads_out_taken = sem("heads_out_taken")
        m.var_ready = sem("var_ready")
        m.std_ready = sem("std_ready")
        m.ln_landed = sem("ln_landed")
        m.mix_out_ready = sem("mix_out_ready")
        m.tile_modulated = sem("tile_modulated")
        m.query_ready = sem("query_ready")
        m.query_taken = sem("query_taken")
        m.keys_landed = sem("keys_landed")
        m.key_scores_ready = sem("key_scores_ready")
        m.key_scores_taken = sem("key_scores_taken")
        m.section_selected = sem("section_selected")
        m.shifted_ready = sem("shifted_ready")
        m.exps_ready = sem("exps_ready")
        m.current_ready = sem("current_ready")
        m.dots_done = sem("dots_done")
        m.v_used = sem("v_used")
        m.acted_ready = sem("acted_ready")
        m.weights_ready = sem("weights_ready")
        m.diagonals_ready = sem("diagonals_ready")
        m.zeros_ready = sem("zeros_ready")
        m.experts_ready = sem("experts_ready")
        m.tile_done = sem("tile_done")
        m.out_stored = sem("out_stored")
        m.ffn_landed = sem("ffn_landed")
        m.hidden_ready = sem("hidden_ready")
        m.angle_ready = sem("angle_ready")
        m.sine_ready = sem("sine_ready")
        m.filter_ready = sem("filter_ready")
        m.filter_taken = sem("filter_taken")
        m.parts_final = sem("parts_final")
        m.abs_ready = sem("abs_ready")
        m.abs_summed = sem("abs_summed")
        m.parts_ready = sem("parts_ready")
        m.dft_landed = sem("dft_landed")
        m.spectrum_ready = sem("spectrum_ready")
        m.spectrum_taken = sem("spectrum_taken")
        m.highest_ready = sem("highest_ready")
        m.highest_taken = sem("highest_taken")
        m.hy_vectors_landed = sem("hy_vectors_landed")
        m.z_ready = sem("z_ready")
        m.z_taken = sem("z_taken")
        m.pads_ready = sem("pads_ready")
        m.conv_done = sem("conv_done")
        m.inverse_landed = sem("inverse_landed")
        m.v_turned = sem("v_turned")
        m.v_rows_taken = sem("v_rows_taken")
        m.v_spectrum_ready = sem("v_spectrum_ready")
        m.spectra_used = sem("spectra_used")
        m.spectra_multiplied = sem("spectra_multiplied")
        m.y_ready = sem("y_ready")
        m.y_taken = sem("y_taken")
        m.ring_landed = [sem(f"ring_landed{slot}") for slot in range(2)]
        m.table_landed = [sem(f"table_landed{slot}") for slot in range(2)]
        m.decay_landed = [sem(f"decay_landed{slot}") for slot in range(2)]
        m.u_landed = [sem(f"u_landed{slot}") for slot in range(RING)]
        m.v_landed = [sem(f"v_landed{slot}") for slot in range(RING)]
        m.vector = Chain(m.vector_steps)
        m.select = SelectionChain(m.selection_steps)
        m.rows_before = m.turned_before = m.norms = m.roots = 0

        def sb(scope, name, shape):
            return scope.enter_context(nc.sbuf_tensor(name, shape, F32))
        m.psum = whole.enter_context(nc.psum_tensor("psum", [P, 8, HALF], F32))
        m.x = sb(whole, "x_rows", [P, TT, D])
        m.xm = sb(whole, "xm_rows", [P, TT, D])
        m.mod = sb(whole, "mod_rows", [P, 6 * D])
        m.cols = sb(whole, "cols", [P, KT, KEYS_ALL])
        m.ident = sb(whole, "ident_sb", [P, P])
        m.ones = sb(whole, "ones", [P, P])
        m.ranks = sb(whole, "ranks_sb", [P, TOPK])
        m.cond_silu = sb(whole, "cond_silu", [P, KT, 2])
        m.picks = sb(whole, "picks_sb", [3, 2, P])
        m.ring = sb(whole, "weight_ring", [P, 2, KT, HALF])
        m.x0 = m.xm[:].rearrange("p t (a n) -> p (t a) n", n=SEQ)
        setup(nc, m, a)
        modulation(nc, m, a, 0)
        with ExitStack() as scope:
            m.q_cols = sb(scope, "q_cols", [P, 4, SEQ])
            m.k_cols = sb(scope, "k_cols", [P, 4, KEYS_ALL])
            m.v_rows = sb(scope, "v_rows0", [P, TT + CT, NA_DIM])
            m.gate_rows = sb(scope, "gate_rows", [P, TT, D])
            project(nc, m, a)
            mix(nc, m, a)
        residual(nc, m, a, 0)
        with ExitStack() as scope:
            m.scores = sb(scope, "scores0", [P, 4 * TT + 1, 4 * NKEYS])
            score_keys(nc, m, a, 0)
            experts(nc, m, a, 0)
        modulation(nc, m, a, 1)
        with ExitStack() as scope:
            m.k_re, m.k_im = sb(scope, "k_re", [P, 4, D]), sb(scope, "k_im", [P, 4, D])
            m.cos_in, m.sin_in = sb(scope, "cos_in_sb", [P, TT, SEQ]), sb(scope, "sin_in_sb", [P, TT, SEQ])
            filter_spectrum(nc, m, a)
            m.v_cols = sb(scope, "v_cols", [P, KT, SEQ])
            hyena_project(nc, m, a)
            convolve(nc, m, a)
        residual(nc, m, a, 1)
        with ExitStack() as scope:
            m.scores = sb(scope, "scores1", [P, 4 * TT + 1, 4 * NKEYS])
            score_keys(nc, m, a, 1)
            experts(nc, m, a, 1)


def constants():
    f = np.float32
    col = np.arange(GRID_W)
    first = np.clip(col - WIN_COLS // 2, 0, GRID_W - WIN_COLS)
    inside = (col[None, :] >= first[:, None]) & (col[None, :] < first[:, None] + WIN_COLS)
    window = np.where(inside, 0.0, MASKED).astype(f)
    t = np.linspace(0.0, 1.0, SEQ, dtype=f)
    angle = (f(2.0 * np.pi) * np.arange(SEQ, dtype=f) / f(SEQ))[:, None]
    bands = np.linspace(1e-4, (EMB - 1) // 2 - 1, (EMB - 1) // 2, dtype=f)[None, :]
    position = np.concatenate([t[:, None], np.cos(bands * angle), np.sin(-bands * angle)], axis=1)
    deltas = np.abs(np.linspace(np.log(1e-2) / 1.5, np.log(1e-2) / 0.3, D, dtype=f))
    n = np.arange(SEQ)
    turn = 2 * np.pi * (np.outer(n, n) % NFFT) / NFFT
    alternating = 1.0 - 2.0 * (n % 2)
    cos_in, sin_in = np.cos(turn), np.sin(turn)
    weight = np.where(n == 0, 1.0, 2.0)[:, None] / NFFT
    cos_out, sin_out = weight * cos_in, weight * sin_in
    sin_in[:, 0] = alternating
    sin_out[0, :] = alternating / NFFT
    picks = np.zeros((3, 2, P), dtype=f)
    picks[0, 0], picks[1, 1], picks[2] = 1.0, 1.0, 1.0
    return {
        "picks": picks, "ident": np.eye(P, dtype=f), "ranks": np.tile(np.arange(TOPK, dtype=f), (P, 1)),
        "window": np.concatenate([window, window]), "position": np.ascontiguousarray(position.T.astype(f)),
        "decay": np.exp(-t[:, None] * deltas[None, :]).astype(f),
        "cos_in": cos_in.astype(f), "sin_in": sin_in.astype(f), "cos_out": cos_out.astype(f), "sin_out": sin_out.astype(f),
    }


AS_THEY_COME = ("x", "c", "ctx", "c_ctx", "mod_w", "mod_b", "ln_g", "ln_b", "ab_w_in", "ab_w_out", "hy_w_in",
                "hy_ffn_w1", "hy_ffn_w2", "hy_ffn_w3", "hy_w_out", "peer_wq")


def laid_out(inputs):
    g = {name: np.asarray(value) for name, value in inputs.items()}
    arrays = {name: g[name] for name in AS_THEY_COME}
    for layer in range(2):
        arrays[f"peer_u{layer}"], arrays[f"peer_v{layer}"] = g["peer_u"][layer], g["peer_v"][layer]
    padded = np.pad(g["na_rpb"][0], ((0, 0), (0, 0), (GRID_W - WIN_COLS, GRID_W - WIN_COLS)))
    column = np.arange(GRID_W)
    shifted = padded[:, :, (GRID_W - 1 - column)[:, None] + column[None, :]]
    arrays["rpb_shifted"] = shifted.transpose(0, 2, 1, 3)
    arrays["gm_w_s_t"] = g["gm_w_s"][0].transpose(0, 2, 1)
    arrays["gm_b_s_t"] = g["gm_b_s"][0].T
    arrays["peer_keys_t"] = g["peer_keys"].transpose(0, 1, 2, 4, 3).reshape(2, HP, P, NKEYS)
    arrays["ffn_vectors"] = np.stack([g["hy_ffn_b1"][0], g["hy_ffn_f1"][0], g["hy_ffn_b2"][0], g["hy_ffn_f2"][0]], axis=1)
    per_feature = np.concatenate([g["hy_b_in"], g["hy_conv_b"], g["hy_conv_w"][0]])
    arrays["hy_vectors"] = per_feature.reshape(5, 3 * KT, P).transpose(2, 0, 1)
    arrays["hy_d_t"] = g["hy_d"][0].reshape(KT, P).T
    return {name: np.ascontiguousarray(value) for name, value in arrays.items()} | constants()


def kernel(**inputs):
    import concourse.bacc as bacc
    from concourse.bass_utils import run_bass_kernel_spmd

    nc = bacc.Bacc("TRN2", target_bir_lowering=False, num_devices=1)
    arrays = laid_out(inputs)
    a = {name: nc.dram_tensor(f"in_{name}", value.shape, mybir.dt.from_np(value.dtype), kind="ExternalInput").ap()
         for name, value in arrays.items()}
    a["out"] = nc.dram_tensor("out_x", (1, SEQ, D), F32, kind="ExternalOutput").ap()
    program(nc, a)
    result = run_bass_kernel_spmd(nc, [{f"in_{name}": value for name, value in arrays.items()}], core_ids=[0])
    return result.results[0]["out_x"]
```

```python
from contextlib import ExitStack

import numpy as np

import concourse.bass as bass
from concourse import mybir

F32 = mybir.dt.float32
U32 = mybir.dt.uint32
ALU = mybir.AluOpType
ACT = mybir.ActivationFunctionType
AX_X = mybir.AxisListType.X

P = 128
D = 1024
SEQ = 512
CTX = 256
KT = D // P
TT = SEQ // P
CT = CTX // P
HALF = 512
ALPHA = 4 ** 0.25
EPS = 1e-5

HEADS = 8
HEAD_DIM = 64
GRID_W = 64
GRID_ROWS = SEQ // GRID_W
WIN_COLS = 16
NA_DIM = HEADS * HEAD_DIM
KEYS_ALL = SEQ + CTX
RPB_ROWS = 2 * 8 - 1
TAB = RPB_ROWS - 1
MASKED = -1e30

GROUPS = 4
PEER_HEADS = 8
NKEYS = 128
TOPK = 16
SLOTS = PEER_HEADS * TOPK
HP = 2 * PEER_HEADS
RING = 8
LOWEST = -3.4e38

NFFT = 2 * SEQ
EMB = 33
FFN = 64
MAGIC = 1.5 * 2 ** 23
TWO_PI_HIGH = 6.28125
TWO_PI_MID = float(np.floor((2 * np.pi - TWO_PI_HIGH) * 2 ** 21) / 2 ** 21)
TWO_PI_LOW = float(2 * np.pi - TWO_PI_HIGH - TWO_PI_MID)
PI_BELOW = float(np.nextafter(np.float32(np.pi), np.float32(0)))


class Machine:
    pass


class Chain:

    def __init__(self, semaphore):
        self.semaphore, self.count = semaphore, 0

    def mark(self, instruction):
        instruction.then_inc(self.semaphore, 1)
        self.count += 1

    def wait(self, engine):
        engine.wait_ge(self.semaphore, self.count)

    def link(self, engine, instruction):
        self.mark(instruction)
        self.wait(engine)


class SelectionChain(Chain):

    def __init__(self, semaphore):
        super().__init__(semaphore)
        self.each, self.before = None, 0

    def begin(self, nth):
        if self.each is None and self.count:
            self.each = self.count
        self.before = (nth - 1) * self.each if self.each else 0
        self.count = 0

    def wait(self, engine):
        engine.wait_ge(self.semaphore, self.before + self.count)
        engine.nop(nofuse=True)


MOD_FIRST = (0, 19)
PROJECT_FIRST = 12
HYENA_FIRST = 31
RESIDUAL_FIRST = (17, 37)


QUERY_SLOT = 0
PAIRS = PEER_HEADS


def query_weights(m, pair):
    half = m.ring[:, QUERY_SLOT, 4 * (pair % 2):4 * (pair % 2) + 4, :].rearrange("p a n -> p (a n)")
    return half.rearrange("p (k n) -> p k n", k=KT)


def load_query_weights(m, sp, a, layer, pair):
    sp.dma_start(query_weights(m, pair),
                 feature_major(a["peer_wq"][layer])[:, :, pair * 2 * P:(pair + 1) * 2 * P]).then_inc(m.query_weights_landed[pair % 2], 16)


def wait_query_weights(m, pe, layer, pair):
    pe.wait_ge(m.query_weights_landed[pair % 2], 16 * (layer * PAIRS // 2 + pair // 2 + 1))
    return query_weights(m, pair)


def block_of(weights, n):
    return weights[:, :, n * HALF:(n + 1) * HALF]


def load_block(m, sp, number, source):
    sp.dma_start(m.ring[:, number % 2], source).then_inc(m.ring_landed[number % 2], 16)


def wait_block(m, pe, number):
    pe.wait_ge(m.ring_landed[number % 2], 16 * (number // 2 + 1))
    return m.ring[:, number % 2]


def feature_major(weights):
    return weights.rearrange("(k p) n -> p k n", p=P)


def setup(nc, m, a):
    with ExitStack() as scope:
        cond = scope.enter_context(nc.sbuf_tensor("cond", [P, 2, KT], F32))
        block = scope.enter_context(nc.Block(no_gpsimd_drain=True))

        @block.sync
        def _(sp):
            sp.dma_start(cond[:, 0, :], a["c"].rearrange("a (p k) -> p (a k)", k=KT)).then_inc(m.cond_landed, 16)
            sp.dma_start(cond[:, 1, :], a["c_ctx"].rearrange("(p k) -> p k", k=KT)).then_inc(m.cond_landed, 16)
            sp.dma_start(m.picks[:], a["picks"]).then_inc(m.cond_landed, 16)
            for n in range(2):
                modulation_bias(m, sp, a, 0, n)
                load_block(m, sp, MOD_FIRST[0] + n, block_of(modulation_weights(a, 0), n))

        @block.scalar
        def _(act):
            act.wait_ge(m.padding_zero, 1)
            act.wait_ge(m.cond_landed, 48)
            act.activation(m.cond_silu[:, :, 0:2].rearrange("p k c -> p c k"), cond[:], ACT.Silu).then_inc(m.silu_done, 1)

        @block.vector
        def _(dve):
            dve.memset(m.cond_silu[:], 0.0).then_inc(m.padding_zero, 1)
            m.vector.mark(dve.memset(m.ones[:], 1.0))


def modulation_weights(a, layer):
    return a["mod_w"][layer].rearrange("(p k) n -> p k n", k=KT)


MOD_BLOCKS = 6 * D // HALF
MOD_CTX_BLOCKS = 2 * D // HALF
MOD_ROWS_BEFORE = (0, MOD_BLOCKS + MOD_CTX_BLOCKS)


def modulation_rows(layer, n):
    if layer == 0:
        return [(n + min(n, MOD_CTX_BLOCKS) + who, who) for who in range(2 if n < MOD_CTX_BLOCKS else 1)]
    return [(n, 0)]


def modulation_bias(m, sp, a, layer, n):
    source = a["mod_b"][layer:layer + 1, n * HALF:(n + 1) * HALF]
    sp.dma_start(m.mod_bias[layer][:, n % 2, :], source).then_inc(m.mod_bias_landed[n % 2], 16)


def modulation_load(m, sp, a, layer, n):
    for group_ready in m.mod_group_ready:
        sp.wait_ge(group_ready, layer * MOD_BLOCKS + n - 1)
    load_block(m, sp, MOD_FIRST[layer] + n, block_of(modulation_weights(a, layer), n))
    modulation_bias(m, sp, a, layer, n)


def modulation_load_next(m, sp, a, layer):
    first, weights = (PROJECT_FIRST, a["ab_w_in"][0]) if layer == 0 else (HYENA_FIRST, a["hy_w_in"][0])
    for n in range(2):
        for group_ready in m.mod_group_ready:
            sp.wait_ge(group_ready, (layer + 1) * MOD_BLOCKS - 1 + n)
        load_block(m, sp, first + n, block_of(feature_major(weights), n))


def modulation_tensor(m, pe, parts, layer, n):
    before = layer * MOD_BLOCKS
    if n < MOD_BLOCKS:
        w = wait_block(m, pe, MOD_FIRST[layer] + n)
        pe.wait_ge(m.mod_bias_landed[n % 2], 16 * ((before + n) // 2 + 1))
        if n >= 2:
            pe.wait_ge(m.mod_parts_taken, before + n - 1)
        pe.matmul(m.psum[0:32, n % 2, :], m.ones[0:1, 0:32], m.mod_bias[layer][:, n % 2, :], start=True, stop=False, tile_position=(0, 0))
        for k in range(KT):
            group = slice(32 * (k % 4), 32 * (k % 4) + 32)
            mm = pe.matmul(m.psum[group, n % 2, :], m.cond_silu[:, k, :], w[:, k, :], start=1 <= k < 4, stop=k >= 4,
                           tile_position=(0, 32 * (k % 4)))
            if k >= 4:
                mm.then_inc(m.mod_group_ready[k % 4], 1)
    if n >= 1:
        pe.wait_ge(m.mod_parts_taken, before + n)
        for i, who in modulation_rows(layer, n - 1):
            if i >= 2:
                pe.wait_ge(m.mod_row_taken, MOD_ROWS_BEFORE[layer] + i - 1)
            pe.matmul(m.psum[:, 2 + i % 2, :], m.picks[:, who, :], parts[:, (n - 1) % 2, :],
                      start=True, stop=True).then_inc(m.mod_row_ready, 1)


def modulation_vector(m, dve, parts, layer, n):
    if n < MOD_BLOCKS:
        for group_ready in m.mod_group_ready:
            dve.wait_ge(group_ready, layer * MOD_BLOCKS + n + 1)
        dve.tensor_copy(parts[:, n % 2, :], m.psum[:, n % 2, :]).then_inc(m.mod_parts_taken, 1)
    if n >= 1:
        for i, who in modulation_rows(layer, n - 1):
            dve.wait_ge(m.mod_row_ready, MOD_ROWS_BEFORE[layer] + i + 1)
            is_scale = (n - 1) * HALF // D in (1, 4)
            cols = slice((n - 1) * HALF, n * HALF)
            out = m.mod[:, cols] if who == 0 else m.xm[:, 2:4, :].rearrange("p t d -> p (t d)")[:, cols]
            dve.tensor_scalar_add(out, m.psum[:, 2 + i % 2, :], 1.0 if is_scale else 0.0).then_inc(m.mod_row_taken, 1)


def modulation(nc, m, a):
    with ExitStack() as scope:
        parts = scope.enter_context(nc.sbuf_tensor("mod_parts0", [P, 2, HALF], F32))
        block = scope.enter_context(nc.Block(no_gpsimd_drain=True))

        @block.sync
        def _(sp):
            for n in range(2, MOD_BLOCKS):
                modulation_load(m, sp, a, 0, n)
                if n == MOD_BLOCKS // 2:
                    sp.dma_start(m.ident[:], a["ident"]).then_inc(m.setup_landed, 16)
                    sp.dma_start(m.ranks[:], a["ranks"]).then_inc(m.setup_landed, 16)
                    sp.dma_start(m.x[:], a["x"][0].rearrange("(t p) d -> p t d", p=P)).then_inc(m.setup_landed, 16)
                    sp.dma_start(m.xm[:, 0:CT, :], a["ctx"][0].rearrange("(t p) d -> p t d", p=P)).then_inc(m.setup_landed, 16)
            modulation_load_next(m, sp, a, 0)

        @block.tensor
        def _(pe):
            for n in range(MOD_BLOCKS + 1):
                modulation_tensor(m, pe, parts, 0, n)

        @block.vector
        def _(dve):
            for n in range(MOD_BLOCKS + 1):
                modulation_vector(m, dve, parts, 0, n)


def project(nc, m, a):
    blocks = 5
    weights = feature_major(a["ab_w_in"][0])
    products = [(0, "q", f) for f in range(4)] + [(1, part, f) for f in range(4) for part in ("k", "kc")]
    products += [(2, "v", t) for t in range(TT + CT)] + [(3, "u", t) for t in range(TT)] + [(4, "g", t) for t in range(TT)]
    with ExitStack() as scope:
        h = scope.enter_context(nc.sbuf_tensor("h_rows0", [P, 2, D], F32))
        block = scope.enter_context(nc.Block(no_gpsimd_drain=True))

        @block.sync
        def _(sp):
            for n in range(2, blocks + 2):
                last = max(i for i, product in enumerate(products) if product[0] == n - 2)
                sp.wait_ge(m.proj_ready, last + 1)
                if n < blocks:
                    load_block(m, sp, PROJECT_FIRST + n, block_of(weights, n))
                else:
                    load_block(m, sp, RESIDUAL_FIRST[0] + n - blocks, block_of(feature_major(a["ab_w_out"][0]), n - blocks))

        @block.vector
        def _(dve):
            dve.wait_ge(m.setup_landed, 64)
            modulate_rows_vector(m, dve, h, TT + CT)

        @block.tensor
        def _(pe):
            for t in range(TT + CT):
                pe.wait_ge(m.rows_ready, m.rows_before + t + 1)
                transpose_tile_tensor(m, pe, h[:, t % 2, :], t)
            pe.wait_ge(m.columns_ready, m.turned_before + 2 * (TT + CT))
            for i, (n, what, j) in enumerate(products):
                w = wait_block(m, pe, PROJECT_FIRST + n)
                if i >= 4:
                    pe.wait_ge(m.proj_taken, i - 3)
                for k in range(KT):
                    if what == "q":
                        out, left, right = m.psum[:, i % 4, :], w[:, k, j * P:(j + 1) * P], m.cols[:, k, 0:SEQ]
                    elif what == "k":
                        out, left, right = m.psum[:, i % 4, :], w[:, k, j * P:(j + 1) * P], m.cols[:, k, 0:SEQ]
                    elif what == "kc":
                        out, left, right = m.psum[:, i % 4, 0:CTX], w[:, k, j * P:(j + 1) * P], m.cols[:, k, SEQ:KEYS_ALL]
                    else:
                        out, left, right = m.psum[:, i % 4, :], m.cols[:, k, j * P:(j + 1) * P], w[:, k, :]
                    mm = pe.matmul(out, left, right, start=k == 0, stop=k == KT - 1)
                mm.then_inc(m.proj_ready, 1)

        @block.scalar
        def _(act):
            for t in range(TT + CT):
                transpose_tile_scalar(m, act, t, t)
            for i, (n, what, j) in enumerate(products):
                act.wait_ge(m.proj_ready, i + 1)
                bank = m.psum[:, i % 4, :]
                if what == "q":
                    act.mul(m.q_cols[:, j, :], bank, HEAD_DIM ** -0.5).then_inc(m.proj_taken, 1)
                elif what == "k":
                    act.copy(m.k_cols[:, j, 0:SEQ], bank).then_inc(m.proj_taken, 1)
                elif what == "kc":
                    act.copy(m.k_cols[:, j, SEQ:KEYS_ALL], bank[:, 0:CTX]).then_inc(m.proj_taken, 1)
                elif what == "v":
                    act.copy(m.v_rows[:, j, :], bank).then_inc(m.proj_taken, 1)
                else:
                    half = m.gate_rows[:, j, (0 if what == "u" else HALF):(HALF if what == "u" else D)]
                    act.activation(half, bank, ACT.Gelu).then_inc(m.proj_taken, 1)
    m.rows_before += TT + CT
    m.turned_before += 2 * (TT + CT)


def modulate_rows_vector(m, dve, h, tiles):
    for t in range(tiles):
        if t >= 2:
            dve.wait_ge(m.rows_transposed, m.turned_before + 2 * (t - 1))
        if t < TT:
            rows, shift, scale = m.x[:, t, :], m.mod[:, 0:D], m.mod[:, D:2 * D]
        else:
            rows, shift, scale = m.xm[:, t - TT, :], m.xm[:, 2, :], m.xm[:, 3, :]
        m.vector.link(dve, dve.tensor_tensor(h[:, t % 2, :], rows, scale, ALU.mult))
        dve.tensor_tensor(h[:, t % 2, :], h[:, t % 2, :], shift, ALU.add).then_inc(m.rows_ready, 1)


def transpose_tile_tensor(m, pe, rows, i):
    for half in range(2):
        n = 2 * i + half
        if n >= 4:
            pe.wait_ge(m.columns_ready, m.turned_before + n - 3)
        for k in range(4):
            tile = rows[:, (4 * half + k) * P:(4 * half + k + 1) * P]
            mm = pe.transpose(m.psum[:, 4 + n % 4, k * P:(k + 1) * P], tile, m.ident[:])
        mm.then_inc(m.rows_transposed, 1)


def transpose_tile_scalar(m, act, t, i):
    for half in range(2):
        n = 2 * i + half
        act.wait_ge(m.rows_transposed, m.turned_before + n + 1)
        bank = m.psum[:, 4 + n % 4, :].rearrange("p (k n) -> p k n", k=4)
        act.copy(m.cols[:, 4 * half:4 * half + 4, t * P:(t + 1) * P], bank).then_inc(m.columns_ready, 1)


def mix(nc, m, a):
    items = [(pair, t, e) for pair in range(HEADS // 2) for t in range(TT) for e in range(2)]
    steps = len(items) // 2
    in_flight = 6
    with ExitStack() as scope:
        table = m.xm[:].rearrange("p t d -> p (t d)")[:, 0:4 * TAB * GRID_W].rearrange("p (h j c) -> p h j c", h=4, j=TAB)
        window = scope.enter_context(nc.sbuf_tensor("window", [P, GRID_W], F32))
        w_s = scope.enter_context(nc.sbuf_tensor("w_s_sb", [P, GROUPS, P], F32))
        b_s = scope.enter_context(nc.sbuf_tensor("b_s_sb", [P, GROUPS], F32))
        logits = scope.enter_context(nc.sbuf_tensor("logits", [P, in_flight, KEYS_ALL], F32))
        probs_t = scope.enter_context(nc.sbuf_tensor("probs_t", [P, 2, KEYS_ALL // P, SEQ], F32))
        neg_max = scope.enter_context(nc.sbuf_tensor("neg_max", [P, in_flight], F32))
        row_sum = scope.enter_context(nc.sbuf_tensor("row_sum", [P, in_flight], F32))
        stats = scope.enter_context(nc.sbuf_tensor("gv_stats", [P, TT, 6], F32))
        moments = scope.enter_context(nc.sbuf_tensor("gv_moments", [P, TT, 2], F32))
        block = scope.enter_context(nc.Block(no_gpsimd_drain=True))
        turn_bank, out_bank = (6, 7), 7
        mixed_bank, g_turn_bank = 7, 6

        def scores_bank(s, e):
            return m.psum[:, 2 * (s % 2) + e, :]

        def ctx_bank(e):
            return m.psum[:, 4 + e, 0:CTX]

        @block.sync
        def _(sp):
            sp.dma_start(w_s[:], a["gm_w_s_t"].rearrange("g q p -> q g p")).then_inc(m.mix_consts_landed, 16)
            sp.dma_start(b_s[:], a["gm_b_s_t"]).then_inc(m.mix_consts_landed, 16)
            sp.dma_start(window[:], a["window"]).then_inc(m.mix_consts_landed, 16)
            for head in range(HEADS):
                if head >= 4:
                    sp.wait_ge(m.scores_biased, 2 * TT * ((head - 4) // 2 + 1))
                for r2 in range(2):
                    source = a["rpb_shifted"][head, :, 1 - r2:1 - r2 + TAB, :]
                    sp.dma_start(table[r2 * GRID_W:(r2 + 1) * GRID_W, head % 4], source).then_inc(m.table_landed[head % 4], 16)

        @block.vector
        def _(dve):
            for t in range(TT):
                m.vector.mark(dve.bn_stats(stats[:, t, :], m.gate_rows[:, t, HALF:D]))
            m.vector.wait(dve)
            for t in range(TT):
                m.vector.mark(dve.bn_aggr(moments[:, t, :], stats[:, t, :]))
            m.vector.wait(dve)
            dve.tensor_scalar_add(moments[:, :, 1], moments[:, :, 1], EPS).then_inc(m.gv_var_ready, 1)
            dve.wait_ge(m.gv_std_ready, 1)
            m.vector.link(dve, dve.reciprocal(moments[:, :, 1], moments[:, :, 1]))
            for t in range(TT):
                gv = m.gate_rows[:, t, HALF:D]
                dve.tensor_scalar(gv, gv, moments[:, t, 0:1], moments[:, t, 1:2], ALU.subtract, ALU.mult).then_inc(m.gv_ready, 1)
            dve.wait_ge(m.mix_consts_landed, 48)

            def gate(t):
                dve.wait_ge(m.mixed_ready, t + 1)
                for g in range(GROUPS):
                    cols = slice(g * P, (g + 1) * P)
                    last = dve.scalar_tensor_tensor(m.gate_rows[:, t, cols], m.psum[:, mixed_bank, cols],
                                                    b_s[:, g:g + 1], m.gate_rows[:, t, cols], ALU.add, ALU.mult)
                last.then_inc(m.mixed_taken, 1)

            def bias_scores(i):
                pair, t, e = items[i]
                head = 2 * pair + e
                if t == 0:
                    dve.wait_ge(m.table_landed[head % 4], 32 * (head // 4 + 1))
                    mask = window[:].unsqueeze(1).to_broadcast([P, TAB, GRID_W])
                    m.vector.link(dve, dve.tensor_tensor(table[:, head % 4], table[:, head % 4], mask, ALU.add))
                dve.wait_ge(m.scores_ready[e], i // 2 + 1)
                slot = i % in_flight
                if i >= in_flight:
                    dve.wait_ge(m.probs_turned, 2 * (i - in_flight + 1))
                j = 2 * (TT - 1 - t)
                rows = table[:, head % 4, j:j + GRID_ROWS, :].rearrange("p r c -> p (r c)")
                dve.tensor_tensor(logits[:, slot, 0:SEQ], scores_bank(i // 2, e), rows, ALU.add).then_inc(m.scores_biased, 1)
                dve.wait_ge(m.scores_biased, i + 1)
                dve.wait_ge(m.ctx_scores_taken, i + 1)
                m.vector.link(dve, dve.reduce_max(neg_max[:, slot:slot + 1], logits[:, slot, :], AX_X))
                dve.tensor_scalar_mul(neg_max[:, slot:slot + 1], neg_max[:, slot:slot + 1], -1.0).then_inc(m.max_ready, 1)

            def invert_sum(i):
                slot = i % in_flight
                dve.wait_ge(m.probs_ready, i + 1)
                dve.reciprocal(row_sum[:, slot:slot + 1], row_sum[:, slot:slot + 1]).then_inc(m.inv_sum_ready, 1)

            def take_turned(i):
                pair, t, e = items[i]
                dve.wait_ge(m.probs_turned, 2 * i + 1)
                if t == 0 and pair >= 1:
                    dve.wait_ge(m.heads_out_ready, 2 * pair)
                dve.tensor_copy(probs_t[:, e, 0:4, t * P:(t + 1) * P],
                                m.psum[:, turn_bank[0], :].rearrange("p (c q) -> p c q", c=4)).then_inc(m.turned_taken_vector, 1)

            bias_scores(0)
            bias_scores(1)
            gate(0)
            bias_scores(2)
            bias_scores(3)
            for t in range(1, TT):
                gate(t)
            invert_sum(0)
            invert_sum(1)
            for s in range(steps):
                take_turned(2 * s)
                if s + 1 < steps:
                    invert_sum(2 * s + 2)
                    invert_sum(2 * s + 3)
                take_turned(2 * s + 1)
                if s + 2 < steps:
                    bias_scores(2 * s + 4)
                    bias_scores(2 * s + 5)

        @block.gpsimd
        def _(pool):
            for i in range(1, len(items), 2):
                slot = i % in_flight
                pool.wait_ge(m.inv_sum_ready, i + 1)
                pool.tensor_scalar(logits[:, slot, :], logits[:, slot, :], row_sum[:, slot:slot + 1], None,
                                   ALU.mult).then_inc(m.probs_normal[1], 1)

        @block.scalar
        def _(act):
            act.wait_ge(m.gv_var_ready, 1)
            act.activation(moments[:, :, 1], moments[:, :, 1], ACT.Sqrt).then_inc(m.gv_std_ready, 1)

            def take_ctx(i):
                e = i % 2
                act.wait_ge(m.scores_ready[e], i // 2 + 1)
                if i >= in_flight:
                    act.wait_ge(m.probs_turned, 2 * (i - in_flight + 1))
                act.copy(logits[:, i % in_flight, SEQ:KEYS_ALL], ctx_bank(e)).then_inc(m.ctx_scores_taken, 1)

            def exponentials(i):
                slot = i % in_flight
                act.wait_ge(m.max_ready, i + 1)
                act.activation(logits[:, slot, :], logits[:, slot, :], ACT.Exp, bias=neg_max[:, slot:slot + 1],
                               accum_out=row_sum[:, slot:slot + 1]).then_inc(m.probs_ready, 1)

            def normalise(i):
                slot = i % in_flight
                act.wait_ge(m.inv_sum_ready, i + 1)
                act.activation(logits[:, slot, :], logits[:, slot, :], ACT.Copy, scale=row_sum[:, slot:slot + 1]).then_inc(m.probs_normal[0], 1)

            def take_turned(i):
                pair, t, e = items[i]
                act.wait_ge(m.probs_turned, 2 * i + 2)
                if t == 0 and pair >= 1:
                    act.wait_ge(m.heads_out_ready, 2 * pair)
                act.copy(probs_t[:, e, 4:6, t * P:(t + 1) * P],
                         m.psum[:, turn_bank[1], 0:CTX].rearrange("p (c q) -> p c q", c=2)).then_inc(m.turned_taken_scalar, 1)

            def take_g_columns(t):
                act.wait_ge(m.g_turned, t + 1)
                act.copy(m.cols[:, 4:8, t * P:(t + 1) * P],
                         m.psum[:, g_turn_bank, :].rearrange("p (k n) -> p k n", k=4)).then_inc(m.g_columns_taken, 1)

            take_ctx(0)
            take_ctx(1)
            take_g_columns(0)
            take_ctx(2)
            take_ctx(3)
            exponentials(0)
            exponentials(1)
            take_g_columns(1)
            exponentials(2)
            exponentials(3)
            normalise(0)
            take_g_columns(2)
            take_g_columns(3)
            for s in range(steps):
                take_turned(2 * s)
                if s + 1 < steps:
                    normalise(2 * s + 2)
                take_turned(2 * s + 1)
                if s + 2 < steps:
                    take_ctx(2 * s + 4)
                    take_ctx(2 * s + 5)
                pair, t, _ = items[2 * s]
                if t == TT - 1:
                    act.wait_ge(m.heads_out_ready, 2 * (pair + 1))
                    act.copy(m.cols[:, pair, 0:SEQ], m.psum[:, out_bank, :]).then_inc(m.heads_out_taken, 1)
                if s + 2 < steps:
                    exponentials(2 * s + 4)
                    exponentials(2 * s + 5)

        def scores(pe, s):
            pair, t, _ = items[2 * s]
            if s >= 2:
                pe.wait_ge(m.scores_biased, 2 * (s - 1))
            for e in range(2):
                part = slice(e * HEAD_DIM, (e + 1) * HEAD_DIM)
                pe.matmul(scores_bank(s, e), m.q_cols[part, pair, t * P:(t + 1) * P], m.k_cols[part, pair, 0:SEQ],
                          start=True, stop=True)

        def ctx_scores(pe, s):
            pair, t, _ = items[2 * s]
            if s >= 1:
                pe.wait_ge(m.ctx_scores_taken, 2 * s)
            for e in range(2):
                part = slice(e * HEAD_DIM, (e + 1) * HEAD_DIM)
                pe.matmul(ctx_bank(e), m.q_cols[part, pair, t * P:(t + 1) * P], m.k_cols[part, pair, SEQ:KEYS_ALL],
                          start=True, stop=True).then_inc(m.scores_ready[e], 1)

        def turn_probs(pe, i):
            pair, t, e = items[i]
            pe.wait_ge(m.probs_normal[e], i // 2 + 1)
            if i == 0:
                pe.wait_ge(m.g_columns_taken, TT)
            else:
                pe.wait_ge(m.turned_taken_vector, i)
                pe.wait_ge(m.turned_taken_scalar, i)
            if t == e == 0 and pair >= 1:
                pe.wait_ge(m.heads_out_taken, pair)
            for c in range(KEYS_ALL // P):
                mm = pe.transpose(m.psum[:, turn_bank[c // 4], (c % 4) * P:(c % 4 + 1) * P],
                                  logits[:, i % in_flight, c * P:(c + 1) * P], m.ident[:])
                if c == 3 or c == 5:
                    mm.then_inc(m.probs_turned, 1)

        def weighted_values(pe, pair):
            pe.wait_ge(m.turned_taken_vector, 2 * TT * (pair + 1))
            pe.wait_ge(m.turned_taken_scalar, 2 * TT * (pair + 1))
            for c in range(KEYS_ALL // P):
                for e in range(2):
                    head = 2 * pair + e
                    mm = pe.matmul(m.psum[e * HEAD_DIM:(e + 1) * HEAD_DIM, out_bank, :],
                                   m.v_rows[:, c, head * HEAD_DIM:(head + 1) * HEAD_DIM], probs_t[:, e, c, :],
                                   start=c == 0, stop=c == KEYS_ALL // P - 1, tile_position=(0, e * HEAD_DIM))
                    if c == KEYS_ALL // P - 1:
                        mm.then_inc(m.heads_out_ready, 1)

        @block.tensor
        def _(pe):
            scores(pe, 0)
            ctx_scores(pe, 0)
            pe.wait_ge(m.mix_consts_landed, 48)
            for t in range(TT):
                pe.wait_ge(m.gv_ready, t + 1)
                for g in range(GROUPS):
                    mm = pe.matmul(m.psum[:, mixed_bank, g * P:(g + 1) * P], w_s[:, g, :],
                                   m.gate_rows[:, t, HALF + g * P:HALF + (g + 1) * P], start=True, stop=True)
                mm.then_inc(m.mixed_ready, 1)
                if t == 0:
                    scores(pe, 1)
                    ctx_scores(pe, 1)
                pe.wait_ge(m.mixed_taken, t + 1)
                if t >= 1:
                    pe.wait_ge(m.g_columns_taken, t)
                for g in range(GROUPS):
                    mm = pe.transpose(m.psum[:, g_turn_bank, g * P:(g + 1) * P],
                                      m.gate_rows[:, t, g * P:(g + 1) * P], m.ident[:])
                mm.then_inc(m.g_turned, 1)
            for s in range(steps):
                turn_probs(pe, 2 * s)
                if s + 2 < steps:
                    scores(pe, s + 2)
                turn_probs(pe, 2 * s + 1)
                if s + 2 < steps:
                    ctx_scores(pe, s + 2)
                pair, t, _ = items[2 * s]
                if t == TT - 1:
                    weighted_values(pe, pair)


def norm_tile_vector(m, dve, t, gate_row, ln, scratch, banks, moments, stats):
    x = m.x[:, t, :]
    for half in range(2):
        cols = slice(half * HALF, (half + 1) * HALF)
        m.vector.mark(dve.tensor_tensor(scratch[:, cols], m.psum[:, banks[half], :], gate_row[:, cols], ALU.mult))
    m.vector.wait(dve)
    m.vector.link(dve, dve.scalar_tensor_tensor(x, x, ALPHA, scratch[:], ALU.mult, ALU.add))
    for half in range(2):
        m.vector.mark(dve.bn_stats(stats[:, half, :], m.x[:, t, half * HALF:(half + 1) * HALF]))
    m.vector.wait(dve)
    m.vector.link(dve, dve.bn_aggr(moments[:], stats[:]))
    dve.tensor_scalar_add(moments[:, 1:2], moments[:, 1:2], EPS).then_inc(m.var_ready, 1)
    m.norms += 1
    dve.wait_ge(m.std_ready, m.norms)
    m.vector.link(dve, dve.reciprocal(moments[:, 1:2], moments[:, 1:2]))
    m.vector.link(dve, dve.tensor_scalar(x, x, moments[:, 0:1], moments[:, 1:2], ALU.subtract, ALU.mult))
    m.vector.link(dve, dve.tensor_tensor(x, x, ln[:, 0, :], ALU.mult))
    return dve.tensor_tensor(x, x, ln[:, 1, :], ALU.add)


def norm_tile_scalar(m, act, moments):
    m.roots += 1
    act.wait_ge(m.var_ready, m.roots)
    act.activation(moments[:, 1:2], moments[:, 1:2], ACT.Sqrt).then_inc(m.std_ready, 1)


def residual(nc, m, a, layer):
    with ExitStack() as scope:
        ln = scope.enter_context(nc.sbuf_tensor(f"ln_mix{layer}", [P, 2, D], F32))
        scratch = scope.enter_context(nc.sbuf_tensor(f"scratch_mix{layer}", [P, D], F32))
        stats = scope.enter_context(nc.sbuf_tensor(f"stats_mix{layer}", [P, 2, 6], F32))
        moments = scope.enter_context(nc.sbuf_tensor(f"moments_mix{layer}", [P, 2], F32))
        block = scope.enter_context(nc.Block(no_gpsimd_drain=True))

        @block.sync
        def _(sp):
            sp.dma_start(ln[:, 0, :], a["ln_g"][layer, 0:1, :].to_broadcast([P, D])).then_inc(m.ln_landed, 16)
            sp.dma_start(ln[:, 1, :], a["ln_b"][layer, 0:1, :].to_broadcast([P, D])).then_inc(m.ln_landed, 16)
            sp.wait_ge(m.mix_out_ready, (layer + 1) * TT)
            for n in range(2):
                load_query_weights(m, sp, a, layer, n)

        @block.tensor
        def _(pe):
            w = [wait_block(m, pe, RESIDUAL_FIRST[layer] + half) for half in range(2)]
            for t in range(TT + 1):
                if t < TT:
                    if t >= 2:
                        pe.wait_ge(m.tile_modulated, layer * TT + t - 1)
                    for half in range(2):
                        for k in range(KT):
                            mm = pe.matmul(m.psum[:, 2 * (t % 2) + half, :], m.cols[:, k, t * P:(t + 1) * P],
                                           w[half][:, k, :], start=k == 0, stop=k == KT - 1)
                    mm.then_inc(m.mix_out_ready, 1)
                if t >= 1:
                    pe.wait_ge(m.tile_modulated, layer * TT + t)
                    transpose_tile_tensor(m, pe, m.xm[:, t - 1, :], t - 1)

        @block.vector
        def _(dve):
            dve.wait_ge(m.ln_landed, 32 * (2 * layer + 1))
            for t in range(TT):
                dve.wait_ge(m.mix_out_ready, layer * TT + t + 1)
                m.vector.link(dve, norm_tile_vector(m, dve, t, m.mod[:, 2 * D:3 * D], ln, scratch,
                                                    (2 * (t % 2), 2 * (t % 2) + 1), moments, stats))
                m.vector.link(dve, dve.tensor_tensor(m.xm[:, t, :], m.x[:, t, :], m.mod[:, 4 * D:5 * D], ALU.mult))
                dve.tensor_tensor(m.xm[:, t, :], m.xm[:, t, :], m.mod[:, 3 * D:4 * D], ALU.add).then_inc(m.tile_modulated, 1)

        @block.scalar
        def _(act):
            for t in range(TT):
                norm_tile_scalar(m, act, moments)
                transpose_tile_scalar(m, act, t, t)
    m.turned_before += 2 * TT


def experts(nc, m, a, layer):
    sections = SLOTS // 32
    groups = 32 // RING
    u_table, v_table = a[f"peer_u{layer}"], a[f"peer_v{layer}"]
    half_ring = RING // 2
    queries = [(hp, 0, 1) for hp in range(4)] + [(hp, 1, TT) for hp in range(4)] + [(hp, 0, TT) for hp in range(4, HP)]
    done = layer * len(queries)
    with ExitStack() as scope:
        def sb(name, shape, dtype=F32):
            return scope.enter_context(nc.sbuf_tensor(f"{name}{layer}", shape, dtype))
        idx = sb("idx", [P, (4 * TT + 1) * 32], U32)
        gates = sb("gates", [P, (4 * TT + 1) * 32])
        v_ring = sb("v_ring", [P, RING, D])
        current_u = sb("current_u", [P, 2, RING], U32)
        current_v = sb("current_v", [P, 2, RING], U32)
        dots = sb("dots", [P, groups, RING])
        weights = sb("weights", [P, groups, RING])
        columns = m.cols[:].rearrange("p k n -> p (k n)")
        ln = columns[:, 0:2 * D].rearrange("p (g d) -> p g d", g=2)
        diagonal = columns[:, 2 * D:4 * D].rearrange("p (g j k) -> p g j k", g=2, j=RING)
        scratch = columns[:, 4 * D:5 * D]
        keys = v_ring[:, RING - 3:RING - 1, :].rearrange("p j (h k) -> p (j h) k", k=NKEYS)
        query = v_ring[:, RING - 1, :].rearrange("p (j n) -> p j n", j=2)
        v_slots_free = RING - 3
        first = sb("first", [P, 4, NKEYS])
        rest = sb("rest", [P, 4, NKEYS])
        zeros = sb("zeros", [1, HALF])
        stats = sb("stats_peer", [P, 2, 6])
        moments = sb("moments_peer", [P, 2])
        top = sb("top", [P, 4, TOPK])
        top_at = sb("top_at", [P, 4, TOPK], U32)
        top_at_f = sb("top_at_f", [P, 4, TOPK])
        sums = sb("sums", [P, 2, TOPK * TOPK])
        sums_rest = sb("sums_rest", [P, 2, TOPK * TOPK])
        best = sb("best", [P, 2, TOPK])
        best_at = sb("best_at", [P, 2, TOPK], U32)
        digits = sb("digits", [P, 2, 2, TOPK], U32)
        digits_f = sb("digits_f", [P, 2, 2, TOPK])
        match = sb("match", [P, 2, TOPK, TOPK])
        found = sb("found", [P, 2, 2 * TOPK])
        expd = sb("expd", [P, 2, TOPK])
        denom = sb("denom", [P, 2])
        u_ring = [m.ring[:, 1 - QUERY_SLOT if j < 4 else QUERY_SLOT, 2 * (j % 4):2 * (j % 4) + 2, :].rearrange("p k n -> p (k n)") for j in range(RING)]
        first_u_ring = [v_ring[:, j, :] if j < 4 else u_ring[j - 4] for j in range(RING)]
        block = scope.enter_context(nc.Block(no_gpsimd_drain=True))
        groups_before = layer * TT * sections * groups
        sections_before = layer * (TT * sections + 1)
        currents_before = 2 * groups * (layer * (TT * sections - 1) - 1)

        def rounds(dve, values, remaining, tops, ats, n):
            for i in range(n):
                m.select.mark(dve.max(tops[:, i, 0:8], values[:, i, :]))
            m.select.wait(dve)
            for i in range(n):
                m.select.mark(dve.max_index(ats[:, i, 0:8], tops[:, i, 0:8], values[:, i, :]))
                m.select.mark(dve.match_replace(remaining[:, i, :], tops[:, i, 0:8], values[:, i, :], LOWEST))
            m.select.wait(dve)
            for i in range(n):
                m.select.mark(dve.max(tops[:, i, 8:16], remaining[:, i, :]))
            m.select.wait(dve)
            for i in range(n):
                m.select.mark(dve.max_index(ats[:, i, 8:16], tops[:, i, 8:16], remaining[:, i, :]))
            m.select.wait(dve)

        def select(dve, section, nth):
            m.select.begin(nth)
            select_keys(dve, section)
            select_experts(dve, section, nth)
            select_gates(dve, section, nth)

        def select_keys(dve, section):
            m.select.link(dve, dve.tensor_copy(first[:].rearrange("p j k -> p (j k)"), m.scores[:, bass.ds(section, 1), :].squeeze(1)))
            rounds(dve, first, rest, top, top_at, 4)

        def select_experts(dve, section, nth):
            m.select.mark(dve.tensor_copy(top_at_f[:], top_at[:]))
            sets = top[:].rearrange("p (h s) r -> p h s r", s=2)
            sets_at = top_at_f[:].rearrange("p (h s) r -> p h s r", s=2)
            square = [P, 2, TOPK, TOPK]
            m.select.link(dve, dve.tensor_tensor(sums[:].rearrange("p h (r s) -> p h r s", r=TOPK),
                                                 sets[:, :, 0, :].unsqueeze(3).to_broadcast(square),
                                                 sets[:, :, 1, :].unsqueeze(2).to_broadcast(square), ALU.add))
            rounds(dve, sums, sums_rest, best, best_at, 2)
            dve.tensor_tensor(expd[:], best[:], best[:, :, 0:1].to_broadcast([P, 2, TOPK]), ALU.subtract).then_inc(m.shifted_ready, 1)
            m.select.mark(dve.tensor_single_scalar(digits[:, 0], best_at[:], 4, ALU.logical_shift_right))
            m.select.mark(dve.tensor_single_scalar(digits[:, 1], best_at[:], TOPK - 1, ALU.bitwise_and))
            m.select.wait(dve)
            m.select.link(dve, dve.tensor_copy(digits_f[:], digits[:]))
            for s in range(2):
                ranks = m.ranks[:].unsqueeze(1).unsqueeze(1).to_broadcast(square)
                m.select.link(dve, dve.tensor_tensor(match[:], digits_f[:, s].unsqueeze(3).to_broadcast(square), ranks, ALU.is_equal))
                m.select.link(dve, dve.tensor_tensor(match[:], match[:], sets_at[:, :, s, :].unsqueeze(2).to_broadcast(square), ALU.mult))
                m.select.link(dve, dve.tensor_reduce(found[:, s, :], match[:].rearrange("p h r s -> p (h r) s"), AX_X, ALU.add))
            m.select.link(dve, dve.scalar_tensor_tensor(found[:, 0, :], found[:, 0, :], float(NKEYS), found[:, 1, :], ALU.mult, ALU.add))
            dve.tensor_copy(idx[:, bass.ds(section * 32, 32)], found[:, 0, :]).then_inc(m.section_selected, 1)

        def select_gates(dve, section, nth):
            dve.wait_ge(m.exps_ready, nth)
            m.select.link(dve, dve.tensor_reduce(denom[:], expd[:], AX_X, ALU.add))
            m.select.link(dve, dve.reciprocal(denom[:], denom[:]))
            dve.tensor_tensor(gates[:, bass.ds(section * 32, 32)].rearrange("p (h r) -> p h r", h=2), expd[:],
                              denom[:].unsqueeze(2).to_broadcast([P, 2, TOPK]), ALU.mult).then_inc(m.gates_ready, 1)

        @block.sync
        def _(sp):
            sp.dma_start(keys, a["peer_keys_t"][layer].rearrange("h d k -> d h k")).then_inc(m.keys_landed, 16)
            for pair in range(2, PAIRS):
                last = max(i for i, (hp, _, _) in enumerate(queries) if hp // 2 == pair - 2)
                sp.wait_ge(m.query_ready, done + last + 1)
                load_query_weights(m, sp, a, layer, pair)
            sp.wait_ge(m.query_ready, done + len(queries))
            sp.dma_start(ln[:, 0, :], a["ln_g"][layer, 1:2, :].to_broadcast([P, D])).then_inc(m.ln_landed, 16)
            sp.dma_start(ln[:, 1, :], a["ln_b"][layer, 1:2, :].to_broadcast([P, D])).then_inc(m.ln_landed, 16)
            if layer == 0:
                sp.wait_ge(m.dots_done, (TT * sections * groups + 1) * RING)
                for n in range(2):
                    load_block(m, sp, MOD_FIRST[1] + n, block_of(modulation_weights(a, 1), n))
            if layer == 1:
                for t in range(TT):
                    sp.wait_ge(m.tile_done, TT + t + 1)
                    sp.dma_start(a["out"][0, t * P:(t + 1) * P, :], m.x[:, t, :]).then_inc(m.out_stored, 16)
                sp.wait_ge(m.out_stored, 16 * TT)

        def gather(pool, table, out, index, landed):
            pool.indirect_dma_start(out=out, out_offset=None, in_=table,
                                    in_offset=bass.IndirectOffsetOnAxis(ap=index, axis=0)).then_inc(landed, 16)

        @block.gpsimd
        def _(pool):
            pool.wait_ge(m.section_selected, sections_before + 1)
            for g in range(groups):
                for j in range(RING):
                    if g >= 1:
                        pool.wait_ge(m.dots_done, (groups_before + g) * RING + j + 1)
                    pool.nop(nofuse=True)
                    gather(pool, u_table, first_u_ring[j], idx[:, g * RING + j:g * RING + j + 1], m.u_landed[j])
            for j in range(RING):
                if j == 0:
                    pool.wait_ge(m.dots_done, (groups_before + groups + 1) * RING)
                    pool.nop(nofuse=True)
                if j == v_slots_free:
                    pool.wait_ge(m.key_scores_ready, done + len(queries))
                    pool.nop(nofuse=True)
                gather(pool, v_table, v_ring[:, j, :], idx[:, j:j + 1], m.v_landed[j])
            with pool.Fori(1, TT * sections) as s:
                pool.wait_ge(m.section_selected, sections_before + s + 1)
                for g in range(groups):
                    group = groups_before + s * groups + g
                    pool.tensor_copy(current_u[:, g % 2, :], idx[:, bass.ds(s * 32 + g * RING, RING)]).then_inc(m.current_ready, 1)
                    pool.wait_ge(m.current_ready, currents_before + s * (2 * groups) + 2 * g + 1)
                    for j in range(RING):
                        if j % half_ring == 0:
                            pool.wait_ge(m.dots_done, group * RING + j + half_ring)
                            pool.nop(nofuse=True)
                        gather(pool, u_table, u_ring[j], current_u[:, g % 2, j:j + 1], m.u_landed[j])
                    pool.tensor_copy(current_v[:, g % 2, :], idx[:, bass.ds(s * 32 - 32 + (g + 1) * RING, RING)]).then_inc(m.current_ready, 1)
                    pool.wait_ge(m.current_ready, currents_before + s * (2 * groups) + 2 * g + 2)
                    for j in range(RING):
                        if j % half_ring == 0:
                            pool.wait_ge(m.v_used, (group + 2 - groups) * RING + j + half_ring)
                            pool.nop(nofuse=True)
                        gather(pool, v_table, v_ring[:, j, :], current_v[:, g % 2, j:j + 1], m.v_landed[j])
            for g in range(1, groups):
                slot = (TT * sections - 1) * 32 + g * RING
                for j in range(RING):
                    pool.wait_ge(m.v_used, (groups_before + (TT * sections - 1) * groups + g + 1) * RING + j + 1)
                    pool.nop(nofuse=True)
                    gather(pool, v_table, v_ring[:, j, :], idx[:, slot + j:slot + j + 1], m.v_landed[j])

        def norm(dve, t):
            if t == 0:
                dve.wait_ge(m.ln_landed, 32 * (2 * layer + 2))
            dve.wait_ge(m.experts_ready, layer * TT + t + 1)
            norm_tile_vector(m, dve, t, m.mod[:, 5 * D:6 * D], ln, scratch, (2 * t, 2 * t + 1), moments, stats).then_inc(m.tile_done, 1)

        @block.vector
        def _(dve):
            def weigh(section):
                dve.wait_ge(m.acted_ready, groups_before + (section + 1) * groups)
                dve.wait_ge(m.gates_ready, sections_before + section + 1)
                dve.tensor_tensor(weights[:].rearrange("p g j -> p (g j)"), dots[:].rearrange("p g j -> p (g j)"),
                                  gates[:, bass.ds(section * 32, 32)], ALU.mult).then_inc(m.sections_weighed, 1)
                dve.wait_ge(m.sections_weighed, layer * TT * sections + section + 1)

            m.vector.mark(dve.memset(zeros[:], 0.0))
            if layer == 0:
                dve.memset(found[:], 0.0).then_inc(m.dots_done, RING)
                dve.memset(match[:], 0.0).then_inc(m.v_used, 2 * RING)
            m.vector.mark(dve.memset(m.scores[:, TT * 4, :], 0.0))
            m.vector.wait(dve)
            dve.engine_nop().then_inc(m.zeros_ready, 1)
            dve.wait_ge(m.key_scores_taken, done + 4)
            select(dve, 0, sections_before + 1)
            for g in range(groups):
                for j in range(RING):
                    dve.wait_ge(m.u_landed[j], (groups_before + g + 1) * 16)
                    dve.tensor_tensor_reduce(out=first_u_ring[j], in0=first_u_ring[j], in1=m.xm[:, 0, :], scale=1.0, scalar=0.0,
                                             op0=ALU.mult, op1=ALU.add, accum_out=dots[:, g, j:j + 1]).then_inc(m.dots_done, 1)
                if g == groups - 2:
                    dve.wait_ge(m.key_scores_taken, done + 12)
                    m.select.begin(sections_before + 2)
                    select_keys(dve, 1)
            select_experts(dve, 1, sections_before + 2)
            weigh(0)
            select_gates(dve, 1, sections_before + 2)
            dve.wait_ge(m.key_scores_taken, done + len(queries))
            for t in range(TT):
                with dve.Fori(1 if t == 0 else 0, sections) as q:
                    section = t * sections + q
                    for g in range(groups):
                        group = groups_before + section * groups + g
                        for j in range(RING):
                            dve.wait_ge(m.u_landed[j], (group + 1) * 16)
                            dve.tensor_tensor_reduce(out=u_ring[j], in0=u_ring[j], in1=m.xm[:, t, :], scale=1.0, scalar=0.0,
                                                     op0=ALU.mult, op1=ALU.add, accum_out=dots[:, g, j:j + 1]).then_inc(m.dots_done, 1)
                        if g == 0:
                            m.select.begin(sections_before + section + 2)
                            select_keys(dve, section + 1)
                        if g == 1:
                            select_experts(dve, section + 1, sections_before + section + 2)
                        if g == 2:
                            select_gates(dve, section + 1, sections_before + section + 2)
                    weigh(section)
                if t >= 1:
                    norm(dve, t - 1)
            norm(dve, TT - 1)

        @block.scalar
        def _(act):
            def exponentials(nth):
                act.wait_ge(m.shifted_ready, nth)
                act.activation(expd[:], expd[:], ACT.Exp).then_inc(m.exps_ready, 1)

            by_tile = m.scores[:, 0:TT * 4, :].rearrange("p (t q) (j k) -> p t q j k", t=TT, j=4)
            for i in range(len(queries) + 1):
                if i < len(queries):
                    _, t0, t1 = queries[i]
                    act.wait_ge(m.query_ready, done + i + 1)
                    if i >= 2:
                        act.wait_ge(m.key_scores_ready, done + i - 1)
                    act.copy(query[:, i % 2, t0 * P:t1 * P], m.psum[:, i % 2, t0 * P:t1 * P]).then_inc(m.query_taken, 1)
                if i >= 1:
                    hp, t0, t1 = queries[i - 1]
                    act.wait_ge(m.key_scores_ready, done + i)
                    act.copy(by_tile[:, t0:t1, hp // 4, hp % 4, :],
                             m.psum[:, 2 + (i - 1) % 2, t0 * P:t1 * P].rearrange("p (t k) -> p t k", k=P)).then_inc(m.key_scores_taken, 1)
                if i == 9:
                    exponentials(sections_before + 1)

            def diagonals(section, g):
                group = groups_before + section * groups + g
                act.wait_ge(m.sections_weighed, layer * TT * sections + section + 1)
                act.wait_ge(m.v_used, (group + 1) * RING)
                for j in range(RING):
                    last = act.activation(diagonal[:, g % 2, j, :], m.ident[:], ACT.Copy, scale=weights[:, g, j:j + 1])
                last.then_inc(m.diagonals_ready, 1)

            act.wait_ge(m.dots_done, (groups_before + groups + 1) * RING)
            act.activation(dots[:], dots[:], ACT.Gelu).then_inc(m.acted_ready, groups)
            exponentials(sections_before + 2)
            for t in range(TT):
                with act.Fori(1 if t == 0 else 0, sections) as q:
                    section = t * sections + q
                    for g in range(groups):
                        if g == 0:
                            diagonals(section - 1, 0)
                        if g + 1 < groups:
                            diagonals(section - 1, g + 1)
                        if g == 2:
                            exponentials(sections_before + section + 2)
                        act.wait_ge(m.dots_done, (groups_before + section * groups + g + 2) * RING)
                        act.activation(dots[:, g, :], dots[:, g, :], ACT.Gelu).then_inc(m.acted_ready, 1)
                if 1 <= t < TT - 1:
                    norm_tile_scalar(m, act, moments)
            for g in range(groups):
                diagonals(TT * sections - 1, g)
                if g == 1:
                    norm_tile_scalar(m, act, moments)
            norm_tile_scalar(m, act, moments)

        @block.tensor
        def _(pe):
            for i in range(len(queries) + 1):
                if i < len(queries):
                    hp, t0, t1 = queries[i]
                    w = wait_query_weights(m, pe, layer, hp // 2)
                    if i >= 2:
                        pe.wait_ge(m.query_taken, done + i - 1)
                    for k in range(KT):
                        mm = pe.matmul(m.psum[:, i % 2, t0 * P:t1 * P], w[:, k, (hp % 2) * P:(hp % 2 + 1) * P],
                                       m.cols[:, k, t0 * P:t1 * P], start=k == 0, stop=k == KT - 1)
                    mm.then_inc(m.query_ready, 1)
                if i >= 1:
                    j = i - 1
                    hp, t0, t1 = queries[j]
                    if j == 0:
                        pe.wait_ge(m.keys_landed, 16 * (layer + 1))
                    pe.wait_ge(m.query_taken, done + j + 1)
                    if j >= 2:
                        pe.wait_ge(m.key_scores_taken, done + j - 1)
                    for t in range(t0, t1):
                        mm = pe.matmul(m.psum[:, 2 + j % 2, t * P:(t + 1) * P], query[:, j % 2, t * P:(t + 1) * P],
                                       keys[:, hp, :], start=True, stop=True)
                    mm.then_inc(m.key_scores_ready, 1)
            pe.wait_ge(m.zeros_ready, layer + 1)
            pe.wait_ge(m.key_scores_taken, done + len(queries))
            for t in range(TT):
                for half in range(2):
                    pe.matmul(m.psum[:, 2 * t + half, :], zeros[:, 0:P], zeros[:], start=True, stop=False)
                with pe.Fori(0, sections) as q:
                    for g in range(groups):
                        group = groups_before + (t * sections + q) * groups + g
                        pe.wait_ge(m.diagonals_ready, group + 1)
                        for j in range(RING):
                            pe.wait_ge(m.v_landed[j], (group + 1) * 16)
                            for half in range(2):
                                mm = pe.matmul(m.psum[:, 2 * t + half, :], diagonal[:, g % 2, j, :],
                                               v_ring[:, j, half * HALF:(half + 1) * HALF], start=False, stop=False)
                            mm.then_inc(m.v_used, 1)
                for half in range(2):
                    mm = pe.matmul(m.psum[:, 2 * t + half, :], zeros[:, 0:P], zeros[:], start=False, stop=True)
                mm.then_inc(m.experts_ready, 1)


def sine_vector(m, dve, out, product, bias, freq, turns):
    m.vector.link(dve, dve.tensor_scalar(out, product, bias, freq, ALU.add, ALU.mult))
    m.vector.link(dve, dve.tensor_scalar(turns, out, 1 / (2 * np.pi), MAGIC, ALU.mult, ALU.add))
    m.vector.link(dve, dve.tensor_scalar_add(turns, turns, -MAGIC))
    for part in (TWO_PI_HIGH, TWO_PI_MID, TWO_PI_LOW):
        m.vector.link(dve, dve.scalar_tensor_tensor(out, turns, -part, out, ALU.mult, ALU.add))
    dve.tensor_scalar(out, out, PI_BELOW, -PI_BELOW, ALU.min, ALU.max).then_inc(m.angle_ready, 1)


def modulation_and_filter(nc, m, a):
    turns = range(MOD_BLOCKS + 1)
    filter_turn, sum_turn, spectrum_turn, highest_turn = 2, 3, 8, 12
    with ExitStack() as scope:
        def sb(name, shape):
            return scope.enter_context(nc.sbuf_tensor(name, shape, F32))
        parts = sb("mod_parts1", [P, 2, HALF])
        fwd, bwd = sb("fwd", [P, TT, D]), sb("bwd", [P, TT + 1, D])
        w1, w2, ffn = sb("ffn_w1", [EMB, FFN]), sb("ffn_w2", [FFN, FFN]), sb("ffn_vectors", [FFN, 4])
        free = m.cols[:].rearrange("p k n -> p (k n)")
        decay = free[:, 0:2 * D].rearrange("p (s d) -> p s d", s=2)
        w3 = free[0:FFN, 2 * D:4 * D]
        absolute = free[:, 4 * D:6 * D].rearrange("p (s d) -> p s d", s=2)
        hidden = m.xm[0:FFN, 0, :].rearrange("p (s n) -> p s n", s=2)
        full_turns, position = m.xm[0:FFN, 1, 0:SEQ], m.xm[0:EMB, 1, SEQ:2 * SEQ]
        inv_l1 = m.xm[:, 2, :]
        block = scope.enter_context(nc.Block(no_gpsimd_drain=True))

        @block.sync
        def _(sp):
            for n in range(2):
                modulation_bias(m, sp, a, 1, n)
            sp.dma_start(position, a["position"]).then_inc(m.ffn_landed, 16)
            sp.dma_start(w1[:], a["hy_ffn_w1"][0]).then_inc(m.ffn_landed, 16)
            sp.dma_start(w2[:], a["hy_ffn_w2"][0]).then_inc(m.ffn_landed, 16)
            sp.dma_start(w3, a["hy_ffn_w3"][0]).then_inc(m.ffn_landed, 16)
            sp.dma_start(ffn[:], a["ffn_vectors"]).then_inc(m.ffn_landed, 16)
            for t in range(2):
                sp.dma_start(decay[:, t, :], a["decay"][t * P:(t + 1) * P, :]).then_inc(m.decay_landed[t], 16)
            for n in range(2, MOD_BLOCKS):
                modulation_load(m, sp, a, 1, n)
                t = n - filter_turn
                if 2 <= t < TT:
                    sp.wait_ge(m.filter_taken, 4 * (t - 1))
                    sp.dma_start(decay[:, t % 2, :], a["decay"][t * P:(t + 1) * P, :]).then_inc(m.decay_landed[t % 2], 16)
                if n == spectrum_turn - 2:
                    sp.dma_start(m.cos_in[:], a["cos_in"].rearrange("(t p) f -> p t f", p=P)).then_inc(m.dft_landed, 16)
                    sp.dma_start(m.sin_in[:], a["sin_in"].rearrange("(t p) f -> p t f", p=P)).then_inc(m.dft_landed, 16)
            modulation_load_next(m, sp, a, 1)

        def filter_tensor(pe, n):
            if n == 0:
                pe.wait_ge(m.ffn_landed, 80)
                pe.matmul(m.psum[0:FFN, 4, :], w1[:], position, start=True, stop=True).then_inc(m.hidden_ready, 1)
            if n == 1:
                pe.wait_ge(m.sine_ready, 1)
                pe.matmul(m.psum[0:FFN, 5, :], w2[:], hidden[:, 0, :], start=True, stop=True).then_inc(m.hidden_ready, 1)
            if n == filter_turn:
                pe.wait_ge(m.sine_ready, 2)
            if 0 <= n - filter_turn < TT:
                t = n - filter_turn
                for q in range(4):
                    i = 4 * t + q
                    if i >= 2:
                        pe.wait_ge(m.filter_taken, i - 1)
                    pe.matmul(m.psum[:, 4 + i % 2, :], hidden[:, 1, t * P:(t + 1) * P], w3[:, q * HALF:(q + 1) * HALF],
                              start=True, stop=True).then_inc(m.filter_ready, 1)
            if 0 <= n - sum_turn < TT:
                t = n - sum_turn
                for b in range(2):
                    pe.wait_ge(m.abs_ready, 2 * t + b + 1)
                    for half in range(2):
                        mm = pe.matmul(m.psum[:, 6 + half, :], m.ones[:], absolute[:, b, half * HALF:(half + 1) * HALF],
                                       start=t == b == 0, stop=t == TT - 1 and b == 1)
                    mm.then_inc(m.abs_summed, 1)
            if 0 <= n - spectrum_turn < TT:
                ft = n - spectrum_turn
                if ft == 0:
                    pe.wait_ge(m.dft_landed, 32)
                    pe.wait_ge(m.parts_ready, TT)
                    pe.wait_ge(m.l1_taken, 2)
                for half in range(2):
                    i = 2 * ft + half
                    if i >= 2:
                        pe.wait_ge(m.spectrum_taken, 2 * (i - 1))
                    for table, part, bank in ((m.cos_in, fwd, 4 + 2 * (i % 2)), (m.sin_in, bwd, 5 + 2 * (i % 2))):
                        for t in range(TT):
                            mm = pe.matmul(m.psum[:, bank, :], table[:, t, ft * P:(ft + 1) * P],
                                           part[:, t, half * HALF:(half + 1) * HALF], start=t == 0, stop=t == TT - 1)
                    mm.then_inc(m.spectrum_ready, 1)
            if n == highest_turn:
                pe.wait_ge(m.spectrum_taken, 14)
                for t in range(TT):
                    for half in range(2):
                        mm = pe.matmul(m.psum[32 * half:32 * half + 1, 4 + half, :], m.sin_in[:, t, 0:1],
                                       fwd[:, t, half * HALF:(half + 1) * HALF], start=t == 0, stop=t == TT - 1,
                                       tile_position=(0, 32 * half))
                        if t == TT - 1:
                            mm.then_inc(m.highest_ready, 1)

        @block.tensor
        def _(pe):
            for n in turns:
                modulation_tensor(m, pe, parts, 1, n)
                filter_tensor(pe, n)

        def filter_vector(dve, n):
            if n < 2:
                if n == 0:
                    dve.wait_ge(m.ffn_landed, 80)
                dve.wait_ge(m.hidden_ready, n + 1)
                sine_vector(m, dve, hidden[:, n, :], m.psum[0:FFN, 4 + n, :], ffn[:, 2 * n:2 * n + 1], ffn[:, 2 * n + 1:2 * n + 2], full_turns)
            if 0 <= n - filter_turn < TT:
                t = n - filter_turn
                dve.wait_ge(m.decay_landed[t % 2], 16 * (t // 2 + 1))
                for q in range(4):
                    dve.wait_ge(m.filter_ready, 4 * t + q + 1)
                    part, cols = (fwd[:, t] if q < 2 else bwd[:, t + 1]), slice((q % 2) * HALF, (q % 2 + 1) * HALF)
                    dve.tensor_tensor(part[:, cols], m.psum[:, 4 + (4 * t + q) % 2, :], decay[:, t % 2, cols], ALU.mult).then_inc(m.filter_taken, 1)
                if t == 0:
                    dve.wait_ge(m.filter_taken, 4)
                    m.vector.link(dve, dve.memset(bwd[0:1, 1, :], 0.0))
                dve.wait_ge(m.filter_taken, 4 * (t + 1))
                dve.engine_nop().then_inc(m.tile_decayed, 1)
            if 0 <= n - sum_turn < TT:
                t = n - sum_turn
                m.vector.mark(dve.tensor_tensor(bwd[:, t, :], fwd[:, t, :], bwd[:, t + 1, :], ALU.subtract))
                dve.wait_ge(m.abs_ready, 2 * (t + 1))
                m.vector.wait(dve)
                dve.tensor_tensor(fwd[:, t, :], fwd[:, t, :], bwd[:, t + 1, :], ALU.add).then_inc(m.parts_ready, 1)
                dve.wait_ge(m.parts_ready, t + 1)
            if n == sum_turn + TT:
                dve.wait_ge(m.abs_summed, 2 * TT)
                for half in range(2):
                    dve.reciprocal(inv_l1[:, half * HALF:(half + 1) * HALF], m.psum[:, 6 + half, :]).then_inc(m.l1_taken, 1)
                dve.wait_ge(m.l1_taken, 2)
            if 0 <= n - spectrum_turn < TT:
                ft = n - spectrum_turn
                for half in range(2):
                    i = 2 * ft + half
                    cols = slice(half * HALF, (half + 1) * HALF)
                    dve.wait_ge(m.spectrum_ready, i + 1)
                    dve.tensor_tensor(m.k_re[:, ft, cols], m.psum[:, 4 + 2 * (i % 2), :], inv_l1[:, cols], ALU.mult).then_inc(m.spectrum_taken, 1)
                    dve.tensor_tensor(m.k_im[:, ft, cols], m.psum[:, 5 + 2 * (i % 2), :], inv_l1[:, cols], ALU.mult).then_inc(m.spectrum_taken, 1)
            if n == highest_turn:
                dve.wait_ge(m.spectrum_taken, 16)
                dve.wait_ge(m.highest_ready, 2)
                for half in range(2):
                    cols = slice(half * HALF, (half + 1) * HALF)
                    dve.tensor_tensor(m.k_im[0:1, 0, cols], m.psum[32 * half:32 * half + 1, 4 + half, :], inv_l1[0:1, cols], ALU.mult).then_inc(m.highest_taken, 1)

        @block.vector
        def _(dve):
            for n in turns:
                modulation_vector(m, dve, parts, 1, n)
                filter_vector(dve, n)

        @block.scalar
        def _(act):
            for n in range(2):
                act.wait_ge(m.angle_ready, n + 1)
                act.activation(hidden[:, n, :], hidden[:, n, :], ACT.Sin).then_inc(m.sine_ready, 1)
            for t in range(TT):
                act.wait_ge(m.tile_decayed, t + 1)
                for b, part in enumerate((fwd[:, t, :], bwd[:, t + 1, :])):
                    if t >= 1:
                        act.wait_ge(m.abs_summed, 2 * (t - 1) + b + 1)
                    act.activation(absolute[:, b, :], part, ACT.Abs).then_inc(m.abs_ready, 1)


def hyena_project(nc, m, a):
    tiles = 3 * KT
    weights = feature_major(a["hy_w_in"][0])
    with ExitStack() as scope:
        h = scope.enter_context(nc.sbuf_tensor("h_rows1", [P, 2, D], F32))
        z = scope.enter_context(nc.sbuf_tensor("z_padded", [P, 2, SEQ + 2], F32))
        conv = scope.enter_context(nc.sbuf_tensor("conv", [P, SEQ], F32))
        vectors = scope.enter_context(nc.sbuf_tensor("hy_vectors_sb", [P, 5, tiles], F32))
        block = scope.enter_context(nc.Block(no_gpsimd_drain=True))

        @block.sync
        def _(sp):
            sp.dma_start(vectors[:], a["hy_vectors"]).then_inc(m.hy_vectors_landed, 16)
            for n in range(2, tiles // 4):
                sp.wait_ge(m.z_ready, 4 * (n - 1))
                load_block(m, sp, HYENA_FIRST + n, block_of(weights, n))

        @block.tensor
        def _(pe):
            for t in range(TT):
                pe.wait_ge(m.rows_ready, m.rows_before + t + 1)
                transpose_tile_tensor(m, pe, h[:, t % 2, :], t)
            pe.wait_ge(m.columns_ready, m.turned_before + 2 * TT)
            for i in range(tiles):
                w = wait_block(m, pe, HYENA_FIRST + i // 4)
                if i >= 4:
                    pe.wait_ge(m.z_taken, i - 3)
                for k in range(KT):
                    mm = pe.matmul(m.psum[:, i % 4, :], w[:, k, (i % 4) * P:(i % 4 + 1) * P], m.cols[:, k, 0:SEQ],
                                   start=k == 0, stop=k == KT - 1)
                mm.then_inc(m.z_ready, 1)

        @block.scalar
        def _(act):
            for t in range(TT):
                transpose_tile_scalar(m, act, t, t)
            act.wait_ge(m.hy_vectors_landed, 16)
            act.wait_ge(m.pads_ready, 1)
            for i in range(tiles):
                act.wait_ge(m.z_ready, i + 1)
                if i >= 2:
                    act.wait_ge(m.conv_done, i - 1)
                act.activation(z[:, i % 2, 1:SEQ + 1], m.psum[:, i % 4, :], ACT.Identity, bias=vectors[:, 0, i:i + 1]).then_inc(m.z_taken, 1)

        @block.vector
        def _(dve):
            dve.memset(z[:], 0.0).then_inc(m.pads_ready, 1)
            modulate_rows_vector(m, dve, h, TT)
            dve.wait_ge(m.hy_vectors_landed, 16)
            for i in range(tiles):
                dve.wait_ge(m.z_taken, i + 1)
                taps = [z[:, i % 2, j:j + SEQ] for j in range(3)]
                out = m.x0[:, i, :] if i < KT else m.v_cols[:, i - KT, :] if i < 2 * KT else conv[:]
                m.vector.link(dve, dve.tensor_scalar(out, taps[0], vectors[:, 2, i:i + 1], vectors[:, 1, i:i + 1], ALU.mult, ALU.add))
                m.vector.link(dve, dve.scalar_tensor_tensor(out, taps[1], vectors[:, 3, i:i + 1], out, ALU.mult, ALU.add))
                dve.scalar_tensor_tensor(out, taps[2], vectors[:, 4, i:i + 1], out, ALU.mult, ALU.add).then_inc(m.conv_done, 1)
                if i >= 2 * KT:
                    dve.wait_ge(m.conv_done, i + 1)
                    v = m.v_cols[:, i - 2 * KT, :]
                    m.vector.link(dve, dve.tensor_tensor(v, v, conv[:], ALU.mult))
    m.rows_before += TT
    m.turned_before += 2 * TT


def convolve(nc, m, a):
    with ExitStack() as scope:
        def sb(name, shape):
            return scope.enter_context(nc.sbuf_tensor(name, shape, F32))
        slot = (RESIDUAL_FIRST[1] + 1) % 2
        v_rows = m.ring[:, slot].rearrange("p (t a) n -> p t (a n)", t=TT)
        cos_out, sin_out = sb("cos_out_sb", [P, 4, SEQ]), sb("sin_out_sb", [P, 4, SEQ])
        skip = sb("skip", [P, KT])
        parts = m.mod[:, 0:2 * D].rearrange("p (s n) -> p s n", s=4)
        minus = sb("minus", [P, 2])
        mixed = sb("skip_mixed", [P, SEQ])
        block = scope.enter_context(nc.Block(no_gpsimd_drain=True))

        @block.sync
        def _(sp):
            weights = feature_major(a["hy_w_out"][0])
            load_block(m, sp, RESIDUAL_FIRST[1], block_of(weights, 0))
            sp.dma_start(skip[:], a["hy_d_t"]).then_inc(m.inverse_landed, 16)
            sp.dma_start(cos_out[:], a["cos_out"].rearrange("(f p) t -> p f t", p=P)).then_inc(m.inverse_landed, 16)
            sp.dma_start(sin_out[:], a["sin_out"].rearrange("(f p) t -> p f t", p=P)).then_inc(m.inverse_landed, 16)
            sp.wait_ge(m.v_spectrum_ready, 8)
            load_block(m, sp, RESIDUAL_FIRST[1] + 1, block_of(weights, 1))

        @block.tensor
        def _(pe):
            for i in range(2 * TT):
                t, half = i // 2, i % 2
                if i >= 4:
                    pe.wait_ge(m.v_rows_taken, i - 3)
                for k in range(4):
                    mm = pe.transpose(m.psum[:, 4 + i % 4, k * P:(k + 1) * P], m.v_cols[:, 4 * half + k, t * P:(t + 1) * P], m.ident[:])
                mm.then_inc(m.v_turned, 1)
            pe.wait_ge(m.v_rows_taken, 2 * TT)
            for i in range(8):
                ft, cols = i // 2, slice((i % 2) * HALF, (i % 2 + 1) * HALF)
                if i >= 2:
                    pe.wait_ge(m.spectra_used, i - 1)
                for table, bank in ((m.cos_in, 2 * (i % 2)), (m.sin_in, 2 * (i % 2) + 1)):
                    for t in range(TT):
                        mm = pe.matmul(m.psum[:, bank, :], table[:, t, ft * P:(ft + 1) * P], v_rows[:, t, cols],
                                       start=t == 0, stop=t == TT - 1)
                mm.then_inc(m.v_spectrum_ready, 1)
            pe.wait_ge(m.inverse_landed, 48)
            pe.wait_ge(m.spectra_multiplied, 8)
            for k in range(KT):
                if k >= 4:
                    pe.wait_ge(m.y_taken, k - 3)
                for n, (part, table) in enumerate(((m.k_re, cos_out), (m.k_im, sin_out))):
                    for ft in range(4):
                        mm = pe.matmul(m.psum[:, 4 + k % 4, :], part[:, ft, k * P:(k + 1) * P], table[:, ft, :],
                                       start=n == ft == 0, stop=n == 1 and ft == 3)
                mm.then_inc(m.y_ready, 1)

        @block.scalar
        def _(act):
            for i in range(2 * TT):
                act.wait_ge(m.v_turned, i + 1)
                act.copy(v_rows[:, i // 2, (i % 2) * HALF:(i % 2 + 1) * HALF], m.psum[:, 4 + i % 4, :]).then_inc(m.v_rows_taken, 1)

        @block.vector
        def _(dve):
            m.vector.mark(dve.memset(minus[:], -1.0))
            m.vector.wait(dve)
            m.vector.link(dve, dve.memset(minus[0:1, 0:1], 0.0))
            for i in range(8):
                ft, cols = i // 2, slice((i % 2) * HALF, (i % 2 + 1) * HALF)
                dve.wait_ge(m.v_spectrum_ready, i + 1)
                v_re, v_im = m.psum[:, 2 * (i % 2), :], m.psum[:, 2 * (i % 2) + 1, :]
                k_re, k_im = m.k_re[:, ft, cols], m.k_im[:, ft, cols]
                m.vector.mark(dve.tensor_tensor(parts[:, 0, :], v_re, k_re, ALU.mult))
                m.vector.mark(dve.tensor_tensor(parts[:, 1, :], v_im, k_im, ALU.mult))
                m.vector.mark(dve.tensor_tensor(parts[:, 2, :], v_re, k_im, ALU.mult))
                dve.tensor_tensor(parts[:, 3, :], v_im, k_re, ALU.mult).then_inc(m.spectra_used, 1)
                m.vector.wait(dve)
                dve.wait_ge(m.spectra_used, i + 1)
                sign = minus[:, 0:1] if ft == 0 else minus[:, 1:2]
                m.vector.mark(dve.scalar_tensor_tensor(k_re, parts[:, 1, :], sign, parts[:, 0, :], ALU.mult, ALU.add))
                m.vector.mark(dve.tensor_tensor(k_im, parts[:, 2, :], parts[:, 3, :], ALU.add))
                m.vector.wait(dve)
                if ft == 0:
                    m.vector.link(dve, dve.tensor_copy(m.k_im[0:1, 0, cols], parts[0:1, 1, :]))
                dve.engine_nop().then_inc(m.spectra_multiplied, 1)
            dve.wait_ge(m.inverse_landed, 48)
            for k in range(KT):
                dve.wait_ge(m.y_ready, k + 1)
                dve.scalar_tensor_tensor(mixed[:], m.v_cols[:, k, :], skip[:, k:k + 1], m.psum[:, 4 + k % 4, :],
                                         ALU.mult, ALU.add).then_inc(m.y_taken, 1)
                dve.wait_ge(m.y_taken, k + 1)
                m.vector.link(dve, dve.tensor_tensor(m.cols[:, k, 0:SEQ], mixed[:], m.x0[:, k, :], ALU.mult))


def program(nc, a):
    with ExitStack() as whole:
        def sem(name):
            return whole.enter_context(nc.semaphore(name))
        m = Machine()
        m.setup_landed = sem("setup_landed")
        m.silu_done = sem("silu_done")
        m.cond_landed = sem("cond_landed")
        m.padding_zero = sem("padding_zero")
        m.mod_parts_taken = sem("mod_parts_taken")
        m.mod_row_ready = sem("mod_row_ready")
        m.mod_row_taken = sem("mod_row_taken")
        m.vector_steps = sem("vector_steps")
        m.selection_steps = sem("selection_steps")
        m.proj_ready = sem("proj_ready")
        m.proj_taken = sem("proj_taken")
        m.rows_ready = sem("rows_ready")
        m.rows_transposed = sem("rows_transposed")
        m.columns_ready = sem("columns_ready")
        m.mix_consts_landed = sem("mix_consts_landed")
        m.scores_biased = sem("scores_biased")
        m.gv_var_ready = sem("gv_var_ready")
        m.gv_std_ready = sem("gv_std_ready")
        m.gv_ready = sem("gv_ready")
        m.mixed_ready = sem("mixed_ready")
        m.mixed_taken = sem("mixed_taken")
        m.scores_ready = [sem(f"scores_ready{head}") for head in range(2)]
        m.probs_turned = sem("probs_turned")
        m.ctx_scores_taken = sem("ctx_scores_taken")
        m.max_ready = sem("max_ready")
        m.probs_ready = sem("probs_ready")
        m.inv_sum_ready = sem("inv_sum_ready")
        m.probs_normal = [sem(f"probs_normal{head}") for head in range(2)]
        m.g_turned = sem("g_turned")
        m.g_columns_taken = sem("g_columns_taken")
        m.turned_taken_vector = sem("turned_taken_vector")
        m.turned_taken_scalar = sem("turned_taken_scalar")
        m.heads_out_ready = sem("heads_out_ready")
        m.heads_out_taken = sem("heads_out_taken")
        m.var_ready = sem("var_ready")
        m.std_ready = sem("std_ready")
        m.ln_landed = sem("ln_landed")
        m.mix_out_ready = sem("mix_out_ready")
        m.tile_modulated = sem("tile_modulated")
        m.query_ready = sem("query_ready")
        m.query_taken = sem("query_taken")
        m.keys_landed = sem("keys_landed")
        m.key_scores_ready = sem("key_scores_ready")
        m.key_scores_taken = sem("key_scores_taken")
        m.section_selected = sem("section_selected")
        m.gates_ready = sem("gates_ready")
        m.shifted_ready = sem("shifted_ready")
        m.exps_ready = sem("exps_ready")
        m.current_ready = sem("current_ready")
        m.dots_done = sem("dots_done")
        m.v_used = sem("v_used")
        m.acted_ready = sem("acted_ready")
        m.sections_weighed = sem("sections_weighed")
        m.diagonals_ready = sem("diagonals_ready")
        m.zeros_ready = sem("zeros_ready")
        m.experts_ready = sem("experts_ready")
        m.tile_done = sem("tile_done")
        m.out_stored = sem("out_stored")
        m.ffn_landed = sem("ffn_landed")
        m.hidden_ready = sem("hidden_ready")
        m.angle_ready = sem("angle_ready")
        m.sine_ready = sem("sine_ready")
        m.filter_ready = sem("filter_ready")
        m.filter_taken = sem("filter_taken")
        m.tile_decayed = sem("tile_decayed")
        m.l1_taken = sem("l1_taken")
        m.abs_ready = sem("abs_ready")
        m.abs_summed = sem("abs_summed")
        m.parts_ready = sem("parts_ready")
        m.dft_landed = sem("dft_landed")
        m.spectrum_ready = sem("spectrum_ready")
        m.spectrum_taken = sem("spectrum_taken")
        m.highest_ready = sem("highest_ready")
        m.highest_taken = sem("highest_taken")
        m.hy_vectors_landed = sem("hy_vectors_landed")
        m.z_ready = sem("z_ready")
        m.z_taken = sem("z_taken")
        m.pads_ready = sem("pads_ready")
        m.conv_done = sem("conv_done")
        m.inverse_landed = sem("inverse_landed")
        m.v_turned = sem("v_turned")
        m.v_rows_taken = sem("v_rows_taken")
        m.v_spectrum_ready = sem("v_spectrum_ready")
        m.spectra_used = sem("spectra_used")
        m.spectra_multiplied = sem("spectra_multiplied")
        m.y_ready = sem("y_ready")
        m.y_taken = sem("y_taken")
        m.ring_landed = [sem(f"ring_landed{slot}") for slot in range(2)]
        m.mod_bias_landed = [sem(f"mod_bias_landed{slot}") for slot in range(2)]
        m.mod_group_ready = [sem(f"mod_group_ready{group}") for group in range(4)]
        m.table_landed = [sem(f"table_landed{slot}") for slot in range(4)]
        m.decay_landed = [sem(f"decay_landed{slot}") for slot in range(2)]
        m.query_weights_landed = [sem(f"query_weights_landed{place}") for place in range(2)]
        m.u_landed = [sem(f"u_landed{slot}") for slot in range(RING)]
        m.v_landed = [sem(f"v_landed{slot}") for slot in range(RING)]
        m.vector = Chain(m.vector_steps)
        m.select = SelectionChain(m.selection_steps)
        m.rows_before = m.turned_before = m.norms = m.roots = 0

        def sb(scope, name, shape):
            return scope.enter_context(nc.sbuf_tensor(name, shape, F32))
        m.psum = whole.enter_context(nc.psum_tensor("psum", [P, 8, HALF], F32))
        m.x = sb(whole, "x_rows", [P, TT, D])
        m.xm = sb(whole, "xm_rows", [P, TT, D])
        m.mod = sb(whole, "mod_rows", [P, 6 * D])
        m.cols = sb(whole, "cols", [P, KT, KEYS_ALL])
        m.ident = sb(whole, "ident_sb", [P, P])
        m.ones = sb(whole, "ones", [P, P])
        m.ranks = sb(whole, "ranks_sb", [P, TOPK])
        m.cond_silu = sb(whole, "cond_silu", [P, KT, 32])
        m.mod_bias = [m.cols[0:1, 0:2, 0:HALF], m.xm[0:1, 3, :].rearrange("p (s n) -> p s n", s=2)]
        m.picks = sb(whole, "picks_sb", [P, 2, P])
        m.ring = sb(whole, "weight_ring", [P, 2, KT, HALF])
        m.x0 = m.xm[:].rearrange("p t (a n) -> p (t a) n", n=SEQ)
        setup(nc, m, a)
        modulation(nc, m, a)
        with ExitStack() as scope:
            m.q_cols = sb(scope, "q_cols", [P, 4, SEQ])
            m.k_cols = sb(scope, "k_cols", [P, 4, KEYS_ALL])
            m.v_rows = sb(scope, "v_rows0", [P, TT + CT, NA_DIM])
            m.gate_rows = sb(scope, "gate_rows", [P, TT, D])
            project(nc, m, a)
            mix(nc, m, a)
        residual(nc, m, a, 0)
        with ExitStack() as scope:
            m.scores = sb(scope, "scores0", [P, 4 * TT + 1, 4 * NKEYS])
            experts(nc, m, a, 0)
        with ExitStack() as scope:
            m.k_re, m.k_im = sb(scope, "k_re", [P, 4, D]), sb(scope, "k_im", [P, 4, D])
            m.cos_in, m.sin_in = sb(scope, "cos_in_sb", [P, TT, SEQ]), sb(scope, "sin_in_sb", [P, TT, SEQ])
            modulation_and_filter(nc, m, a)
            m.v_cols = sb(scope, "v_cols", [P, KT, SEQ])
            hyena_project(nc, m, a)
            convolve(nc, m, a)
        residual(nc, m, a, 1)
        with ExitStack() as scope:
            m.scores = sb(scope, "scores1", [P, 4 * TT + 1, 4 * NKEYS])
            experts(nc, m, a, 1)


def constants():
    f = np.float32
    col = np.arange(GRID_W)
    first = np.clip(col - WIN_COLS // 2, 0, GRID_W - WIN_COLS)
    inside = (col[None, :] >= first[:, None]) & (col[None, :] < first[:, None] + WIN_COLS)
    window = np.where(inside, 0.0, MASKED).astype(f)
    t = np.linspace(0.0, 1.0, SEQ, dtype=f)
    angle = (f(2.0 * np.pi) * np.arange(SEQ, dtype=f) / f(SEQ))[:, None]
    bands = np.linspace(1e-4, (EMB - 1) // 2 - 1, (EMB - 1) // 2, dtype=f)[None, :]
    position = np.concatenate([t[:, None], np.cos(bands * angle), np.sin(-bands * angle)], axis=1)
    deltas = np.abs(np.linspace(np.log(1e-2) / 1.5, np.log(1e-2) / 0.3, D, dtype=f))
    n = np.arange(SEQ)
    turn = 2 * np.pi * (np.outer(n, n) % NFFT) / NFFT
    alternating = 1.0 - 2.0 * (n % 2)
    cos_in, sin_in = np.cos(turn), np.sin(turn)
    weight = np.where(n == 0, 1.0, 2.0)[:, None] / NFFT
    cos_out, sin_out = weight * cos_in, weight * sin_in
    sin_in[:, 0] = alternating
    sin_out[0, :] = alternating / NFFT
    picks = np.zeros((P, 2, P), dtype=f)
    picks[0::32, 0], picks[1::32, 1] = 1.0, 1.0
    return {
        "picks": picks, "ident": np.eye(P, dtype=f), "ranks": np.tile(np.arange(TOPK, dtype=f), (P, 1)),
        "window": np.concatenate([window, window]), "position": np.ascontiguousarray(position.T.astype(f)),
        "decay": np.exp(-t[:, None] * deltas[None, :]).astype(f),
        "cos_in": cos_in.astype(f), "sin_in": sin_in.astype(f), "cos_out": cos_out.astype(f), "sin_out": sin_out.astype(f),
    }


AS_THEY_COME = ("x", "c", "ctx", "c_ctx", "mod_w", "mod_b", "ln_g", "ln_b", "ab_w_in", "ab_w_out", "hy_w_in",
                "hy_ffn_w1", "hy_ffn_w2", "hy_ffn_w3", "hy_w_out", "peer_wq")


def laid_out(inputs):
    g = {name: np.asarray(value) for name, value in inputs.items()}
    arrays = {name: g[name] for name in AS_THEY_COME}
    for layer in range(2):
        arrays[f"peer_u{layer}"], arrays[f"peer_v{layer}"] = g["peer_u"][layer], g["peer_v"][layer]
    padded = np.pad(g["na_rpb"][0], ((0, 0), (0, 0), (GRID_W - WIN_COLS, GRID_W - WIN_COLS)))
    column = np.arange(GRID_W)
    shifted = padded[:, :, (GRID_W - 1 - column)[:, None] + column[None, :]]
    arrays["rpb_shifted"] = shifted.transpose(0, 2, 1, 3)
    arrays["gm_w_s_t"] = g["gm_w_s"][0].transpose(0, 2, 1)
    arrays["gm_b_s_t"] = g["gm_b_s"][0].T
    arrays["peer_keys_t"] = g["peer_keys"].transpose(0, 1, 2, 4, 3).reshape(2, HP, P, NKEYS)
    arrays["ffn_vectors"] = np.stack([g["hy_ffn_b1"][0], g["hy_ffn_f1"][0], g["hy_ffn_b2"][0], g["hy_ffn_f2"][0]], axis=1)
    per_feature = np.concatenate([g["hy_b_in"], g["hy_conv_b"], g["hy_conv_w"][0]])
    arrays["hy_vectors"] = per_feature.reshape(5, 3 * KT, P).transpose(2, 0, 1)
    arrays["hy_d_t"] = g["hy_d"][0].reshape(KT, P).T
    return {name: np.ascontiguousarray(value) for name, value in arrays.items()} | constants()


def kernel(**inputs):
    import concourse.bacc as bacc
    from concourse.bass_utils import run_bass_kernel_spmd

    nc = bacc.Bacc("TRN2", target_bir_lowering=False, num_devices=1)
    arrays = laid_out(inputs)
    a = {name: nc.dram_tensor(f"in_{name}", value.shape, mybir.dt.from_np(value.dtype), kind="ExternalInput").ap()
         for name, value in arrays.items()}
    a["out"] = nc.dram_tensor("out_x", (1, SEQ, D), F32, kind="ExternalOutput").ap()
    program(nc, a)
    result = run_bass_kernel_spmd(nc, [{f"in_{name}": value for name, value in arrays.items()}], core_ids=[0])
    return result.results[0]["out_x"]
```
